# Optimizing a Trainium2 kernel written in Bass

```python
import math
import jax, jax.numpy as jnp
from jax import lax
import numpy as np
import jax
import jax.numpy as jnp

D_MODEL = 1024
BATCH = 1
SEQ = 512
DEPTH = 2

ATT_HEADS = 8
ATT_KV_HEADS = 2
HEAD_DIM = 64
IDX_HEADS = 8
IDX_DIM = 64
TOPK_MAX = 256
Q_BLOCK = 128
ROPE_THETA = 10000.0
RWKV_HEADS = 4
RWKV_HEAD = 64
RWKV_DECAY_LORA = 32
RWKV_A_LORA = 32
RWKV_MV_LORA = 32
RWKV_GATE_LORA = 64
RWKV_GN_EPS = 64e-5
GDN_HEADS = 4
GDN_HEAD = 64
GDN_CONV = 4
GDN_CHUNK = 64
D_FF = 2816
NORM_EPS = 1e-6

ATT_W = ATT_HEADS * HEAD_DIM
KV_W = ATT_KV_HEADS * HEAD_DIM
RWKV_W = RWKV_HEADS * RWKV_HEAD
GDN_W = GDN_HEADS * GDN_HEAD
MIX_W = ATT_W + RWKV_W + GDN_W
ATT_SPLITS = (ATT_W, KV_W, KV_W, IDX_HEADS * IDX_DIM, IDX_DIM, IDX_HEADS)
RWKV_SPLITS = (RWKV_W, RWKV_W, RWKV_W, RWKV_DECAY_LORA, RWKV_A_LORA, RWKV_GATE_LORA)
GDN_SPLITS = (GDN_W, GDN_W, GDN_W, GDN_W, GDN_HEADS, GDN_HEADS)
RWKV_IN = sum(RWKV_SPLITS)
GROUP_SPLITS = (sum(ATT_SPLITS), RWKV_IN, sum(GDN_SPLITS))
IN_W = sum(GROUP_SPLITS)


def split_cols(p, sizes):
    offs = [int(o) for o in np.cumsum(sizes)[:-1]]
    return jnp.split(p, offs, axis=-1)

def rms_norm(x, g, eps=NORM_EPS):
    xf = x.astype(jnp.float32)
    y = xf * lax.rsqrt(jnp.mean(xf * xf, axis=-1, keepdims=True) + eps)
    return (y * g.astype(jnp.float32)).astype(x.dtype)

def l2_normalize(x, eps):
    xf = x.astype(jnp.float32)
    return xf * lax.rsqrt(jnp.sum(xf * xf, axis=-1, keepdims=True) + eps)

def rope(x, pos):
    half = x.shape[-1] // 2
    inv = ROPE_THETA ** (-jnp.arange(half, dtype=jnp.float32) / half)
    ang = pos.astype(jnp.float32)[:, None] * inv[None, :]
    cos, sin = jnp.cos(ang)[:, None, :], jnp.sin(ang)[:, None, :]
    xf = x.astype(jnp.float32)
    x1, x2 = xf[..., :half], xf[..., half:]
    return jnp.concatenate([x1 * cos - x2 * sin, x2 * cos + x1 * sin], axis=-1).astype(x.dtype)

def swiglu(h, w_gate, w_up, w_down):
    return (jax.nn.silu(h @ w_gate) * (h @ w_up)) @ w_down

def dsa_attention(pa, q_norm, k_norm):
    B, L, _ = pa.shape
    q, k, v, qi, ki, wi = split_cols(pa, ATT_SPLITS)
    pos = jnp.arange(L)
    q = rope(rms_norm(q.reshape(B, L, ATT_HEADS, HEAD_DIM), q_norm), pos)
    k = rope(rms_norm(k.reshape(B, L, ATT_KV_HEADS, HEAD_DIM), k_norm), pos)
    v = v.reshape(B, L, ATT_KV_HEADS, HEAD_DIM)
    qi = rope(qi.reshape(B, L, IDX_HEADS, IDX_DIM), pos).astype(jnp.float32)
    ki = rope(ki[:, :, None, :], pos)[:, :, 0].astype(jnp.float32)
    wi = wi.astype(jnp.float32) * (IDX_HEADS ** -0.5 * IDX_DIM ** -0.5)
    n_sel = min(TOPK_MAX, L // 4)
    n_blk = L // Q_BLOCK
    rep = ATT_HEADS // ATT_KV_HEADS
    scale = HEAD_DIM ** -0.5

    def to_blocks(a):
        return a.reshape(B, n_blk, Q_BLOCK, *a.shape[2:]).swapaxes(0, 1)

    def block(args):
        qb, qib, wib, tb = args
        logits = jnp.einsum('bqhd,bsd->bqhs', qib, ki)
        score = jnp.einsum('bqhs,bqh->bqs', jax.nn.relu(logits), wib)
        score = jnp.where(pos[None, None, :] <= tb[None, :, None], score, -jnp.inf)
        _, idx = lax.top_k(score, n_sel)
        valid = idx <= tb[None, :, None]
        ks = jax.vmap(lambda kb, ib: kb[ib])(k, idx).astype(jnp.float32)
        vs = jax.vmap(lambda vb, ib: vb[ib])(v, idx)
        qg = qb.reshape(B, Q_BLOCK, ATT_KV_HEADS, rep, HEAD_DIM).astype(jnp.float32)
        s = jnp.einsum('bqgrd,bqkgd->bqgrk', qg, ks) * scale
        s = jnp.where(valid[:, :, None, None, :], s, -jnp.inf)
        p = jax.nn.softmax(s, axis=-1).astype(vs.dtype)
        o = jnp.einsum('bqgrk,bqkgd->bqgrd', p, vs)
        return o.reshape(B, Q_BLOCK, ATT_W)

    out = lax.map(block, (to_blocks(q), to_blocks(qi), to_blocks(wi), pos.reshape(n_blk, Q_BLOCK)))
    return out.swapaxes(0, 1).reshape(B, L, ATT_W).astype(pa.dtype)

def rwkv7_scan(r, w, k, v, a, b):
    B, L, H, N = r.shape

    def step(S, inp):
        rt, wt, kt, vt, at, bt = inp
        sa = jnp.einsum('bhij,bhj->bhi', S, at)
        S = S * wt[:, :, None, :] + sa[..., None] * bt[:, :, None, :] + vt[..., None] * kt[:, :, None, :]
        return S, jnp.einsum('bhij,bhj->bhi', S, rt)

    xs = tuple(jnp.moveaxis(t, 1, 0) for t in (r, w, k, v, a, b))
    _, y = lax.scan(step, jnp.zeros((B, H, N, N), jnp.float32), xs)
    return jnp.moveaxis(y, 0, 1)

def rwkv7_time_mix(pb, mu, w0, w_up, a0, a_up, g_up, k_k, k_a, r_k, gn_w, gn_b, v_first, v0, v_down, v_up):
    dt = pb.dtype
    B, L, _ = pb.shape
    hb = pb.astype(jnp.float32)
    prev = jnp.pad(hb, ((0, 0), (1, 0), (0, 0)))[:, :-1]
    hb = hb + (prev - hb) * mu
    r, k, v, wd, ad, gd = split_cols(hb, RWKV_SPLITS)
    heads = lambda t: t.reshape(B, L, RWKV_HEADS, RWKV_HEAD)
    w_log = -jax.nn.softplus(-(w0 + jnp.tanh(wd) @ w_up)) - 0.5
    decay = jnp.exp(-jnp.exp(w_log))
    a = jax.nn.sigmoid(a0 + ad @ a_up)
    g = jax.nn.sigmoid(gd) @ g_up
    kk = l2_normalize(heads(k * k_k), 1e-12)
    k = k * (1.0 + (a - 1.0) * k_a)
    if v_first is None:
        v_first = v
    else:
        v = v + (v_first - v) * jax.nn.sigmoid(v0 + (v @ v_down) @ v_up)
    rh, kh, vh = heads(r), heads(k), heads(v)
    y = rwkv7_scan(rh, heads(decay), kh, vh, -kk, kk * heads(a))
    mean = jnp.mean(y, axis=-1, keepdims=True)
    var = jnp.mean(jnp.square(y - mean), axis=-1, keepdims=True)
    y = ((y - mean) * lax.rsqrt(var + RWKV_GN_EPS)).reshape(B, L, RWKV_W) * gn_w + gn_b
    bonus = jnp.sum(rh * kh * r_k, axis=-1, keepdims=True) * vh
    y = (y + bonus.reshape(B, L, RWKV_W)) * g
    return y.astype(dt), v_first

def causal_dwconv(x, w):
    C = x.shape[-1]
    return lax.conv_general_dilated(x, w[:, None, :], window_strides=(1,), padding=[(w.shape[0] - 1, 0)],
                                    dimension_numbers=('NWC', 'WIO', 'NWC'), feature_group_count=C)

def chunk_gated_delta_rule(q, k, v, g, beta):
    B, L, H, Dk = q.shape
    Dv = v.shape[-1]
    C = GDN_CHUNK
    n = L // C
    chunks = lambda t: t.reshape(B, n, C, H, t.shape[-1]).transpose(0, 3, 1, 2, 4)
    q, k, v = chunks(q), chunks(k), chunks(v)
    beta = beta.reshape(B, n, C, H).transpose(0, 3, 1, 2)
    g = jnp.cumsum(g.reshape(B, n, C, H).transpose(0, 3, 1, 2), axis=-1)
    incl = jnp.tril(jnp.ones((C, C), bool))
    strict = jnp.tril(jnp.ones((C, C), bool), -1)
    decay = jnp.exp(jnp.where(incl, g[..., :, None] - g[..., None, :], -jnp.inf))
    kb = k * beta[..., None]
    lower = jnp.where(strict, jnp.einsum('bhncd,bhnsd->bhncs', kb, k) * decay, 0.0)
    rhs = jnp.concatenate([v * beta[..., None], kb * jnp.exp(g)[..., None]], axis=-1)
    sol = lax.linalg.triangular_solve(jnp.eye(C, dtype=jnp.float32) + lower, rhs,
                                      left_side=True, lower=True, unit_diagonal=True)
    u, wk = sol[..., :Dv], sol[..., Dv:]
    intra = jnp.where(incl, jnp.einsum('bhncd,bhnsd->bhncs', q, k) * decay, 0.0)

    def step(S, inp):
        qc, kc, uc, wc, gc, ac = inp
        v_new = uc - jnp.einsum('bhck,bhkv->bhcv', wc, S)
        o = jnp.einsum('bhck,bhkv->bhcv', qc * jnp.exp(gc)[..., None], S) + jnp.einsum('bhcs,bhsv->bhcv', ac, v_new)
        g_last = gc[..., -1]
        S = S * jnp.exp(g_last)[..., None, None] + jnp.einsum(
            'bhck,bhcv->bhkv', kc * jnp.exp(g_last[..., None] - gc)[..., None], v_new)
        return S, o

    xs = tuple(jnp.moveaxis(t, 2, 0) for t in (q, k, u, wk, g, intra))
    _, o = lax.scan(step, jnp.zeros((B, H, Dk, Dv), jnp.float32), xs)
    return o.transpose(1, 0, 3, 2, 4).reshape(B, L, H, Dv)

def gated_deltanet(pc, conv_w, a_log, dt_bias, o_norm):
    dt = pc.dtype
    B, L, _ = pc.shape
    q, k, v, z, b_in, a_in = split_cols(pc.astype(jnp.float32), GDN_SPLITS)
    qkv = jax.nn.silu(causal_dwconv(jnp.concatenate([q, k, v], axis=-1), conv_w.astype(jnp.float32)))
    q, k, v = jnp.split(qkv, 3, axis=-1)
    heads = lambda t: t.reshape(B, L, GDN_HEADS, GDN_HEAD)
    q = l2_normalize(heads(q), 1e-6) * (GDN_HEAD ** -0.5)
    k = l2_normalize(heads(k), 1e-6)
    beta = jax.nn.sigmoid(b_in)
    g = -jnp.exp(a_log.astype(jnp.float32)) * jax.nn.softplus(a_in + dt_bias)
    o = chunk_gated_delta_rule(q, k, heads(v), g, beta)
    o = rms_norm(o, o_norm) * jax.nn.silu(heads(z))
    return o.reshape(B, L, GDN_W).astype(dt)

def first_inputs(seed: int = 0) -> dict:
    key = jax.random.key(seed)
    ks = iter(jax.random.split(key, 40))
    nrm = lambda shape, s: jax.random.normal(next(ks), shape, jnp.float32) * s
    uni = lambda shape, lo, hi: jax.random.uniform(next(ks), shape, jnp.float32, lo, hi)
    D, F = D_MODEL, D_FF
    dt0 = jnp.exp(uni((DEPTH, GDN_HEADS), math.log(1e-3), math.log(1e-1)))
    return {
        'x': nrm((BATCH, SEQ, D), 1.0),
        'ffn_norm': 1.0 + nrm((DEPTH, 2, D), 0.02),
        'ffn_w_gate': nrm((DEPTH, 2, D, F), D ** -0.5),
        'ffn_w_up': nrm((DEPTH, 2, D, F), D ** -0.5),
        'ffn_w_down': nrm((DEPTH, 2, F, D), F ** -0.5),
        'mix_norm': 1.0 + nrm((DEPTH, D), 0.02),
        'w_in': nrm((DEPTH, D, IN_W), D ** -0.5),
        'w_out': nrm((DEPTH, MIX_W, D), MIX_W ** -0.5),
        'att_q_norm': 1.0 + nrm((DEPTH, HEAD_DIM), 0.02),
        'att_k_norm': 1.0 + nrm((DEPTH, HEAD_DIM), 0.02),
        'rwkv_mu': uni((DEPTH, RWKV_IN), 0.0, 1.0),
        'rwkv_w0': uni((DEPTH, RWKV_W), -6.5, -1.5),
        'rwkv_w_up': nrm((DEPTH, RWKV_DECAY_LORA, RWKV_W), RWKV_DECAY_LORA ** -0.5),
        'rwkv_a0': nrm((DEPTH, RWKV_W), 0.1),
        'rwkv_a_up': nrm((DEPTH, RWKV_A_LORA, RWKV_W), RWKV_A_LORA ** -0.5),
        'rwkv_g_up': nrm((DEPTH, RWKV_GATE_LORA, RWKV_W), RWKV_GATE_LORA ** -0.5),
        'rwkv_k_k': 0.85 + nrm((DEPTH, RWKV_W), 0.05),
        'rwkv_k_a': 1.0 + nrm((DEPTH, RWKV_W), 0.05),
        'rwkv_r_k': nrm((DEPTH, RWKV_HEADS, RWKV_HEAD), 0.1),
        'rwkv_gn_w': 1.0 + nrm((DEPTH, RWKV_W), 0.02),
        'rwkv_gn_b': nrm((DEPTH, RWKV_W), 0.02),
        'rwkv_v0': 1.0 + nrm((DEPTH - 1, RWKV_W), 0.05),
        'rwkv_v_down': nrm((DEPTH - 1, RWKV_W, RWKV_MV_LORA), RWKV_W ** -0.5),
        'rwkv_v_up': nrm((DEPTH - 1, RWKV_MV_LORA, RWKV_W), 0.1 * RWKV_MV_LORA ** -0.5),
        'gdn_conv': nrm((DEPTH, GDN_CONV, 3 * GDN_W), GDN_CONV ** -0.5),
        'gdn_a_log': jnp.log(uni((DEPTH, GDN_HEADS), 1.0, 16.0)),
        'gdn_dt_bias': dt0 + jnp.log(-jnp.expm1(-dt0)),
        'gdn_o_norm': 1.0 + nrm((DEPTH, GDN_HEAD), 0.02),
    }

def first_block(x, ffn_norm, ffn_w_gate, ffn_w_up, ffn_w_down, mix_norm, w_in, w_out, att_q_norm, att_k_norm,
              rwkv_mu, rwkv_w0, rwkv_w_up, rwkv_a0, rwkv_a_up, rwkv_g_up, rwkv_k_k, rwkv_k_a, rwkv_r_k,
              rwkv_gn_w, rwkv_gn_b, rwkv_v0, rwkv_v_down, rwkv_v_up, gdn_conv, gdn_a_log, gdn_dt_bias, gdn_o_norm):
    v_first = None
    for l in range(DEPTH):
        x = x + 0.5 * swiglu(rms_norm(x, ffn_norm[l, 0]), ffn_w_gate[l, 0], ffn_w_up[l, 0], ffn_w_down[l, 0])
        p = rms_norm(x, mix_norm[l]) @ w_in[l]
        pa, pb, pc = split_cols(p, GROUP_SPLITS)
        ya = dsa_attention(pa, att_q_norm[l], att_k_norm[l])
        if l == 0:
            vres = (None, None, None)
        else:
            vres = (rwkv_v0[l - 1], rwkv_v_down[l - 1], rwkv_v_up[l - 1])
        yb, v_first = rwkv7_time_mix(pb, rwkv_mu[l], rwkv_w0[l], rwkv_w_up[l], rwkv_a0[l], rwkv_a_up[l],
                                     rwkv_g_up[l], rwkv_k_k[l], rwkv_k_a[l], rwkv_r_k[l], rwkv_gn_w[l],
                                     rwkv_gn_b[l], v_first, *vres)
        yc = gated_deltanet(pc, gdn_conv[l], gdn_a_log[l], gdn_dt_bias[l], gdn_o_norm[l])
        x = x + jnp.concatenate([ya, yb, yc], axis=-1) @ w_out[l]
        x = x + 0.5 * swiglu(rms_norm(x, ffn_norm[l, 1]), ffn_w_gate[l, 1], ffn_w_up[l, 1], ffn_w_down[l, 1])
    return x


DEPTH_2 = 1

MEM_LEN = 256
EPS = 1e-6
FOX_HEADS = 8
FOX_HEAD_DIM = 64
FOX_WIDTH = FOX_HEADS * FOX_HEAD_DIM
FOX_BLOCK = 128
FORGET_BIAS_INIT = 3.0
GLA_HEADS = 4
GLA_KEY_DIM = 64
GLA_VAL_DIM = 128
GLA_QK_WIDTH = GLA_HEADS * GLA_KEY_DIM
GLA_V_WIDTH = GLA_HEADS * GLA_VAL_DIM
GLA_GATE_RANK = 16
GLA_GATE_TAU = 16.0
GLA_CHUNK = 64
MIX_WIDTH = FOX_WIDTH + GLA_V_WIDTH
IN_WIDTHS = (FOX_WIDTH, FOX_WIDTH, FOX_WIDTH, FOX_HEADS, GLA_QK_WIDTH, GLA_QK_WIDTH, GLA_V_WIDTH, GLA_V_WIDTH, GLA_GATE_RANK)
IN_PROJ_WIDTH = 3096
X_HEADS = 4
X_HEAD_DIM = 128
X_WIDTH = X_HEADS * X_HEAD_DIM
N_GROUPS = 4
EXPERTS_PER_GROUP = 4
N_EXPERTS = N_GROUPS * EXPERTS_PER_GROUP
TOP_K = 2
D_EXPERT = 512
MOE_BLOCK = 128
RESID_SCALE = 0.5


def rms_norm_2(x, gain):
    xf = x.astype(jnp.float32)
    y = xf * lax.rsqrt(jnp.mean(xf * xf, axis=-1, keepdims=True) + EPS)
    return (y * gain.astype(jnp.float32)).astype(x.dtype)

def forgetting_attention(q, k, v, f_logit):
    B, S, H, d = q.shape
    q = q.transpose(0, 2, 1, 3)
    k = k.transpose(0, 2, 1, 3)
    v = v.transpose(0, 2, 1, 3)
    log_f = jax.nn.log_sigmoid(f_logit.astype(jnp.float32)).transpose(0, 2, 1)
    c = jnp.cumsum(log_f, axis=-1)
    scale = d ** -0.5
    outs = []
    for blk in range(S // FOX_BLOCK):
        q0 = blk * FOX_BLOCK
        q1 = q0 + FOX_BLOCK
        s = jnp.einsum('bhqd,bhkd->bhqk', q[:, :, q0:q1], k[:, :, :q1], preferred_element_type=jnp.float32) * scale
        s = s + c[:, :, q0:q1, None] - c[:, :, None, :q1]
        causal = jnp.arange(q0, q1)[:, None] >= jnp.arange(q1)[None, :]
        p = jax.nn.softmax(jnp.where(causal, s, -jnp.inf), axis=-1)
        outs.append(jnp.einsum('bhqk,bhkd->bhqd', p.astype(v.dtype), v[:, :, :q1]))
    return jnp.concatenate(outs, axis=2).transpose(0, 2, 1, 3)

def gla_chunked(q, k, v, log_a):
    B, S, H, dk = q.shape
    dv = v.shape[-1]
    C = GLA_CHUNK
    nc = S // C

    def to_chunks(t):
        return t.astype(jnp.float32).reshape(B, nc, C, H, t.shape[-1]).transpose(1, 0, 3, 2, 4)

    qc = to_chunks(q) * (dk ** -0.5)
    kc = to_chunks(k)
    vc = to_chunks(v)
    gc = to_chunks(log_a)
    causal = jnp.tril(jnp.ones((C, C), dtype=bool))[:, :, None]

    def step(state, inp):
        qi, ki, vi, gi = inp
        b = jnp.cumsum(gi, axis=2)
        b_last = b[:, :, -1:, :]
        o_inter = jnp.einsum('bhtd,bhdv->bhtv', qi * jnp.exp(b), state)
        diff = b[:, :, :, None, :] - b[:, :, None, :, :]
        decay = jnp.exp(jnp.where(causal, diff, -jnp.inf))
        attn = jnp.einsum('bhtd,bhsd,bhtsd->bhts', qi, ki, decay)
        o_intra = jnp.einsum('bhts,bhsv->bhtv', attn, vi)
        new_state = jnp.exp(b_last[:, :, 0, :])[..., None] * state + jnp.einsum('bhsd,bhsv->bhdv', ki * jnp.exp(b_last - b), vi)
        return new_state, o_inter + o_intra

    state0 = jnp.zeros((B, H, dk, dv), jnp.float32)
    _, o = lax.scan(step, state0, (qc, kc, vc, gc))
    return o.transpose(1, 0, 3, 2, 4).reshape(B, S, H, dv).astype(v.dtype)

def hybrid_mixer(h, w_in, b_forget, w_alpha_up, b_alpha, fox_out_gain, gla_out_gain, w_out):
    B, S, _ = h.shape
    offsets = [int(o) for o in np.cumsum(IN_WIDTHS)[:-1]]
    fq, fk, fv, ff, gq, gk, gv, gg, ga = jnp.split(h @ w_in, offsets, axis=-1)
    fox = forgetting_attention(
        fq.reshape(B, S, FOX_HEADS, FOX_HEAD_DIM),
        fk.reshape(B, S, FOX_HEADS, FOX_HEAD_DIM),
        fv.reshape(B, S, FOX_HEADS, FOX_HEAD_DIM),
        ff + b_forget)
    fox = rms_norm_2(fox, fox_out_gain.reshape(FOX_HEADS, FOX_HEAD_DIM))
    log_a = jax.nn.log_sigmoid((ga @ w_alpha_up + b_alpha).astype(jnp.float32)) / GLA_GATE_TAU
    gla = gla_chunked(
        gq.reshape(B, S, GLA_HEADS, GLA_KEY_DIM),
        gk.reshape(B, S, GLA_HEADS, GLA_KEY_DIM),
        gv.reshape(B, S, GLA_HEADS, GLA_VAL_DIM),
        log_a.reshape(B, S, GLA_HEADS, GLA_KEY_DIM))
    gla = rms_norm_2(gla, gla_out_gain.reshape(GLA_HEADS, GLA_VAL_DIM)) * jax.nn.silu(gg.reshape(B, S, GLA_HEADS, GLA_VAL_DIM))
    y = jnp.concatenate([fox.reshape(B, S, FOX_WIDTH), gla.reshape(B, S, GLA_V_WIDTH)], axis=-1)
    return y @ w_out

def memory_cross_attention(h, mem_n, w_xq, w_xk, w_xv, w_xo):
    B, S, _ = h.shape
    M = mem_n.shape[1]
    q = (h @ w_xq).reshape(B, S, X_HEADS, X_HEAD_DIM)
    k = (mem_n @ w_xk).reshape(B, M, X_HEADS, X_HEAD_DIM)
    v = (mem_n @ w_xv).reshape(B, M, X_HEADS, X_HEAD_DIM)
    s = jnp.einsum('bqhd,bkhd->bhqk', q, k, preferred_element_type=jnp.float32) * (X_HEAD_DIM ** -0.5)
    p = jax.nn.softmax(s, axis=-1)
    o = jnp.einsum('bhqk,bkhd->bqhd', p.astype(v.dtype), v).reshape(B, S, X_WIDTH)
    return o @ w_xo

def hierarchical_moe(h, w_rg, b_rg, w_re, b_re, w_e_gate, w_e_up, w_e_down):
    B, S, D = h.shape
    N = B * S
    hf = h.reshape(N, D)
    g_prob = jax.nn.softmax((hf @ w_rg).astype(jnp.float32) + b_rg.astype(jnp.float32), axis=-1)
    grp = jnp.argmax(g_prob, axis=-1)
    p_grp = jnp.take_along_axis(g_prob, grp[:, None], axis=-1)
    e_logits = ((hf @ w_re).astype(jnp.float32) + b_re.astype(jnp.float32)).reshape(N, N_GROUPS, EXPERTS_PER_GROUP)
    e_logits = jnp.take_along_axis(e_logits, grp[:, None, None], axis=1)[:, 0]
    top_p, top_i = lax.top_k(jax.nn.softmax(e_logits, axis=-1), TOP_K)
    gate = p_grp * top_p / jnp.sum(top_p, axis=-1, keepdims=True)
    expert = grp[:, None].astype(jnp.int32) * EXPERTS_PER_GROUP + top_i.astype(jnp.int32)
    Mrows = N * TOP_K
    flat_e = expert.reshape(Mrows)
    flat_g = gate.reshape(Mrows)
    flat_tok = jnp.repeat(jnp.arange(N, dtype=jnp.int32), TOP_K)
    order = jnp.argsort(flat_e)
    sorted_e = flat_e[order]
    counts = jnp.bincount(flat_e, length=N_EXPERTS)
    padded = (counts + MOE_BLOCK - 1) // MOE_BLOCK * MOE_BLOCK
    starts = jnp.cumsum(counts) - counts
    pad_ends = jnp.cumsum(padded)
    pad_starts = pad_ends - padded
    dest = pad_starts[sorted_e] + jnp.arange(Mrows, dtype=jnp.int32) - starts[sorted_e]
    R = Mrows + N_EXPERTS * MOE_BLOCK
    n_blocks = R // MOE_BLOCK
    row_tok = jnp.full((R,), N, dtype=jnp.int32).at[dest].set(flat_tok[order])
    row_gate = jnp.zeros((R,), jnp.float32).at[dest].set(flat_g[order])
    block_e = jnp.minimum(jnp.searchsorted(pad_ends, jnp.arange(n_blocks) * MOE_BLOCK, side='right'), N_EXPERTS - 1)
    x_rows = jnp.concatenate([hf, jnp.zeros((1, D), hf.dtype)], axis=0)[row_tok].reshape(n_blocks, MOE_BLOCK, D)

    def expert_block(args):
        xb, e = args
        u = jax.nn.silu(xb @ w_e_gate[e]) * (xb @ w_e_up[e])
        return u @ w_e_down[e]

    y_rows = lax.map(expert_block, (x_rows, block_e)).reshape(R, D)
    y = jax.ops.segment_sum(y_rows.astype(jnp.float32) * row_gate[:, None], row_tok, num_segments=N + 1)[:N]
    return y.reshape(B, S, D).astype(h.dtype)

def second_inputs(seed: int = 0) -> dict:
    key = jax.random.key(seed)
    ks = jax.random.split(key, 26)
    f32 = jnp.float32
    L = DEPTH_2

    def w(k, shape, fan_in, scale=1.0):
        return jax.random.normal(k, shape, f32) * (scale * fan_in ** -0.5)

    def gain(k, shape):
        return 1.0 + 0.02 * jax.random.normal(k, shape, f32)

    def small(k, shape, scale):
        return scale * jax.random.normal(k, shape, f32)

    return {
        'x': jax.random.normal(ks[0], (BATCH, SEQ, D_MODEL), f32),
        'mem': jax.random.normal(ks[1], (BATCH, MEM_LEN, D_MODEL), f32),
        'mem_norm': gain(ks[2], (D_MODEL,)),
        'mix_norm': gain(ks[3], (L, D_MODEL)),
        'w_in': w(ks[4], (L, D_MODEL, IN_PROJ_WIDTH), D_MODEL),
        'b_forget': FORGET_BIAS_INIT + small(ks[5], (L, FOX_HEADS), 0.1),
        'w_alpha_up': w(ks[6], (L, GLA_GATE_RANK, GLA_QK_WIDTH), GLA_GATE_RANK),
        'b_alpha': small(ks[7], (L, GLA_QK_WIDTH), 0.1),
        'fox_out_gain': gain(ks[8], (L, FOX_WIDTH)),
        'gla_out_gain': gain(ks[9], (L, GLA_V_WIDTH)),
        'w_out': w(ks[10], (L, MIX_WIDTH, D_MODEL), MIX_WIDTH, RESID_SCALE),
        'cross_norm': gain(ks[11], (L, D_MODEL)),
        'w_xq': w(ks[12], (L, D_MODEL, X_WIDTH), D_MODEL),
        'w_xk': w(ks[13], (L, D_MODEL, X_WIDTH), D_MODEL),
        'w_xv': w(ks[14], (L, D_MODEL, X_WIDTH), D_MODEL),
        'w_xo': w(ks[15], (L, X_WIDTH, D_MODEL), X_WIDTH, RESID_SCALE),
        'moe_norm': gain(ks[16], (L, D_MODEL)),
        'w_router_group': w(ks[17], (L, D_MODEL, N_GROUPS), D_MODEL),
        'b_router_group': small(ks[18], (L, N_GROUPS), 0.01),
        'w_router_expert': w(ks[19], (L, D_MODEL, N_EXPERTS), D_MODEL),
        'b_router_expert': small(ks[20], (L, N_EXPERTS), 0.01),
        'w_expert_gate': w(ks[21], (L, N_EXPERTS, D_MODEL, D_EXPERT), D_MODEL),
        'w_expert_up': w(ks[22], (L, N_EXPERTS, D_MODEL, D_EXPERT), D_MODEL),
        'w_expert_down': w(ks[23], (L, N_EXPERTS, D_EXPERT, D_MODEL), D_EXPERT, RESID_SCALE),
        'final_norm': gain(ks[24], (D_MODEL,)),
    }

def second_block(x, mem, mem_norm, mix_norm, w_in, b_forget, w_alpha_up, b_alpha, fox_out_gain, gla_out_gain, w_out,
              cross_norm, w_xq, w_xk, w_xv, w_xo, moe_norm, w_router_group, b_router_group, w_router_expert,
              b_router_expert, w_expert_gate, w_expert_up, w_expert_down, final_norm):
    mem_n = rms_norm_2(mem, mem_norm)
    h = x
    for l in range(DEPTH_2):
        h = h + hybrid_mixer(rms_norm_2(h, mix_norm[l]), w_in[l], b_forget[l], w_alpha_up[l], b_alpha[l],
                             fox_out_gain[l], gla_out_gain[l], w_out[l])
        h = h + memory_cross_attention(rms_norm_2(h, cross_norm[l]), mem_n, w_xq[l], w_xk[l], w_xv[l], w_xo[l])
        h = h + hierarchical_moe(rms_norm_2(h, moe_norm[l]), w_router_group[l], b_router_group[l],
                                 w_router_expert[l], b_router_expert[l], w_expert_gate[l], w_expert_up[l],
                                 w_expert_down[l])
    return rms_norm_2(h, final_norm)


def setup_inputs(seed=0):
    out = dict(first_inputs(seed))
    for name, value in second_inputs(seed + 1).items():
        if name != "x":
            out[name + "_2"] = value
    return out


def reference(
    x, ffn_norm, ffn_w_gate, ffn_w_up, ffn_w_down, mix_norm, w_in, w_out, att_q_norm,
    att_k_norm, rwkv_mu, rwkv_w0, rwkv_w_up, rwkv_a0, rwkv_a_up, rwkv_g_up, rwkv_k_k, rwkv_k_a,
    rwkv_r_k, rwkv_gn_w, rwkv_gn_b, rwkv_v0, rwkv_v_down, rwkv_v_up, gdn_conv, gdn_a_log,
    gdn_dt_bias, gdn_o_norm, mem_2, mem_norm_2, mix_norm_2, w_in_2, b_forget_2, w_alpha_up_2,
    b_alpha_2, fox_out_gain_2, gla_out_gain_2, w_out_2, cross_norm_2, w_xq_2, w_xk_2, w_xv_2,
    w_xo_2, moe_norm_2, w_router_group_2, b_router_group_2, w_router_expert_2,
    b_router_expert_2, w_expert_gate_2, w_expert_up_2, w_expert_down_2, final_norm_2,
):
    x = first_block(
        x, ffn_norm, ffn_w_gate, ffn_w_up, ffn_w_down, mix_norm, w_in, w_out, att_q_norm,
        att_k_norm, rwkv_mu, rwkv_w0, rwkv_w_up, rwkv_a0, rwkv_a_up, rwkv_g_up, rwkv_k_k,
        rwkv_k_a, rwkv_r_k, rwkv_gn_w, rwkv_gn_b, rwkv_v0, rwkv_v_down, rwkv_v_up, gdn_conv,
        gdn_a_log, gdn_dt_bias, gdn_o_norm,
    )
    return second_block(
        x, mem_2, mem_norm_2, mix_norm_2, w_in_2, b_forget_2, w_alpha_up_2, b_alpha_2,
        fox_out_gain_2, gla_out_gain_2, w_out_2, cross_norm_2, w_xq_2, w_xk_2, w_xv_2, w_xo_2,
        moe_norm_2, w_router_group_2, b_router_group_2, w_router_expert_2, b_router_expert_2,
        w_expert_gate_2, w_expert_up_2, w_expert_down_2, final_norm_2,
    )


_drawn_inputs = setup_inputs


def setup_inputs(seed=0):
    import zlib

    import numpy as np

    out = dict(_drawn_inputs(seed))
    spreads = {}
    factors = {'att_q_norm': 7.054,
     'att_k_norm': 7.094,
     'rwkv_a0': 3.278,
     'rwkv_gn_w': 5.221,
     'rwkv_gn_b': 4.617,
     'rwkv_v0': 8.0,
     'rwkv_v_down': 7.445,
     'rwkv_v_up': 5.538,
     'gdn_o_norm': 4.659,
     'mem_norm_2': 8.0,
     'mix_norm_2': 4.607,
     'b_forget_2': 3.298,
     'w_alpha_up_2': 2.831,
     'b_alpha_2': 6.7,
     'fox_out_gain_2': 7.544,
     'gla_out_gain_2': 8.0,
     'cross_norm_2': 8.0,
     'moe_norm_2': 4.241,
     'b_router_group_2': 6.172,
     'b_router_expert_2': 28.024,
     'final_norm_2': 8.051}
    for name, (base, spread) in spreads.items():
        noise = np.random.default_rng([zlib.crc32(name.encode()), seed]).standard_normal(out[name].shape)
        drawn = base * np.exp(spread * noise) if base else spread * noise
        out[name] = jnp.asarray(drawn.astype(out[name].dtype))
    for name, factor in factors.items():
        out[name] = (out[name] * factor).astype(out[name].dtype)
    return out
```

```python
from contextlib import ExitStack, contextmanager

import concourse.bass as bass
from concourse import mybir

F32 = mybir.dt.float32
F32R = mybir.dt.float32r
U32 = mybir.dt.uint32
ALU = mybir.AluOpType
ACT = mybir.ActivationFunctionType
AX = mybir.AxisListType.X

P = 128
DEPTH, D, SEQ, D_FF = 2, 1024, 512, 2816
KC = D // P
NT = SEQ // P
SLOT = 2048
SLOT_COLS = SLOT // KC
RING = 2
PAIRS = D_FF // (2 * P)
FFN_PARTS = (6, 5)
FFN_SLOTS = 3 * PAIRS
IN_SLOTS = 13
LAYER_SLOTS = 1 + 2 * FFN_SLOTS + IN_SLOTS + 4
E_SLOTS = 6
N_EXPERTS, GROUPS, PER_GROUP = 16, 4, 4
AT_ONCE = 2
SECOND_SLOTS = 1 + 13 + 4 + 6 + 2 + 1 + N_EXPERTS * E_SLOTS + 1
MEM = 256
HD = 64
TOPK = 128
ARENA = 28000
NEG = -1e30
EPS = 1e-6

CONST = {}
_at = 0
for _n, _w in [("ident", P), ("ones", P), ("bones", P), ("rope", NT * 2 * HD), ("cmask", 4 * P), ("upper", P),
               ("lower", P), ("slower", P), ("supper", P), ("lev", 7 * P), ("levT", 7 * P), ("rank4", 4)]:
    CONST[_n] = (_at, _w)
    _at += _w
NCONST = _at

def _columns(widths):
    out, at = {}, 0
    for name, w in widths:
        out[name] = (at, w)
        at += w
    return out, at


PAR1, NPAR1 = _columns([
    ("ffn_norm0", KC), ("ffn_norm1", KC), ("mix_norm", KC), ("qk_norm", 10 * HD), ("mu", 7), ("w0", 2), ("a0", 2),
    ("k_k", 2), ("k_a", 2), ("r_k", 2), ("gn_w", 2), ("gn_b", 2), ("v0", 2), ("conv", 24), ("a_log", 4),
    ("dt_bias", 4), ("o_norm", 2), ("lora_up", 256), ("v_down", 64), ("v_up", 256)])
PAR2, NPAR2 = _columns([
    ("mem_norm", KC), ("mix_norm", KC), ("cross_norm", KC), ("moe_norm", KC), ("final_norm", KC), ("b_forget", 1),
    ("b_alpha", 2), ("fox_gain", 4), ("gla_gain", 4), ("b_router", 20), ("alpha_up", 256)])
NPAR = max(NPAR1, NPAR2)


class Counter:

    def __init__(self, sem, step=1):
        self.sem, self.step, self.path, self.off = sem, step, (), 0

    def bump(self):
        self.off += self.step
        return self.now()

    def now(self, back=0):
        return (self, self.path, self.off - back)


class Loop:

    def __init__(self, n):
        self.n, self.delta, self.i = n, {}, None

    def value(self, k):
        return self.i * k


class Line:

    def __init__(self, prog, name, counter):
        self.prog, self.name, self.counter, self.items, self.seen = prog, name, counter, [], {}

    def __call__(self, fn, after=(), signal=None, own=True):
        waits = list(after) + ([self.counter.now()] if own else [])
        self.items.append(("op", fn, self._new(waits), None if signal is False else (signal or self.counter)))
        if signal is False:
            return None
        return (signal or self.counter).bump()

    def wait(self, *after):
        self.items.append(("op", None, self._new(after), None))

    def _new(self, waits):
        best = {}
        for c, path, off in waits:
            if off <= 0 and not path:
                continue
            if c not in best or (path == c.path and off > best[c][1]) or best[c][0] != path:
                best[c] = (path, off)
        out = []
        for c, (path, off) in best.items():
            if self.seen.get(c, (None, 0))[0] == path and self.seen[c][1] >= off:
                continue
            self.seen[c] = (path, off)
            out.append((c, path, off))
        return out

    def emit(self, eng, items=None):
        for item in self.items if items is None else items:
            if item[0] == "loop":
                _, loop, body, start = item
                with eng.Fori(0, loop.n) as i:
                    loop.i = i
                    self.emit(eng, body)
                loop.i = None
                continue
            _, fn, waits, signal = item
            for counter, path, off in waits:
                value = off
                for loop, base in path:
                    turn = loop.delta.get(counter, 0)
                    value = value + base + (loop.i * turn if loop.i is not None else (loop.n - 1) * turn)
                eng.wait_ge(counter.sem, value)
            if fn is not None:
                made = fn(eng)
                if signal is not None:
                    made.then_inc(signal.sem, signal.step)


class Program:

    def __init__(self, nc, ctx):
        self.nc = nc
        self.sem = lambda name: ctx.enter_context(nc.semaphore(name))
        self.counters = []
        self.used = self.counter("slots_used")
        self.landed = [self.counter(f"slot{n}_landed", 16) for n in range(RING)]
        self.pe, self.act, self.dve, self.pool = (Line(self, n, self.counter(f"{n}_done"))
                                                  for n in ("pe", "act", "dve", "pool"))
        self.sp = Line(self, "sp", self.counter("misc_dma", 16))
        self.lines = [self.pe, self.act, self.dve, self.pool, self.sp]
        self.arrived, self.met, self.cleared = self.sem("arrived"), self.sem("met"), self.sem("cleared")
        self.slot = 0
        self.layer = None

    def counter(self, name, step=1):
        c = Counter(self.sem(name), step)
        self.counters.append(c)
        return c

    @contextmanager
    def loop(self, n):
        loop = Loop(n)
        saved = [(line, line.items) for line in self.lines]
        at = [(c, c.path, c.off) for c in self.counters]
        for c, path, off in at:
            c.path, c.off = (*path, (loop, off)), 0
        for line in self.lines:
            line.items, line.seen = [], {}
        first = self.slot
        yield loop
        assert (self.slot - first) % RING == 0
        self.slot = first + n * (self.slot - first)
        for c, path, off in at:
            loop.delta[c] = c.off
            c.path, c.off = path, off + n * c.off
        for line, items in saved:
            if line.items:
                items.append(("loop", loop, line.items, None))
            line.items, line.seen = items, {}

    @contextmanager
    def layers(self, n):
        self.layer = Loop(n)
        saved = [(line, line.items) for line in self.lines]
        for line in self.lines:
            line.items = []
        yield self.layer
        for line, items in saved:
            items.append(("loop", self.layer, line.items, None))
            line.items = items
        self.layer = None

    def epoch(self, before):
        layer = self.layer
        done = [c.now() for c in self.counters]

        def count(k):
            return k * (before + 1) + (layer.i * k if layer is not None else 0)

        for line in self.lines:
            line.wait(*done)
            if line is not self.sp:
                line.items.append(("op", lambda e: e.sem_inc(self.arrived, 1), [], None))
                line.items.append(("op", lambda e: e.wait_ge(self.cleared, count(1)), [], None))
        self.sp.items.append(("op", lambda e: e.wait_ge(self.arrived, count(4)), [], None))
        self.sp.items.append(("op", lambda e: e.sem_inc(self.met, 1), [], None))
        for c in self.counters:
            self.sp.items.append(("op", lambda e, c=c: e.sem_clear(c.sem), [], None))
        self.sp.items.append(("op", lambda e: e.sem_inc(self.cleared, 1), [], None))
        for c in self.counters:
            c.off = 0
        for line in self.lines:
            line.seen = {}
        self.slot = 0

    def take(self):
        s = self.slot % RING
        self.slot += 1
        return s, self.landed[s].bump()


def build(nc, x_in, mem_in, const_in, w1_in, w2_in, y_out):
    with ExitStack() as ctx:
        def sb(name, n):
            return ctx.enter_context(nc.sbuf_tensor(name, [P, n], F32))

        prog = Program(nc, ctx)
        pe, act, dve, pool, sp = prog.pe, prog.act, prog.dve, prog.pool, prog.sp
        pe_now, act_now, dve_now, pool_now = pe.counter.now, act.counter.now, dve.counter.now, pool.counter.now
        used_now = prog.used.now

        bank = [ctx.enter_context(nc.psum_tensor(f"bank{n}", [P, 512], F32)) for n in range(8)]
        xT = sb("xT", KC * SEQ)[:, :].rearrange("p (c t) -> p c t", c=KC)
        xn_at = -(-nc.sbuf_base // 32) * 32
        xn = sb("xn", KC * SEQ)[:, :].rearrange("p (c t) -> p c t", c=KC)
        ring = sb("ring", RING * SLOT)[:, :].rearrange("p (s n) -> p s n", s=RING)
        const = sb("const", NCONST)
        par = sb("par", NPAR)
        mixed_at = -(-nc.sbuf_base // 32) * 32
        mixed = sb("mixed", KC * SEQ)[:, :].rearrange("p (c t) -> p c t", c=KC)
        tmp = [sb(f"tmp{n}", 512) for n in range(4)]
        v_first = sb("v_first", 2 * SEQ)
        is_first = sb("is_first", 1)
        eps = sb("eps", 4)
        col = sb("col", 512)
        arena_at = -(-nc.sbuf_base // 32) * 32
        arena = sb("arena", ARENA)

        def over(name, offset, n):
            return nc.alloc_sbuf_tensor_at(name, [P, n], F32R, offset=offset)

        x_hi, x_lo = (over(n, at, KC * SEQ)[:, :].rearrange("p (c t) -> p c t", c=KC)
                      for n, at in (("x_hi", xn_at), ("x_lo", mixed_at)))
        HT = 2 * max(FFN_PARTS)
        h_hi, h_lo = (over(n, arena_at + 4 * (4 * SLOT + m * HT * SEQ), HT * SEQ)[:, :].rearrange("p (f t) -> p f t", t=SEQ)
                      for m, n in enumerate(("h_hi", "h_lo")))
        w_hi, w_lo = (over(n, arena_at + 4 * m * 2 * SLOT, 2 * SLOT)[:, :].rearrange(
            "p (s n) -> p s n", s=2) for m, n in enumerate(("w_hi", "w_lo")))
        GATES_AT = 4 * SLOT + (HT + 4 * AT_ONCE) * SEQ
        assert GATES_AT + N_EXPERTS * SEQ <= ARENA

        def C(name, n=None):
            a, w = CONST[name]
            return const[:, a:a + w] if n is None else const[:, a + n * P:a + (n + 1) * P]

        def par1(name):
            a, w = PAR1[name]
            return par[:, a:a + w]

        def par2(name):
            a, w = PAR2[name]
            return par[:, a:a + w]

        class Arena:

            def __init__(self):
                self.at = 0

            def take(self, n):
                a = self.at
                self.at += n
                assert self.at <= ARENA, self.at
                return arena[:, a:a + n]

        ident, ones, bones = C("ident"), C("ones"), C("bones")

        def wide(ap, shape):
            return ap.unsqueeze(len(ap.shape)).to_broadcast(shape)

        def sweep(ap, n):
            return ap.unsqueeze(1).to_broadcast([P, n, ap.shape[-1]])


        def everything():
            return [used_now(), pe_now(), act_now(), dve_now(), pool_now()]

        def reciprocal_root(out, in_, scale, eps_col, after):
            t = act(lambda e: e.activation(out, in_, ACT.Sqrt, bias=eps[:out.shape[0], eps_col:eps_col + 1],
                                           scale=scale), after=after)
            return dve(lambda e: e.reciprocal(out, out), after=[t])

        def rms_norm(src, gains, out, width, n=SEQ, ready=None, split=False):
            start = ready or [dve_now()]
            mm = [None] * 4
            for c in range(width):
                square = act(lambda e, c=c: e.activation(tmp[c % 4][:, :n], src[:, c, :], ACT.Square),
                             after=start + ([mm[c % 4]] if mm[c % 4] else [pe_now(), dve_now()]), own=False)
                mm[c % 4] = pe(lambda e, c=c: e.matmul(bank[0][:, :n], ones, tmp[c % 4][:, :n], start=c == 0,
                                                       stop=c == width - 1),
                               after=[square] + ([dve_now(), act_now(1)] if c == 0 else []), own=False)
            rstd = tmp[3][:, :n]
            reciprocal_root(rstd, bank[0][:, :n], 1.0 / (width * P), 0, [pe_now()])
            if split:
                for c in range(width):
                    full = tmp[c % 2][:, :n]
                    dve(lambda e, c=c, full=full: e.scalar_tensor_tensor(
                        out=full, in0=src[:, c, :], scalar=gains[:, c:c + 1], in1=rstd, op0=ALU.mult,
                        op1=ALU.mult), own=c == 0, after=[pe_now(), used_now(), act_now()])
                    t = dve(lambda e, c=c, full=full: e.tensor_scalar(x_hi[:, c, :], full, 1.0, None, ALU.mult))
                    dve(lambda e, c=c, full=full: e.tensor_tensor(x_lo[:, c, :], full, x_hi[:, c, :].bitcast(F32),
                                                                  ALU.subtract))
                return
            for c in range(width):
                dve(lambda e, c=c: e.scalar_tensor_tensor(out=out[:, c, :], in0=src[:, c, :],
                                                          scalar=gains[:, c:c + 1], in1=rstd, op0=ALU.mult,
                                                          op1=ALU.mult), own=c == 0, after=[pe_now(), used_now()])

        def columns(slot):
            return ring[:, slot, :].rearrange("p (k n) -> p k n", k=KC)

        def rows(slot):
            return ring[:, slot, :].rearrange("p (f n) -> p f n", f=2)

        def by_channel(slot, c0, out, src, last, after=(), m=P, n=SEQ):
            w = columns(slot)
            for k in range(KC):
                t = pe(lambda e, k=k: e.matmul(out, w[:, k, c0:c0 + m], src[:, k, :n], start=k == 0,
                                               stop=k == KC - 1),
                       after=after if k == 0 else (), own=False,
                       signal=(prog.used if last else pe.counter) if k == KC - 1 else False)
            return t

        def by_token(slot, c0, n, out, src, tile, last, after=()):
            w = columns(slot)
            for k in range(KC):
                t = pe(lambda e, k=k: e.matmul(out, src[:, k, tile * P:(tile + 1) * P], w[:, k, c0:c0 + n],
                                               start=k == 0, stop=k == KC - 1),
                       after=after if k == 0 else (), own=False,
                       signal=(prog.used if last else pe.counter) if k == KC - 1 else False)
            return t


        def split_slot():
            s, there = prog.take()
            hi = act(lambda e: e.activation(w_hi[:, s, :], ring[:, s, :], ACT.Copy), after=[there, pe_now()],
                     own=False)
            dve(lambda e: e.tensor_tensor(w_lo[:, s, :], ring[:, s, :], w_hi[:, s, :].bitcast(F32), ALU.subtract),
                after=[hi, used_now(), pe_now()], own=False, signal=prog.used)

        def passes(s):
            return ((w_hi[:, s, :], 0), (w_hi[:, s, :], 1), (w_lo[:, s, :], 0))

        def split_products(out, s, pick, data, ks, start, stop, after=(), signal=None):
            for k in ks:
                for n, (w, part) in enumerate(passes(s)):
                    end = k == ks[-1] and n == 2
                    t = pe(lambda e, k=k, w=w, part=part, n=n, end=end: e.matmul(
                        out, pick(w, k), data(part, k), start=start and k == ks[0] and n == 0, stop=stop and end),
                        after=after if k == ks[0] and n == 0 else (), own=False, signal=signal if end else False)
            return t

        def gate_up(j, finish_before=None, free=None):
            column = lambda w, k, f: w.rearrange("p (k n) -> p k n", k=KC)[:, k, f * P:(f + 1) * P]
            xs = lambda part, k: (x_hi, x_lo)[part][:, k, :]
            for n in range(2):
                ready = [used_now()] + ([free or dve_now()] if n == 0 else [])
                s = (prog.slot - 1) % RING
                split_slot()
                if n == 0 and finish_before is not None:
                    finish_before()
                for f in range(2):
                    split_products(bank[4 * j + 2 * n + f][:, :], s, lambda w, k, f=f: column(w, k, f), xs,
                                   range(KC), True, True, after=ready)

        def finish(j, index, gate=None):
            for f in range(2):
                full, g, u = tmp[2 * j + f][:, :], bank[4 * j + f], bank[4 * j + 2 + f]
                silu = act(lambda e, g=g, full=full: e.activation(full, g[:, :], ACT.Silu),
                           after=[pe_now(), dve_now()], own=False)
                dve(lambda e, u=u, full=full: e.tensor_tensor(full, full, u[:, :], ALU.mult),
                    after=[silu, pe_now()], own=False)
                if gate is not None:
                    dve(lambda e, full=full: e.tensor_tensor(full, full, gate(), ALU.mult))
                dve(lambda e, f=f, full=full: e.tensor_scalar(h_hi[:, index() + f, :], full, 1.0, None, ALU.mult))
                dve(lambda e, f=f, full=full: e.tensor_tensor(
                    h_lo[:, index() + f, :], full, h_hi[:, index() + f, :].bitcast(F32), ALU.subtract))

        def down(n, n_slots, ahead, post=None):
            ready = [used_now()]
            s = (prog.slot - 1) % RING
            if ahead:
                split_slot()
            if post is not None:
                post()
                ready.append(dve_now())
            rows_ = lambda w, k, d: w.rearrange("p (f n) -> p f n", f=2)[:, k, d * P:(d + 1) * P]
            out = []
            for d in range(KC):
                last = n == n_slots - 1
                out.append(split_products(
                    bank[d][:, :], s, lambda w, k, d=d: rows_(w, k, d),
                    lambda part, k: (h_hi, h_lo)[part][:, 2 * n + k, :], range(2), n == 0, last, after=ready,
                    signal=None if last or d == KC - 1 else False))
            return out

        def down_slot(hidden, index, start, stop):
            slot, there = prog.take()
            w = rows(slot)
            pe.wait(there)
            ready = []
            for d in range(KC):
                for f in range(2):
                    end = d == KC - 1 and f == 1
                    t = pe(lambda e, d=d, f=f: e.matmul(bank[d][:, :], w[:, f, d * P:(d + 1) * P],
                                                        hidden(index() + f), start=start and f == 0,
                                                        stop=stop and f == 1), own=False,
                           signal=prog.used if end else (pe.counter if stop and f == 1 else False))
                ready.append(t)
            return ready

        def add_to_residual(ready, scale):
            for d in range(KC):
                dve(lambda e, d=d: e.scalar_tensor_tensor(out=xT[:, d, :], in0=bank[d][:, :], scalar=scale,
                                                          in1=xT[:, d, :], op0=ALU.mult, op1=ALU.add),
                    after=[ready[d]], own=d == 0)

        def ffn(norm):
            sync_all()
            split_slot()
            rms_norm(xT, norm, xn, KC, split=True)
            pe.wait(dve_now(), act_now())
            for part, pairs in enumerate(FFN_PARTS):
                gate_up(0, free=dve_now(4) if part else None)
                turns, odd = divmod(pairs - 1, 2)
                with prog.loop(turns) as turn:
                    gate_up(1, lambda turn=turn: finish(0, lambda: turn.i * 4))
                    gate_up(0, lambda turn=turn: finish(1, lambda: turn.i * 4 + 2))
                if odd:
                    gate_up(1, lambda turns=turns: finish(0, lambda: 4 * turns))
                for n in range(pairs):
                    ready = down(n, pairs, part + 1 < len(FFN_PARTS) or n + 1 < pairs,
                                 (lambda turns=turns, odd=odd: finish(odd, lambda: 4 * turns + 2 * odd)) if n == 0 else None)
                add_to_residual(ready, 0.5)

        def project_out(scale=1.0):
            pe.wait(*everything())
            for s in range(4):
                ready = down_slot(lambda c: mixed[:, c, :], lambda s=s: 2 * s, s == 0, s == 3)
            add_to_residual(ready, scale)

        def load_parameters(n):
            slot, there = prog.take()
            copied = pool(lambda e: e.tensor_copy(par[:, :n], ring[:, slot, :n]), after=[there], own=False,
                          signal=prog.used)
            for line in (pe, act, dve):
                line.wait(copied)

        def sync_all():
            done = everything()
            for line in (pe, act, dve, pool):
                line.wait(*done)

        def transpose(out, in_, after=(), signal=None):
            n = in_.shape[0]
            return pe(lambda e: e.transpose(out, in_, ident[:n, :n]), after=after, own=False, signal=signal)

        def unit_inverse(Lt, T, Tt, after):
            pe.wait(*after)
            for lv in range(1, 7):
                last = lv == 6
                stages = []
                for q in range(NT):
                    t = [pe(lambda e, q=q, h=h: e.matmul(bank[q][:, h * P:(h + 1) * P], Lt[:, q, h, :],
                                                         T[:, q, h, :], start=True, stop=True),
                            after=[dve_now()] if q == 0 and h == 0 else (), own=False,
                            signal=None if h == 3 else False) for h in range(4)][3]
                    stages.append(dve(lambda e, q=q, lv=lv: e.tensor_tensor(
                        tmp[q][:, :].rearrange("p (h s) -> p h s", h=4),
                        bank[q][:, :].rearrange("p (h s) -> p h s", h=4), sweep(C("lev", lv), 4), ALU.mult),
                        after=[t], own=False))
                for q in range(NT):
                    b0, b1 = bank[q], bank[4 + q]
                    if not last:
                        t0 = [pe(lambda e, q=q, h=h, b0=b0: e.matmul(b0[:, h * P:(h + 1) * P], Tt[:, q, h, :],
                                                              tmp[q][:, h * P:(h + 1) * P], start=True, stop=True),
                                 after=[stages[q]], own=False, signal=None if h == 3 else False)
                              for h in range(4)][3]
                    t1 = [pe(lambda e, q=q, h=h, b1=b1: e.matmul(b1[:, h * P:(h + 1) * P], tmp[q][:, h * P:(h + 1) * P],
                                                          Tt[:, q, h, :], start=True, stop=True),
                             after=[stages[q]], own=False, signal=None if h == 3 else False)
                          for h in range(4)][3]
                    if not last:
                        dve(lambda e, q=q, b0=b0: e.tensor_tensor(T[:, q], T[:, q], b0[:, :].rearrange(
                            "p (h s) -> p h s", h=4), ALU.add), after=[t0], own=False)
                    dve(lambda e, q=q, b1=b1: e.tensor_tensor(Tt[:, q], Tt[:, q], b1[:, :].rearrange(
                        "p (h s) -> p h s", h=4), ALU.add), after=[t1], own=False)

        def softmax_rows(scores, w, out, scale, mask=None, after=(), buf=0):
            mx = col[:, 480 + 4 * buf:481 + 4 * buf]
            nm = col[:, 481 + 4 * buf:482 + 4 * buf]
            sm = col[:, 482 + 4 * buf:483 + 4 * buf]
            iv = col[:, 483 + 4 * buf:484 + 4 * buf]
            if mask is None:
                dve(lambda e: e.tensor_reduce(mx, scores, AX, ALU.max), after=after)
                src = scores
            else:
                dve(lambda e: e.tensor_tensor_reduce(out=out, in0=scores, in1=mask, scale=1.0, scalar=-3e38,
                                                     op0=ALU.add, op1=ALU.max, accum_out=mx), after=after)
                src = out
            t = dve(lambda e: e.tensor_scalar(nm, mx, -scale, None, ALU.mult))
            t = act(lambda e: e.activation(out, src, ACT.Exp, bias=nm, scale=scale, accum_out=sm), after=[t])
            dve(lambda e: e.reciprocal(iv, sm), after=[t])
            return dve(lambda e: e.tensor_scalar(out, out, iv, None, ALU.mult))

        def attend(p_row, w, values, out, buf, after):
            tb = bank[2 + buf]
            turned = tmp[2 + buf]
            n = w // P
            for s in range(n):
                t = transpose(tb[:, s * P:(s + 1) * P], p_row[:, s * P:(s + 1) * P],
                              after=after if s == 0 else (), signal=None if s == n - 1 else False)
            t = act(lambda e: e.activation(turned[:, :w], tb[:, :w], ACT.Copy), after=[t, pe_now()])
            for s in range(n):
                r = pe(lambda e, s=s: e.matmul(out, values(s), turned[:, s * P:(s + 1) * P], start=s == 0,
                                               stop=s == n - 1), after=[t], own=False,
                       signal=None if s == n - 1 else False)
            return r


        there = [sp(lambda e: e.dma_start(const[:, :], const_in), own=False),
                 sp(lambda e: e.dma_start(xT, x_in), own=False)][-1]
        for n, v in enumerate((1e-6, 1e-12, 64e-5, 0.0)):
            dve(lambda e, n=n, v=v: e.memset(eps[:, n:n + 1], v), own=False)
        dve(lambda e: e.memset(is_first[:, :], 1.0), own=False)
        dve(lambda e: e.memset(v_first[:, :], 0.0), own=False)
        for line in (pe, act, dve, pool):
            line.wait(there)
        prog.epoch(0)


        def attention_projections(A):
            tok = A.take(NT * 20 * HD).rearrange("p (t n) -> p t n", t=NT)
            v = A.take(NT * P).rearrange("p (t n) -> p t n", t=NT)
            for n, (width, dst) in enumerate([(256, 0), (256, 256), (256, 512), (256, 640), (256, 896)]):
                slot, there = prog.take()
                for t in range(NT):
                    b = bank[4 * (n % 2) + t]
                    r = by_token(slot, 0, width, b[:, :width], xn, t, t == NT - 1,
                                 after=[there, act_now(NT) if n in (2, 3) else act_now(), dve_now()])
                    if n == 2:
                        act(lambda e, b=b, t=t: e.activation(tok[:, t, 512:640], b[:, 0:128], ACT.Copy),
                            after=[r], own=False)
                        act(lambda e, b=b, t=t: e.activation(v[:, t, :], b[:, 128:256], ACT.Copy), after=[r],
                            own=False)
                    else:
                        act(lambda e, b=b, t=t, dst=dst: e.activation(tok[:, t, dst:dst + 256], b[:, 0:256],
                                                                      ACT.Copy), after=[r], own=False)
            return tok, v

        def shifted(raw, mu, out, ready):
            dve(lambda e: e.tensor_tensor(out, raw[:, 0:SEQ], raw[:, 1:SEQ + 1], ALU.subtract), after=ready)
            return dve(lambda e: e.scalar_tensor_tensor(out=out, in0=out, scalar=mu, in1=raw[:, 1:SEQ + 1],
                                                        op0=ALU.mult, op1=ALU.add))

        def mixed_slot(A):
            keys = A.take(NT * P).rearrange("p (t n) -> p t n", t=NT)
            small = A.take(NT * 16).rearrange("p (t n) -> p t n", t=NT)
            raw = A.take(SEQ + 1)
            lora = A.take(SEQ)
            slot, there = prog.take()
            free = [dve_now(), act_now()]
            for t in range(NT):
                r = by_token(slot, 0, 80, bank[t][:, 0:80], xn, t, False, after=[there] + free)
                act(lambda e, t=t: e.activation(keys[:, t, 0:64], bank[t][:, 0:64], ACT.Copy), after=[r], own=False)
                act(lambda e, t=t: e.activation(small[:, t, :], bank[t][:, 64:80], ACT.Copy), after=[r], own=False)
            r = by_channel(slot, P, bank[4][:, :], xn, True)
            act(lambda e: e.activation(raw[:, 1:SEQ + 1], bank[4][:, :], ACT.Copy), after=[r], own=False)
            dve(lambda e: e.memset(raw[:, 0:1], 0.0))
            shifted(raw, par1("mu")[:, 6:7], lora, [act_now()])
            act(lambda e: e.activation(lora[0:32, :], lora[0:32, :], ACT.Tanh), after=[dve_now()])
            act(lambda e: e.activation(lora[64:128, :], lora[64:128, :], ACT.Sigmoid), after=[dve_now()])
            return keys, small, lora

        def dsa(tok, keys, small, v, A):
            heads = tok.rearrange("p t (h d) -> p t h d", d=HD)
            turned = A.take(10 * SEQ).rearrange("p (b t) -> p b t", b=10)
            work = A.take(20 * HD)
            other = A.take(20 * HD)
            stat = col[:, 0:40].rearrange("p (t h) -> p t h", t=NT)
            rope = C("rope").rearrange("p (t n) -> p t n", t=NT)
            w3 = work.rearrange("p (h d) -> p h d", d=HD)
            o3 = other.rearrange("p (h d) -> p h d", d=HD)
            for t in range(NT):
                for n in range(2):
                    act(lambda e, t=t, n=n: e.activation(tok[:, t, (18 + n) * HD:(19 + n) * HD], keys[:, t, 0:64],
                                                         ACT.Copy), after=[act_now(), dve_now()])
                act(lambda e, t=t: e.activation(work[:, 0:640], tok[:, t, 0:640], ACT.Square), after=[dve_now()])
                dve(lambda e, t=t: e.tensor_reduce(stat[:, t, :], w3[:, 0:10, :], AX, ALU.add), after=[act_now()])
                reciprocal_root(stat[:, t, :], stat[:, t, :], 1.0 / HD, 0, [dve_now()])
                dve(lambda e, t=t: e.tensor_tensor(heads[:, t, 0:10, :], heads[:, t, 0:10, :],
                                                   wide(stat[:, t, :], [P, 10, HD]), ALU.mult))
                dve(lambda e, t=t: e.tensor_tensor(tok[:, t, 0:640], tok[:, t, 0:640], par1("qk_norm"), ALU.mult))
                cos, sin = rope[:, t, 0:HD], rope[:, t, HD:2 * HD]
                pool(lambda e, t=t, sin=sin: e.tensor_tensor(w3[:, :, 0:32], heads[:, t, :, 32:64],
                                                             sweep(sin[:, 0:32], 20), ALU.mult),
                     after=[dve_now(), act_now()])
                pool(lambda e, t=t, sin=sin: e.tensor_tensor(w3[:, :, 32:64], heads[:, t, :, 0:32],
                                                             sweep(sin[:, 32:64], 20), ALU.mult))
                dve(lambda e, t=t, cos=cos: e.tensor_tensor(o3, heads[:, t], sweep(cos, 20), ALU.mult),
                    after=[pe_now()])
                r = dve(lambda e: e.tensor_tensor(other, other, work, ALU.add), after=[pool_now()])
                for b in range(10):
                    dst = bank[b // 4][:, (b % 4) * P:(b % 4 + 1) * P]
                    transpose(dst, other[:, b * P:(b + 1) * P], after=[r, act_now()], signal=None if b == 9 else False)
                for g in range(3):
                    n = 4 if g < 2 else 2
                    act(lambda e, g=g, n=n, t=t: e.activation(
                        turned[:, 4 * g:4 * g + n, t * P:(t + 1) * P],
                        bank[g][:, 0:n * P].rearrange("p (b t) -> p b t", b=n), ACT.Copy), after=[pe_now()])
            sync_all()
            dve(lambda e: e.tensor_scalar(small[:, :, 0:8], small[:, :, 0:8], float(8 ** -0.5 * 64 ** -0.5), None,
                                          ALU.mult))
            score, spare = work[:, 0:512], other[:, 0:512]
            for q in range(NT):
                w = P * (q + 1)
                mask = C("cmask")[:, 4 * P - w:4 * P]
                keep = tok[:, 0, 0:w] if False else tok[:, q, 0:w]
                if q > 0:
                    for h in range(8):
                        base = HD * (h % 2)
                        b = bank[h % 4]
                        r = pe(lambda e, h=h, b=b, base=base, q=q, w=w: e.matmul(
                            b[:, :w], turned[base:base + HD, 5 + h // 2, q * P:(q + 1) * P],
                            turned[base:base + HD, 9, 0:w], start=True, stop=True), after=[act_now()], own=False)
                        positive = tmp[h % 2]
                        a = act(lambda e, b=b, positive=positive, w=w: e.activation(positive[:, :w], b[:, :w],
                                                                                    ACT.Relu),
                                after=[r, dve_now()], own=False)
                        if h == 0:
                            dve(lambda e, q=q, w=w, positive=positive: e.tensor_scalar(
                                score[:, :w], positive[:, :w], small[:, q, 0:1], None, ALU.mult), after=[a])
                        else:
                            dve(lambda e, q=q, w=w, h=h, positive=positive: e.scalar_tensor_tensor(
                                out=score[:, :w], in0=positive[:, :w], scalar=small[:, q, h:h + 1],
                                in1=score[:, :w], op0=ALU.mult, op1=ALU.add), after=[a])
                    dve(lambda e, w=w, mask=mask: e.tensor_tensor(score[:, :w], score[:, :w], mask, ALU.add))
                    dve(lambda e, w=w: e.tensor_copy(spare[:, :w], score[:, :w]))
                    best = col[:, 64:72]
                    for _ in range(TOPK // 8 - 1):
                        dve(lambda e, w=w: e.max(best, spare[:, :w]))
                        dve(lambda e, w=w: e.match_replace(spare[:, :w], best, spare[:, :w], 3 * NEG))
                    dve(lambda e, w=w: e.max(best, spare[:, :w]))
                    thr, need = col[:, 71:72], col[:, 72:73]
                    dve(lambda e, w=w, keep=keep: e.tensor_scalar(keep, score[:, :w], thr, None, ALU.is_gt))
                    dve(lambda e, keep=keep: e.tensor_reduce(need, keep, AX, ALU.add))
                    dve(lambda e: e.tensor_scalar(need, need, -1.0, float(TOPK), ALU.mult, ALU.add))
                    dve(lambda e, w=w: e.tensor_scalar(score[:, :w], score[:, :w], thr, None, ALU.is_equal))
                    dve(lambda e, w=w: e.tensor_tensor_scan(spare[:, :w], const[:, CONST["ones"][0]:CONST["ones"][0] + 1].to_broadcast([P, w]),
                                                            score[:, :w], 0.0, ALU.mult, ALU.add))
                    dve(lambda e, w=w: e.scalar_tensor_tensor(out=score[:, :w], in0=spare[:, :w], scalar=need,
                                                              in1=score[:, :w], op0=ALU.is_le, op1=ALU.mult))
                    dve(lambda e, w=w, keep=keep: e.tensor_tensor(keep, keep, score[:, :w], ALU.add))
                    dve(lambda e, keep=keep: e.tensor_scalar(keep, keep, -1.0, -NEG, ALU.add, ALU.mult))
                else:
                    dve(lambda e, keep=keep, mask=mask: e.tensor_copy(keep, mask))
            sync_all()
            for q in range(NT):
                w = P * (q + 1)
                keep = tok[:, q, 0:w]
                for h in range(8):
                    base, buf = HD * (h // 4), h % 2
                    r = pe(lambda e, h=h, base=base, q=q, w=w, buf=buf: e.matmul(
                        bank[buf][:, :w], turned[base:base + HD, h % 4, q * P:(q + 1) * P],
                        turned[base:base + HD, 4, 0:w], start=True, stop=True), after=[act_now(), dve_now()],
                        own=False)
                    p_row = tmp[buf][:, :w]
                    s = softmax_rows(bank[buf][:, :w], w, p_row, HD ** -0.5, mask=keep, after=[r], buf=buf)
                    g, o = h // 4, bank[4 + h % 2]
                    dst = o[HD * (h % 2):HD * (h % 2) + HD, 0:P]
                    r = attend(p_row, w, lambda s, g=g: v[:, s, g * HD:(g + 1) * HD], dst, buf, [s, dve_now()])
                    act(lambda e, h=h, q=q, dst=dst: e.activation(
                        mixed[HD * (h % 2):HD * (h % 2) + HD, h // 2, q * P:(q + 1) * P], dst, ACT.Copy), after=[r])

        def head_sum(dst, src, after):
            return pe(lambda e: e.matmul(dst, bones, src, start=True, stop=True), after=after, own=False)

        def normalize(x, scale, eps_col, factor, wrk):
            for c in range(2):
                act(lambda e, c=c: e.activation(wrk[c], x[:, c, :], ACT.Square), after=[dve_now(), pe_now()])
                r = head_sum(bank[6 + c][:, :], wrk[c], [act_now(), dve_now()])
                reciprocal_root(wrk[c], bank[6 + c][:, :], scale, eps_col, [r])
                dve(lambda e, c=c: e.scalar_tensor_tensor(out=x[:, c, :], in0=x[:, c, :], scalar=factor,
                                                          in1=wrk[c], op0=ALU.mult, op1=ALU.mult))

        def two(ap):
            return ap.rearrange("p (c t) -> p c t", c=2)

        def rwkv(lora, A):
            raw = [A.take(SEQ + 1) for _ in range(2)]
            r_, k_, v_ = (two(A.take(2 * SEQ)) for _ in range(3))
            for b in range(2):
                dve(lambda e, b=b: e.memset(raw[b][:, 0:1], 0.0))
            for n, dst in enumerate((r_, k_, v_)):
                slot, there = prog.take()
                for c in range(2):
                    b = bank[2 * (n % 2) + c]
                    t = by_channel(slot, c * P, b[:, :], xn, c == 1, after=[there, act_now()])
                    act(lambda e, b=b, c=c: e.activation(raw[c][:, 1:SEQ + 1], b[:, :], ACT.Copy),
                        after=[t, dve_now()])
                    shifted(raw[c], par1("mu")[:, 2 * n + c:2 * n + c + 1], dst[:, c, :], [act_now()])
            ld, a_, g_, kk = (two(A.take(2 * SEQ)) for _ in range(4))
            up = par1("lora_up")
            for c in range(2):
                for n, (lo, hi, dst, bias) in enumerate(((0, 32, ld, "w0"), (32, 64, a_, "a0"), (64, 128, g_, None))):
                    b = bank[4 + n]
                    t = pe(lambda e, lo=lo, hi=hi, c=c, b=b: e.matmul(b[:, :], up[lo:hi, c * P:(c + 1) * P],
                                                                      lora[lo:hi, :], start=True, stop=True),
                           after=[act_now(), dve_now()])
                    if bias:
                        act(lambda e, b=b, dst=dst, c=c, bias=bias: e.activation(
                            dst[:, c, :], b[:, :], ACT.Sigmoid, bias=par1(bias)[:, c:c + 1]), after=[t])
                    else:
                        act(lambda e, b=b, dst=dst, c=c: e.activation(dst[:, c, :], b[:, :], ACT.Copy), after=[t])
            dve(lambda e: e.tensor_scalar(ld, ld, -0.6065306597126334, None, ALU.mult), after=[act_now()])
            for c in range(2):
                dve(lambda e, c=c: e.tensor_scalar(kk[:, c, :], k_[:, c, :], par1("k_k")[:, c:c + 1], None, ALU.mult))
            normalize(kk, 1.0, 1, 1.0, [tmp[0][:, :], tmp[1][:, :]])
            for c in range(2):
                t_ = tmp[c][:, :]
                dve(lambda e, c=c, t_=t_: e.tensor_scalar(t_, a_[:, c, :], -1.0, par1("k_a")[:, c:c + 1], ALU.add,
                                                          ALU.mult))
                dve(lambda e, c=c, t_=t_: e.scalar_tensor_tensor(out=k_[:, c, :], in0=t_, scalar=1.0,
                                                                 in1=k_[:, c, :], op0=ALU.add, op1=ALU.mult))
            vf = two(v_first[:, :])
            dve(lambda e: e.tensor_tensor(two(arena[:, A.at:A.at + 1024]), v_, vf, ALU.subtract))
            dve(lambda e: e.scalar_tensor_tensor(out=vf, in0=two(arena[:, A.at:A.at + 1024]), scalar=is_first[:, 0:1],
                                                 in1=vf, op0=ALU.mult, op1=ALU.add))
            vd = par1("v_down")
            for c in range(2):
                t = pe(lambda e, c=c: e.matmul(bank[0][0:32, :], vd[:, 32 * c:32 * c + 32], v_[:, c, :],
                                               start=c == 0, stop=c == 1), after=[dve_now(), act_now()])
            low = tmp[2][0:32, :]
            act(lambda e: e.activation(low, bank[0][0:32, :], ACT.Copy), after=[t])
            for c in range(2):
                t = pe(lambda e, c=c: e.matmul(bank[1 + c][:, :], par1("v_up")[0:32, c * P:(c + 1) * P], low,
                                               start=True, stop=True), after=[act_now()])
                act(lambda e, c=c: e.activation(tmp[c][:, :], bank[1 + c][:, :], ACT.Sigmoid,
                                                bias=par1("v0")[:, c:c + 1]), after=[t, dve_now()])
            df = two(arena[:, A.at:A.at + 1024])
            dve(lambda e: e.tensor_tensor(df, vf, v_, ALU.subtract), after=[pe_now()])
            for c in range(2):
                dve(lambda e, c=c: e.tensor_tensor(df[:, c, :], df[:, c, :], tmp[c][:, :], ALU.mult),
                    after=[act_now()])
            dve(lambda e: e.tensor_tensor(v_, v_, df, ALU.add))
            bonus = two(A.take(2 * SEQ))
            for c in range(2):
                t = dve(lambda e, c=c: e.scalar_tensor_tensor(out=tmp[c][:, :], in0=r_[:, c, :],
                                                              scalar=par1("r_k")[:, c:c + 1], in1=k_[:, c, :],
                                                              op0=ALU.mult, op1=ALU.mult))
                t = head_sum(bank[c][:, :], tmp[c][:, :], [t, act_now()])
                dve(lambda e, c=c: e.tensor_tensor(bonus[:, c, :], v_[:, c, :], bank[c][:, :], ALU.mult), after=[t])
            cm, e_pos, e_neg, e_prev = (A.take(2 * SEQ) for _ in range(4))
            tiles = lambda ap: ap.rearrange("p (n t) -> p n t", t=P)
            ldf = ld.rearrange("p c t -> p (c t)")
            for n in range(8):
                dve(lambda e, n=n: e.tensor_tensor_scan(cm[:, n * P:(n + 1) * P], ones, ldf[:, n * P:(n + 1) * P],
                                                        0.0, ALU.mult, ALU.add), own=n == 0)
            mid, end = col[:, 0:8], col[:, 8:16]
            dve(lambda e: e.tensor_copy(mid, tiles(cm)[:, :, 63]))
            dve(lambda e: e.tensor_tensor(tiles(cm), tiles(cm), wide(mid, [P, 8, P]), ALU.subtract))
            t = dve(lambda e: e.tensor_tensor(e_prev, cm, ldf, ALU.subtract))
            act(lambda e: e.activation(e_prev, e_prev, ACT.Exp), after=[t])
            act(lambda e: e.activation(e_pos, cm, ACT.Exp))
            act(lambda e: e.activation(e_neg, cm, ACT.Exp, scale=-1.0))
            act(lambda e: e.activation(mid, mid, ACT.Exp))
            t = act(lambda e: e.activation(end, tiles(cm)[:, :, P - 1], ACT.Exp))
            flat = lambda ap: ap.rearrange("p c t -> p (c t)")
            af, kf, kkf, rf = flat(a_), flat(k_), flat(kk), flat(r_)
            dve(lambda e: e.tensor_tensor(af, af, kkf, ALU.mult), after=[t])
            dve(lambda e: e.tensor_tensor(af, af, e_neg, ALU.mult))
            dve(lambda e: e.scalar_tensor_tensor(out=e_prev, in0=kkf, scalar=-1.0, in1=e_prev, op0=ALU.mult,
                                                 op1=ALU.mult))
            dve(lambda e: e.tensor_tensor(e_neg, kf, e_neg, ALU.mult))
            dve(lambda e: e.tensor_tensor(e_pos, rf, e_pos, ALU.mult))
            At, Bt, Kt, Rt = e_prev, af, e_neg, e_pos
            sync_all()
            v_tok, b_tok, k_tok = (x.rearrange("p (t n) -> p t n", t=NT) for x in (rf, kf, kkf))
            for n, (src, dst) in enumerate(((flat(v_), v_tok), (Bt, b_tok), (Kt, k_tok))):
                for c in range(2):
                    b = bank[n * 2 + c]
                    for t in range(NT):
                        r = transpose(b[:, t * P:(t + 1) * P], src[:, c * SEQ + t * P:c * SEQ + (t + 1) * P],
                                      signal=None if t == 3 else False)
                    act(lambda e, b=b, dst=dst, c=c: e.activation(dst[:, :, c * P:(c + 1) * P],
                                                                  b[:, :].rearrange("p (t n) -> p t n", t=NT),
                                                                  ACT.Copy), after=[r], own=False)
            sync_all()
            quad = lambda ap: ap.rearrange("p (q h t) -> p q h t", q=NT, h=4)
            Lt, T, Tt = (quad(A.take(NT * 4 * P)) for _ in range(3))

            def scores(lhs, rhs, q, b, after=()):
                for half in range(2):
                    for c in range(2):
                        cols = slice(c * SEQ + q * P, c * SEQ + (q + 1) * P)
                        part = slice(half * HD, (half + 1) * HD)
                        t = pe(lambda e, half=half, c=c, cols=cols, part=part: e.matmul(
                            b[half][:, c * P:(c + 1) * P], lhs[part, cols], rhs[part, cols], start=True, stop=True),
                            after=after if half == 0 and c == 0 else (), own=False,
                            signal=None if half and c else False)
                return t

            def masked(dst, b, mask, after):
                for half in range(2):
                    dve(lambda e, half=half: e.tensor_tensor(
                        dst[:, 2 * half:2 * half + 2, :], b[half][:, 0:2 * P].rearrange("p (h t) -> p h t", h=2),
                        sweep(mask, 2), ALU.mult), after=after if half == 0 else (), own=False)

            for q in range(NT):
                b = (bank[4 * (q % 2)], bank[4 * (q % 2) + 1])
                t = scores(At, Bt, q, b, [dve_now(6) if q > 1 else dve_now()])
                masked(T[:, q], b, C("lev", 0), [t])
                b = (bank[4 * (q % 2) + 2], bank[4 * (q % 2) + 3])
                t = scores(Bt, At, q, b)
                masked(Tt[:, q], b, C("levT", 0), [t])
                masked(Lt[:, q], b, C("supper"), [t])
            for X in (T, Tt):
                for q in range(NT):
                    dve(lambda e, X=X, q=q: e.tensor_tensor(X[:, q], X[:, q], sweep(ident, 4), ALU.add),
                        own=q == 0)
            unit_inverse(Lt, T, Tt, [dve_now()])
            sync_all()
            state = A.take(2 * HD).rearrange("p (c i) -> p c i", c=2)
            scaled = A.take(2 * HD).rearrange("p (c i) -> p c i", c=2)
            wv, sa = (A.take(4 * HD).rearrange("p (h i) -> p h i", h=4) for _ in range(2))
            AK, RB, RK = (T[:, n] for n in range(3))
            y = two(A.take(2 * SEQ))
            dve(lambda e: e.memset(state, 0.0))
            for q in range(NT):
                for n, (lhs, rhs, mask, dst) in enumerate(((Kt, At, "supper", AK), (Bt, Rt, "upper", RB),
                                                           (Kt, Rt, "upper", RK))):
                    b = (bank[2 * n], bank[2 * n + 1])
                    t = scores(lhs, rhs, q, b, [dve_now(), act_now()])
                    masked(dst, b, C(mask), [t, pe_now()])
                for c in range(2):
                    dve(lambda e, c=c, q=q: e.tensor_scalar(scaled[:, c, :], state[:, c, :],
                                                            mid[:, 4 * c + q:4 * c + q + 1], None, ALU.mult))
                pe.wait(dve_now())
                for half in range(2):
                    part = slice(half * HD, (half + 1) * HD)
                    for c in range(2):
                        h, o = 2 * half + c, bank[6 + half][:, c * HD:(c + 1) * HD]
                        pe(lambda e, part=part, c=c, o=o, q=q: e.matmul(
                            o, At[part, c * SEQ + q * P:c * SEQ + (q + 1) * P], scaled[part, c, :], start=True,
                            stop=False), own=False, signal=False)
                        t = pe(lambda e, h=h, o=o, q=q, c=c, half=half: e.matmul(
                            o, AK[:, h, :], v_tok[:, q, c * P + half * HD:c * P + (half + 1) * HD], start=False,
                            stop=True), own=False)
                    dve(lambda e, half=half: e.tensor_copy(wv[:, 2 * half:2 * half + 2, :], bank[6 + half][
                        :, 0:2 * HD].rearrange("p (h i) -> p h i", h=2)), after=[t], own=False)
                for h in range(4):
                    t = pe(lambda e, h=h, q=q: e.matmul(bank[6][:, 256 + h * HD:256 + (h + 1) * HD], Tt[:, q, h, :],
                                                        wv[:, h, :], start=True, stop=True), after=[dve_now()],
                           own=False)
                dve(lambda e: e.tensor_copy(sa, bank[6][:, 256:512].rearrange("p (h i) -> p h i", h=4)), after=[t])
                pe.wait(dve_now(), act_now())
                vs = lambda h, q=q: v_tok[:, q, (h % 2) * P + (h // 2) * HD:(h % 2) * P + (h // 2 + 1) * HD]
                for half in range(2):
                    part = slice(half * HD, (half + 1) * HD)
                    for c in range(2):
                        h, o = 2 * half + c, bank[half][part, c * P:(c + 1) * P]
                        cols = slice(c * SEQ + q * P, c * SEQ + (q + 1) * P)
                        pe(lambda e, o=o, part=part, c=c, cols=cols: e.matmul(
                            o, scaled[part, c, :], Rt[part, cols], start=True, stop=False), own=False, signal=False)
                        pe(lambda e, o=o, h=h: e.matmul(o, sa[:, h, :], RB[:, h, :], start=False, stop=False),
                           own=False, signal=False)
                        t = pe(lambda e, o=o, h=h, vs=vs: e.matmul(o, vs(h), RK[:, h, :], start=False, stop=True),
                               own=False)
                    act(lambda e, half=half, part=part, q=q: e.activation(
                        y[part, :, q * P:(q + 1) * P], bank[half][part, 0:2 * P].rearrange("p (c t) -> p c t", c=2),
                        ACT.Copy), after=[t], own=False)
                for half in range(2):
                    part = slice(half * HD, (half + 1) * HD)
                    for c in range(2):
                        h, o = 2 * half + c, bank[2 + half][part, c * HD:(c + 1) * HD]
                        hs = slice(c * P + half * HD, c * P + (half + 1) * HD)
                        pe(lambda e, o=o, h=h, hs=hs, q=q: e.matmul(o, b_tok[:, q, hs], sa[:, h, :], start=True,
                                                                    stop=False), own=False, signal=False)
                        t = pe(lambda e, o=o, hs=hs, h=h, vs=vs, q=q: e.matmul(o, k_tok[:, q, hs], vs(h), start=False,
                                                                               stop=True), own=False)
                    dve(lambda e, half=half, part=part: e.tensor_tensor(
                        state[part], scaled[part], bank[2 + half][part, 0:2 * HD].rearrange("p (c i) -> p c i", c=2),
                        ALU.add), after=[t], own=False)
                for c in range(2):
                    dve(lambda e, c=c, q=q: e.tensor_scalar(state[:, c, :], state[:, c, :],
                                                            end[:, 4 * c + q:4 * c + q + 1], None, ALU.mult))
            for c in range(2):
                t = head_sum(bank[c][:, :], y[:, c, :], [act_now(), dve_now()])
                dve(lambda e, c=c: e.scalar_tensor_tensor(out=y[:, c, :], in0=bank[c][:, :], scalar=-1.0 / HD,
                                                          in1=y[:, c, :], op0=ALU.mult, op1=ALU.add), after=[t])
            normalize(y, 1.0 / HD, 2, 1.0, [tmp[0][:, :], tmp[1][:, :]])
            for c in range(2):
                dve(lambda e, c=c: e.tensor_scalar(y[:, c, :], y[:, c, :], par1("gn_w")[:, c:c + 1],
                                                   par1("gn_b")[:, c:c + 1], ALU.mult, ALU.add))
                dve(lambda e, c=c: e.tensor_tensor(y[:, c, :], y[:, c, :], bonus[:, c, :], ALU.add))
                dve(lambda e, c=c: e.tensor_tensor(mixed[:, 4 + c, :], y[:, c, :], g_[:, c, :], ALU.mult))

        def delta_rule(small, A):
            raw = [A.take(SEQ + 3) for _ in range(2)]
            q_, k_, v_, z_ = (two(A.take(2 * SEQ)) for _ in range(4))
            for b in range(2):
                dve(lambda e, b=b: e.memset(raw[b][:, 0:3], 0.0))
            cw = par1("conv")
            for n, dst in enumerate((q_, k_, v_, z_)):
                slot, there = prog.take()
                for c in range(2):
                    b = bank[2 * (n % 2) + c]
                    t = by_channel(slot, c * P, b[:, :], xn, c == 1, after=[there, act_now()])
                    if n == 3:
                        act(lambda e, b=b, c=c: e.activation(z_[:, c, :], b[:, :], ACT.Silu), after=[t])
                        continue
                    act(lambda e, b=b, c=c: e.activation(raw[c][:, 3:SEQ + 3], b[:, :], ACT.Copy),
                        after=[t, dve_now()])
                    at = 4 * (2 * n + c)
                    dve(lambda e, c=c, dst=dst, at=at: e.tensor_scalar(dst[:, c, :], raw[c][:, 3:SEQ + 3],
                                                                       cw[:, at + 3:at + 4], None, ALU.mult),
                        after=[act_now()])
                    for j in range(3):
                        dve(lambda e, c=c, j=j, dst=dst, at=at: e.scalar_tensor_tensor(
                            out=dst[:, c, :], in0=raw[c][:, j:j + SEQ], scalar=cw[:, at + j:at + j + 1],
                            in1=dst[:, c, :], op0=ALU.mult, op1=ALU.add))
                    act(lambda e, c=c, dst=dst: e.activation(dst[:, c, :], dst[:, c, :], ACT.Silu),
                        after=[dve_now()])
            wrk = [tmp[0][:, :], tmp[1][:, :]]
            normalize(q_, 1.0, 0, HD ** -0.5, wrk)
            normalize(k_, 1.0, 0, 1.0, wrk)
            stat = col[:, 0:256].rearrange("p (n t h) -> p n t h", n=16, h=4)
            beta, g, gc, egc, w_, x_, y_, nb, nbe, gl = (stat[:, n] for n in range(10))
            ea = col[:, 256:260]
            act(lambda e: e.activation(beta, small[:, :, 8:12], ACT.Sigmoid), after=[dve_now()])
            dve(lambda e: e.tensor_tensor(g, small[:, :, 12:16], sweep(par1("dt_bias"), NT), ALU.add),
                after=[act_now()])
            dve(lambda e: e.tensor_scalar(w_, g, 0.0, None, ALU.max))
            dve(lambda e: e.tensor_scalar(x_, g, 0.0, None, ALU.min))
            dve(lambda e: e.tensor_tensor(x_, x_, w_, ALU.subtract))
            act(lambda e: e.activation(x_, x_, ACT.Exp), after=[dve_now()])
            act(lambda e: e.activation(x_, x_, ACT.Ln, bias=1.0))
            act(lambda e: e.activation(ea, par1("a_log"), ACT.Exp))
            dve(lambda e: e.tensor_tensor(w_, w_, x_, ALU.add), after=[act_now()])
            dve(lambda e: e.scalar_tensor_tensor(out=g, in0=w_, scalar=-1.0, in1=sweep(ea, NT), op0=ALU.mult,
                                                 op1=ALU.mult))
            pe(lambda e: e.matmul(bank[0][:, 0:16], C("upper"), g, start=True, stop=True),
               after=[dve_now(), act_now()])
            t = pe(lambda e: e.matmul(bank[1][:, 0:16], ones, g, start=True, stop=True))
            dve(lambda e: e.tensor_copy(gc.rearrange("p t h -> p (t h)"), bank[0][:, 0:16]), after=[t])
            dve(lambda e: e.tensor_copy(gl.rearrange("p t h -> p (t h)"), bank[1][:, 0:16]))
            dve(lambda e: e.tensor_tensor(x_, gl, gc, ALU.subtract))
            act(lambda e: e.activation(egc, gc, ACT.Exp), after=[dve_now()])
            act(lambda e: e.activation(x_, x_, ACT.Exp))
            act(lambda e: e.activation(gl, gl, ACT.Exp))
            dve(lambda e: e.tensor_scalar(nb, beta, -1.0, None, ALU.mult), after=[act_now()])
            dve(lambda e: e.tensor_tensor(nbe, nb, egc, ALU.mult))
            flat = lambda ap: ap.rearrange("p c t -> p (c t)")
            qf, kf, vf = flat(q_), flat(k_), flat(v_)
            k_tok, vb = (A.take(NT * 256).rearrange("p (t n) -> p t n", t=NT) for _ in range(2))
            sync_all()
            for c in range(2):
                for t in range(NT):
                    r = transpose(bank[c][:, t * P:(t + 1) * P], kf[:, c * SEQ + t * P:c * SEQ + (t + 1) * P],
                                  signal=None if t == 3 else False)
                act(lambda e, c=c: e.activation(k_tok[:, :, c * P:(c + 1) * P],
                                                bank[c][:, :].rearrange("p (t n) -> p t n", t=NT), ACT.Copy),
                    after=[r], own=False)
                for t in range(NT):
                    r = transpose(bank[2 + c][:, t * P:(t + 1) * P], vf[:, c * SEQ + t * P:c * SEQ + (t + 1) * P],
                                  signal=None if t == 3 else False)
                for half in range(2):
                    dve(lambda e, c=c, half=half: e.tensor_tensor(
                        vb[:, :, c * P + half * HD:c * P + (half + 1) * HD],
                        bank[2 + c][:, :].rearrange("p (t n) -> p t n", t=NT)[:, :, half * HD:(half + 1) * HD],
                        wide(beta[:, :, 2 * half + c], [P, NT, HD]), ALU.mult), after=[r], own=False)
            sync_all()
            quad = lambda ap: ap.rearrange("p (q h t) -> p q h t", q=NT, h=4)
            Lt, T, Tt, Xt = (quad(A.take(NT * 4 * P)) for _ in range(4))
            h4 = lambda ap: ap.rearrange("p (h t) -> p h t", h=4)
            dec, dst_, att = (h4(tmp[n][:, :]) for n in range(3))
            for q in range(NT):
                for h in range(4):
                    t = pe(lambda e, q=q, h=h: e.matmul(bank[0][:, h * P:(h + 1) * P],
                                                        g[:, q, h:h + 1].to_broadcast([P, P]), C("upper"),
                                                        start=True, stop=True), after=[dve_now()], own=False)
                dve(lambda e, q=q: e.tensor_tensor(dec, h4(bank[0][:, :]), wide(gc[:, q, :], [P, 4, P]),
                                                   ALU.subtract), after=[t])
                dve(lambda e: e.tensor_scalar(dec, dec, 0.0, None, ALU.max))
                act(lambda e: e.activation(dec, dec, ACT.Exp, scale=-1.0), after=[dve_now()])
                dve(lambda e: e.tensor_tensor(dec, dec, sweep(C("lower"), 4), ALU.mult), after=[act_now()])
                for n, src in enumerate((kf, qf)):
                    for half in range(2):
                        for c in range(2):
                            cols = slice(c * SEQ + q * P, c * SEQ + (q + 1) * P)
                            part = slice(half * HD, (half + 1) * HD)
                            t = pe(lambda e, n=n, half=half, c=c, cols=cols, part=part, src=src: e.matmul(
                                bank[2 + 2 * n + half][:, c * P:(c + 1) * P], src[part, cols], kf[part, cols],
                                start=True, stop=True), own=False, after=[dve_now()])
                    for half in range(2):
                        dve(lambda e, n=n, half=half: e.tensor_tensor(
                            (dst_, att)[n][:, 2 * half:2 * half + 2, :],
                            bank[2 + 2 * n + half][:, 0:2 * P].rearrange("p (h t) -> p h t", h=2),
                            dec[:, 2 * half:2 * half + 2, :], ALU.mult), after=[t, pe_now()])
                dve(lambda e, q=q: e.tensor_tensor(dst_, dst_, wide(nb[:, q, :], [P, 4, P]), ALU.mult))
                dve(lambda e: e.tensor_tensor(dst_, dst_, sweep(C("slower"), 4), ALU.mult))
                dve(lambda e, q=q: e.tensor_tensor(T[:, q], dst_, sweep(C("lev", 0), 4), ALU.mult))
                for n, src in enumerate((dst_, att)):
                    for h in range(4):
                        t = transpose(bank[6 + n][:, h * P:(h + 1) * P], src[:, h, :], after=[dve_now(), act_now()],
                                      signal=None if h == 3 else False)
                    act(lambda e, n=n, q=q: e.activation((Lt, Xt)[n][:, q], h4(bank[6 + n][:, :]), ACT.Copy),
                        after=[t])
                dve(lambda e, q=q: e.tensor_tensor(Tt[:, q], Lt[:, q], sweep(C("levT", 0), 4), ALU.mult),
                    after=[act_now(), pe_now()])
            for X in (T, Tt):
                for q in range(NT):
                    dve(lambda e, X=X, q=q: e.tensor_tensor(X[:, q], X[:, q], sweep(ident, 4), ALU.add),
                        own=q == 0)
            sync_all()
            unit_inverse(Lt, T, Tt, [dve_now()])
            for c in range(2):
                for q in range(NT):
                    for half in range(2):
                        h = 2 * half + c
                        t = pe(lambda e, c=c, q=q, h=h, half=half: e.matmul(
                            bank[c][half * HD:(half + 1) * HD, q * P:(q + 1) * P],
                            g[:, q, h:h + 1].to_broadcast([P, HD]), C("upper"), start=True, stop=True),
                            after=[dve_now(), act_now()], own=False)
                act(lambda e, c=c: e.activation(tmp[c][:, :], bank[c][:, :], ACT.Exp), after=[t])
                dve(lambda e, c=c: e.tensor_tensor(q_[:, c, :], q_[:, c, :], tmp[c][:, :], ALU.mult),
                    after=[act_now()])
            sync_all()
            state = A.take(2 * HD).rearrange("p (c i) -> p c i", c=2)
            rest, vn, vs = (A.take(4 * HD).rearrange("p (h i) -> p h i", h=4) for _ in range(3))
            y = two(A.take(2 * SEQ))
            dve(lambda e: e.memset(state, 0.0))
            for q in range(NT):
                pe.wait(dve_now(), act_now())
                for half in range(2):
                    part = slice(half * HD, (half + 1) * HD)
                    for c in range(2):
                        h, o = 2 * half + c, bank[6 + half][:, c * HD:(c + 1) * HD]
                        t = pe(lambda e, part=part, c=c, o=o, q=q: e.matmul(
                            o, kf[part, c * SEQ + q * P:c * SEQ + (q + 1) * P], state[part, c, :], start=True,
                            stop=True), own=False)
                    for c in range(2):
                        h, o = 2 * half + c, bank[6 + half][:, c * HD:(c + 1) * HD]
                        dve(lambda e, o=o, h=h, q=q, c=c, half=half: e.scalar_tensor_tensor(
                            out=rest[:, h, :], in0=o, scalar=nbe[:, q, h:h + 1],
                            in1=vb[:, q, c * P + half * HD:c * P + (half + 1) * HD], op0=ALU.mult, op1=ALU.add),
                            after=[t], own=False)
                for h in range(4):
                    t = pe(lambda e, h=h, q=q: e.matmul(bank[5][:, h * HD:(h + 1) * HD], Tt[:, q, h, :],
                                                        rest[:, h, :], start=True, stop=True), after=[dve_now()],
                           own=False)
                v4 = bank[5][:, 0:256].rearrange("p (h i) -> p h i", h=4)
                dve(lambda e, v4=v4: e.tensor_copy(vn, v4), after=[t])
                dve(lambda e, q=q: e.tensor_tensor(vs, vn, wide(x_[:, q, :], [P, 4, HD]), ALU.mult))
                pe.wait(dve_now())
                for half in range(2):
                    part = slice(half * HD, (half + 1) * HD)
                    for c in range(2):
                        h, o = 2 * half + c, bank[half][part, c * P:(c + 1) * P]
                        cols = slice(c * SEQ + q * P, c * SEQ + (q + 1) * P)
                        pe(lambda e, o=o, part=part, c=c, cols=cols: e.matmul(
                            o, state[part, c, :], qf[part, cols], start=True, stop=False), own=False, signal=False)
                        t = pe(lambda e, o=o, h=h, q=q: e.matmul(o, vn[:, h, :], Xt[:, q, h, :], start=False,
                                                                 stop=True), own=False)
                    act(lambda e, half=half, part=part, q=q: e.activation(
                        y[part, :, q * P:(q + 1) * P], bank[half][part, 0:2 * P].rearrange("p (c t) -> p c t", c=2),
                        ACT.Copy), after=[t], own=False)
                for half in range(2):
                    part = slice(half * HD, (half + 1) * HD)
                    for c in range(2):
                        h, o = 2 * half + c, bank[2 + half][part, c * HD:(c + 1) * HD]
                        hs = slice(c * P + half * HD, c * P + (half + 1) * HD)
                        t = pe(lambda e, o=o, h=h, hs=hs, q=q: e.matmul(o, k_tok[:, q, hs], vs[:, h, :], start=True,
                                                                        stop=True), own=False)
                    for c in range(2):
                        h, o = 2 * half + c, bank[2 + half][part, c * HD:(c + 1) * HD]
                        dve(lambda e, o=o, part=part, c=c, h=h, q=q: e.scalar_tensor_tensor(
                            out=state[part, c, :], in0=state[part, c, :], scalar=gl[part, q, h:h + 1], in1=o,
                            op0=ALU.mult, op1=ALU.add), after=[t, pe_now()], own=False)
            sync_all()
            normalize(y, 1.0 / HD, 0, 1.0, wrk)
            for c in range(2):
                dve(lambda e, c=c: e.scalar_tensor_tensor(out=mixed[:, 6 + c, :], in0=y[:, c, :],
                                                          scalar=par1("o_norm")[:, c:c + 1], in1=z_[:, c, :],
                                                          op0=ALU.mult, op1=ALU.mult))

        with prog.layers(DEPTH):
            load_parameters(NPAR1)
            ffn(par1("ffn_norm0"))
            rms_norm(xT, par1("mix_norm"), xn, KC)
            sync_all()
            A = Arena()
            tok, v = attention_projections(A)
            keys, small, lora = mixed_slot(A)
            keep_at = A.at
            sync_all()
            dsa(tok, keys, small, v, A)
            sync_all()
            A = Arena()
            small2 = A.take(NT * 16).rearrange("p (t n) -> p t n", t=NT)
            lora2 = A.take(SEQ)
            dve(lambda e: e.tensor_copy(small2, small))
            dve(lambda e: e.tensor_copy(lora2, lora))
            sync_all()
            start = A.at
            rwkv(lora2, A)
            sync_all()
            A.at = start
            delta_rule(small2, A)
            sync_all()
            project_out()
            ffn(par1("ffn_norm1"))
            dve(lambda e: e.memset(is_first[:, :], 0.0))
            assert prog.slot == LAYER_SLOTS, prog.slot
            prog.epoch(1)


        load_parameters(NPAR2)

        def fox(A):
            q_, k_ = (A.take(4 * SEQ).rearrange("p (c t) -> p c t", c=4) for _ in range(2))
            v = A.take(NT * 512).rearrange("p (t n) -> p t n", t=NT)
            n = 0
            for dst in (q_, k_):
                for s in range(2):
                    slot, there = prog.take()
                    for c in range(2):
                        b = bank[n % 4]
                        n += 1
                        t = by_channel(slot, c * P, b[:, :], xn, c == 1, after=[there, act_now()])
                        act(lambda e, b=b, dst=dst, c=2 * s + c: e.activation(dst[:, c, :], b[:, :], ACT.Copy),
                            after=[t], own=False)
            for s in range(2):
                slot, there = prog.take()
                for t in range(NT):
                    b = bank[4 + t]
                    r = by_token(slot, 0, 256, b[:, 0:256], xn, t, t == NT - 1, after=[there, act_now()])
                    act(lambda e, b=b, t=t, s=s: e.activation(v[:, t, 256 * s:256 * s + 256], b[:, 0:256], ACT.Copy),
                        after=[r], own=False)
            slot, there = prog.take()
            t = by_channel(slot, 0, bank[0][0:48, :], xn, True, after=[there, act_now()], m=48)
            cf, ga = A.take(SEQ), A.take(SEQ)
            s1, s2 = tmp[0][0:8, :], tmp[1][0:8, :]
            act(lambda e: e.activation(ga[32:48, :], bank[0][32:48, :], ACT.Copy), after=[t])
            log_sigmoid(cf[0:8, :], bank[0][0:8, :], par2("b_forget")[0:8, 0:1], s1, s2)
            dve(lambda e: e.tensor_tensor_scan(s1, ones[0:8, 0:1].to_broadcast([8, SEQ]), cf[0:8, :], 0.0, ALU.mult,
                                               ALU.add))
            dve(lambda e: e.tensor_scalar(cf[0:8, :], s1, -(HD ** 0.5), None, ALU.mult))
            sync_all()
            for q in range(NT):
                w = P * (q + 1)
                for h in range(8):
                    base, buf = HD * (h % 2), h % 2
                    b = bank[buf]
                    pe(lambda e, h=h, base=base, q=q, w=w, b=b: e.matmul(
                        b[:, :w], q_[base:base + HD, h // 2, q * P:(q + 1) * P], k_[base:base + HD, h // 2, 0:w],
                        start=True, stop=False), after=[act_now(), dve_now()], own=False, signal=False)
                    r = pe(lambda e, h=h, w=w, b=b: e.matmul(b[:, :w], ident[0:8, h:h + 1].to_broadcast([8, P]),
                                                             cf[0:8, 0:w], start=False, stop=True), own=False)
                    p_row = tmp[buf][:, :w]
                    s = softmax_rows(b[:, :w], w, p_row, HD ** -0.5, mask=C("cmask")[:, 4 * P - w:4 * P], after=[r],
                                     buf=buf)
                    dst = bank[4 + buf][HD * buf:HD * buf + HD, 0:P]
                    r = attend(p_row, w, lambda s, h=h: v[:, s, h * HD:(h + 1) * HD], dst, buf, [s, dve_now()])
                    act(lambda e, h=h, q=q, dst=dst: e.activation(
                        mixed[HD * (h % 2):HD * (h % 2) + HD, h // 2, q * P:(q + 1) * P], dst, ACT.Copy), after=[r])
            sync_all()
            for c in range(2):
                normalize(mixed[:, 2 * c:2 * c + 2, :], 1.0 / HD, 0, 1.0, [tmp[0][:, :], tmp[1][:, :]])
            for c in range(4):
                dve(lambda e, c=c: e.tensor_scalar(mixed[:, c, :], mixed[:, c, :], par2("fox_gain")[:, c:c + 1], None,
                                                   ALU.mult))
            return ga

        def log_sigmoid(out, in_, bias, s1, s2):
            dve(lambda e: e.tensor_scalar(out, in_, bias, None, ALU.add), after=[pe_now(), used_now(), act_now()])
            dve(lambda e: e.tensor_scalar(s1, out, 0.0, None, ALU.max))
            dve(lambda e: e.tensor_scalar(s2, out, 0.0, None, ALU.min))
            dve(lambda e: e.tensor_tensor(s1, s2, s1, ALU.subtract))
            act(lambda e: e.activation(s1, s1, ACT.Exp), after=[dve_now()])
            act(lambda e: e.activation(s1, s1, ACT.Ln, bias=1.0))
            dve(lambda e: e.tensor_tensor(out, s2, s1, ALU.subtract), after=[act_now()])

        def gla(ga, A):
            q_, k_ = (A.take(2 * SEQ) for _ in range(2))
            gate = A.take(4 * SEQ).rearrange("p (c t) -> p c t", c=4)
            v = A.take(NT * 512).rearrange("p (t n) -> p t n", t=NT)
            for dst, scale in ((q_, HD ** -0.5), (k_, 1.0)):
                slot, there = prog.take()
                for c in range(2):
                    b = bank[c]
                    t = by_channel(slot, c * P, b[:, :], xn, c == 1, after=[there, act_now()])
                    act(lambda e, b=b, dst=dst, c=c, scale=scale: e.activation(dst[:, c * SEQ:(c + 1) * SEQ],
                                                                              b[:, :], ACT.Copy, scale=scale),
                        after=[t])
            for s in range(2):
                slot, there = prog.take()
                for t in range(NT):
                    b = bank[4 + t]
                    r = by_token(slot, 0, 256, b[:, 0:256], xn, t, t == NT - 1, after=[there, act_now()])
                    act(lambda e, b=b, t=t, s=s: e.activation(v[:, t, 256 * s:256 * s + 256], b[:, 0:256], ACT.Copy),
                        after=[r], own=False)
            for s in range(2):
                slot, there = prog.take()
                for c in range(2):
                    b = bank[2 * s + c]
                    t = by_channel(slot, c * P, b[:, :], xn, c == 1, after=[there, act_now()])
                    act(lambda e, b=b, c=2 * s + c: e.activation(gate[:, c, :], b[:, :], ACT.Silu), after=[t],
                        own=False)
            la, cs, eq, ek = (A.take(2 * SEQ) for _ in range(4))
            for c in range(2):
                pe(lambda e, c=c: e.matmul(bank[4 + c][:, :], par2("alpha_up")[32:48, c * P:(c + 1) * P],
                                           ga[32:48, :], start=True, stop=True), after=[act_now(), dve_now()])
                log_sigmoid(la[:, c * SEQ:(c + 1) * SEQ], bank[4 + c][:, :], par2("b_alpha")[:, c:c + 1], tmp[0][:, :],
                            tmp[1][:, :])
            dve(lambda e: e.tensor_scalar(la, la, 1.0 / 16.0, None, ALU.mult))
            for n in range(8):
                dve(lambda e, n=n: e.tensor_tensor_scan(cs[:, n * P:(n + 1) * P], ones, la[:, n * P:(n + 1) * P],
                                                        0.0, ALU.mult, ALU.add), own=n == 0)
            tiles = lambda ap: ap.rearrange("p (n t) -> p n t", t=P)
            end = col[:, 0:8]
            dve(lambda e: e.tensor_copy(end, tiles(cs)[:, :, P - 1]))
            dve(lambda e: e.tensor_tensor(tiles(ek), wide(end, [P, 8, P]), tiles(cs), ALU.subtract))
            act(lambda e: e.activation(ek, ek, ACT.Exp), after=[dve_now()])
            act(lambda e: e.activation(end, end, ACT.Exp))
            dve(lambda e: e.tensor_tensor(ek, ek, k_, ALU.mult), after=[act_now()])
            k_tok = A.take(NT * 256).rearrange("p (t n) -> p t n", t=NT)
            sync_all()
            for c in range(2):
                for t in range(NT):
                    r = transpose(bank[c][:, t * P:(t + 1) * P], ek[:, c * SEQ + t * P:c * SEQ + (t + 1) * P],
                                  signal=None if t == 3 else False)
                act(lambda e, c=c: e.activation(k_tok[:, :, c * P:(c + 1) * P],
                                                bank[c][:, :].rearrange("p (t n) -> p t n", t=NT), ACT.Copy),
                    after=[r], own=False)
            sync_all()
            att = A.take(NT * 4 * P).rearrange("p (q h t) -> p q h t", q=NT, h=4)
            level_scores = lambda kx, qx, use: [use(q, half, score_pair(kx, qx, q, half))
                                                for q in range(NT) for half in range(2)]

            def score_pair(kx, qx, q, half):
                b = bank[2 * q + half]
                for c in range(2):
                    cols = slice(c * SEQ + q * P, c * SEQ + (q + 1) * P)
                    part = slice(half * HD, (half + 1) * HD)
                    t = pe(lambda e, b=b, c=c, cols=cols, part=part: e.matmul(
                        b[:, c * P:(c + 1) * P], kx[part, cols], qx[part, cols], start=True, stop=True),
                        after=[dve_now(7)] if c == 0 else (), own=False, signal=None if c else False)
                return t

            def pair_of(q, half):
                return (att[:, q, 2 * half:2 * half + 2, :],
                        bank[2 * q + half][:, 0:2 * P].rearrange("p (h t) -> p h t", h=2))

            def diagonal(q, half, t):
                dst, src = pair_of(q, half)
                dve(lambda e: e.tensor_tensor(dst, src, sweep(ident, 2), ALU.mult), after=[t], own=False)

            pe.wait(dve_now())
            level_scores(k_, q_, diagonal)
            dve(lambda e: e.memset(eq, 0.0), after=[pe_now()])
            dve(lambda e: e.memset(ek, 0.0))
            for lv in range(7):
                half_w = 1 << lv
                view = lambda ap, h=half_w: ap.rearrange("p (n s h) -> p n s h", s=2, h=h)
                ref = view(cs)[:, :, 0, half_w - 1].unsqueeze(2).to_broadcast([P, 512 // half_w, half_w])
                late, early = view(cs)[:, :, 1, :], view(cs)[:, :, 0, :]
                dve(lambda e, ref=ref, late=late, view=view: e.tensor_tensor(view(eq)[:, :, 1, :], late, ref,
                                                                             ALU.subtract), after=[pe_now()])
                dve(lambda e, ref=ref, early=early, view=view: e.tensor_tensor(view(ek)[:, :, 0, :], ref, early,
                                                                               ALU.subtract))
                act(lambda e, view=view: e.activation(view(eq)[:, :, 1, :], view(eq)[:, :, 1, :], ACT.Exp),
                    after=[dve_now()])
                act(lambda e, view=view: e.activation(view(ek)[:, :, 0, :], view(ek)[:, :, 0, :], ACT.Exp))
                dve(lambda e, view=view: e.tensor_tensor(view(eq)[:, :, 1, :], view(eq)[:, :, 1, :],
                                                         view(q_)[:, :, 1, :], ALU.mult), after=[act_now()])
                dve(lambda e, view=view: e.tensor_tensor(view(ek)[:, :, 0, :], view(ek)[:, :, 0, :],
                                                         view(k_)[:, :, 0, :], ALU.mult))
                pe.wait(dve_now())
                mask = sweep(C("levT", lv), 2).bitcast(U32)

                def into(q, half, t, mask=mask):
                    dst, src = pair_of(q, half)
                    dve(lambda e: e.copy_predicated(dst, mask, src), after=[t], own=False)

                level_scores(ek, eq, into)
            act(lambda e: e.activation(eq, cs, ACT.Exp), after=[pe_now(), dve_now()])
            dve(lambda e: e.tensor_tensor(eq, eq, q_, ALU.mult), after=[act_now()])
            sync_all()
            state = A.take(2 * P).rearrange("p (c v) -> p c v", c=2)
            dve(lambda e: e.memset(state, 0.0))
            for q in range(NT):
                pe.wait(dve_now(), act_now())
                for half in range(2):
                    part = slice(half * HD, (half + 1) * HD)
                    for c in range(2):
                        h, head = 2 * half + c, 2 * c + half
                        o = bank[half][:, c * P:(c + 1) * P]
                        pe(lambda e, o=o, part=part, c=c, q=q: e.matmul(
                            o, state[part, c, :], eq[part, c * SEQ + q * P:c * SEQ + (q + 1) * P], start=True,
                            stop=False), own=False, signal=False)
                        t = pe(lambda e, o=o, h=h, head=head, q=q: e.matmul(
                            o, v[:, q, head * P:(head + 1) * P], att[:, q, h, :], start=False, stop=True), own=False)
                    act(lambda e, half=half, q=q: e.activation(
                        mixed[:, 4 + half:8:2, q * P:(q + 1) * P],
                        bank[half][:, 0:2 * P].rearrange("p (c t) -> p c t", c=2), ACT.Copy), after=[t], own=False)
                for half in range(2):
                    part = slice(half * HD, (half + 1) * HD)
                    for c in range(2):
                        head, o = 2 * c + half, bank[2 + half][part, c * P:(c + 1) * P]
                        hs = slice(c * P + half * HD, c * P + (half + 1) * HD)
                        t = pe(lambda e, o=o, hs=hs, head=head, q=q: e.matmul(
                            o, k_tok[:, q, hs], v[:, q, head * P:(head + 1) * P], start=True, stop=True), own=False)
                    for c in range(2):
                        o = bank[2 + half][part, c * P:(c + 1) * P]
                        dve(lambda e, o=o, part=part, c=c, q=q: e.scalar_tensor_tensor(
                            out=state[part, c, :], in0=state[part, c, :], scalar=end[part, 4 * c + q:4 * c + q + 1],
                            in1=o, op0=ALU.mult, op1=ALU.add), after=[t, pe_now()], own=False)
            sync_all()
            for h in range(4):
                y = mixed[:, 4 + h, :]
                w_ = tmp[h % 2][:, :]
                act(lambda e, y=y, w_=w_: e.activation(w_, y, ACT.Square), after=[dve_now()])
                r = pe(lambda e, h=h, w_=w_: e.matmul(bank[h][:, :], ones, w_, start=True, stop=True),
                       after=[act_now()])
                reciprocal_root(w_, bank[h][:, :], 1.0 / P, 0, [r])
                dve(lambda e, y=y, w_=w_, h=h: e.scalar_tensor_tensor(out=y, in0=y, scalar=par2("gla_gain")[:, h:h + 1],
                                                                      in1=w_, op0=ALU.mult, op1=ALU.mult))
                dve(lambda e, y=y, h=h: e.tensor_tensor(y, y, gate[:, h, :], ALU.mult))

        def cross(A):
            mem = A.take(KC * MEM).rearrange("p (c m) -> p c m", c=KC)
            mn = A.take(KC * MEM).rearrange("p (c m) -> p c m", c=KC)
            there = sp(lambda e: e.dma_start(mem, mem_in), after=everything())
            for line in (act, dve):
                line.wait(there)
            rms_norm(mem, par2("mem_norm"), mn, KC, n=MEM)
            sync_all()
            rms_norm(xT, par2("cross_norm"), xn, KC)
            sync_all()
            q_ = A.take(4 * SEQ).rearrange("p (c t) -> p c t", c=4)
            k_ = A.take(4 * MEM).rearrange("p (c t) -> p c t", c=4)
            v = A.take(2 * 512).rearrange("p (t n) -> p t n", t=2)
            for dst, src, n in ((q_, xn, SEQ), (k_, mn, MEM)):
                for s in range(2):
                    slot, there = prog.take()
                    for c in range(2):
                        b = bank[2 * s + c]
                        t = by_channel(slot, c * P, b[:, :n], src, c == 1, after=[there, act_now()], n=n)
                        act(lambda e, b=b, dst=dst, n=n, c=2 * s + c: e.activation(dst[:, c, :], b[:, :n], ACT.Copy),
                            after=[t], own=False)
            for s in range(2):
                slot, there = prog.take()
                for t in range(2):
                    b = bank[4 + t]
                    r = by_token(slot, 0, 256, b[:, 0:256], mn, t, t == 1, after=[there, act_now()])
                    act(lambda e, b=b, t=t, s=s: e.activation(v[:, t, 256 * s:256 * s + 256], b[:, 0:256], ACT.Copy),
                        after=[r], own=False)
            sync_all()
            for q in range(NT):
                for h in range(4):
                    buf = h % 2
                    r = pe(lambda e, h=h, q=q, buf=buf: e.matmul(bank[buf][:, :MEM], q_[:, h, q * P:(q + 1) * P],
                                                                 k_[:, h, :], start=True, stop=True),
                           after=[act_now(), dve_now()], own=False)
                    p_row = tmp[buf][:, :MEM]
                    s = softmax_rows(bank[buf][:, :MEM], MEM, p_row, P ** -0.5, after=[r, act_now()], buf=buf)
                    dst = bank[4 + buf][:, 0:P]
                    r = attend(p_row, MEM, lambda s, h=h: v[:, s, h * P:(h + 1) * P], dst, buf, [s, dve_now()])
                    act(lambda e, h=h, q=q, dst=dst: e.activation(mixed[:, h, q * P:(q + 1) * P], dst, ACT.Copy),
                        after=[r])
            pe.wait(*everything())
            for s in range(2):
                ready = down_slot(lambda c: mixed[:, c, :], lambda s=s: 2 * s, s == 0, s == 1)
            add_to_residual(ready, 1.0)

        def router():
            gates = arena[:, GATES_AT:GATES_AT + N_EXPERTS * SEQ].rearrange("p (e t) -> p e t", e=N_EXPERTS)
            slot, there = prog.take()
            for t in range(NT):
                r = by_token(slot, 0, 20, bank[t][:, 0:20], xn, t, t == NT - 1, after=[there, dve_now(), act_now()])
                dve(lambda e, t=t: e.tensor_tensor(col[:, 20 * t:20 * t + 20], bank[t][:, 0:20], par2("b_router"),
                                                   ALU.add), after=[r])
            logits = col[:, 0:80].rearrange("p (t n) -> p t n", t=NT)
            four = lambda n: col[:, 96 + 16 * n:112 + 16 * n].rearrange("p (t n) -> p t n", t=NT)
            one = lambda n: col[:, 80 + 4 * n:84 + 4 * n]
            ex, oh, es, o1, o2, w_ = (four(n) for n in range(6))
            mx, pg, p1, p2 = (one(n) for n in range(4))
            big = col[:, 192:256].rearrange("p (t e n) -> p t e n", t=NT, e=4)
            rank = sweep(C("rank4"), NT)
            over = lambda ap: wide(ap, [P, NT, 4])

            def first_of(dst, src, top):
                dve(lambda e: e.tensor_tensor(dst, src, over(top), ALU.is_equal))
                dve(lambda e: e.tensor_tensor(dst, dst, rank, ALU.mult))
                dve(lambda e: e.tensor_reduce(mx, dst, AX, ALU.max))
                dve(lambda e: e.tensor_tensor(dst, dst, over(mx), ALU.is_equal))

            def softmax4(dst, src):
                dve(lambda e: e.tensor_reduce(mx, src, AX, ALU.max))
                dve(lambda e: e.tensor_tensor(dst, src, over(mx), ALU.subtract))
                act(lambda e: e.activation(dst, dst, ACT.Exp), after=[dve_now()])
                dve(lambda e: e.tensor_reduce(mx, dst, AX, ALU.add), after=[act_now()])
                dve(lambda e: e.reciprocal(mx, mx))
                dve(lambda e: e.tensor_tensor(dst, dst, over(mx), ALU.mult))

            softmax4(ex, logits[:, :, 0:4])
            dve(lambda e: e.tensor_reduce(pg, ex, AX, ALU.max))
            first_of(oh, ex, pg)
            for t in range(NT):
                for g in range(4):
                    dve(lambda e, t=t, g=g: e.tensor_scalar(big[:, t, :, g], logits[:, t, 4 + 4 * g:8 + 4 * g],
                                                            oh[:, t, g:g + 1], None, ALU.mult))
            dve(lambda e: e.tensor_reduce(es.rearrange("p t n -> p (t n)"), big.rearrange("p t e n -> p (t e) n"),
                                          AX, ALU.add))
            softmax4(es, es)
            dve(lambda e: e.tensor_reduce(p1, es, AX, ALU.max))
            first_of(o1, es, p1)
            dve(lambda e: e.scalar_tensor_tensor(out=w_, in0=o1, scalar=-4.0, in1=es, op0=ALU.mult, op1=ALU.add))
            dve(lambda e: e.tensor_reduce(p2, w_, AX, ALU.max))
            first_of(o2, w_, p2)
            dve(lambda e: e.tensor_tensor(o1, o1, over(p1), ALU.mult))
            dve(lambda e: e.tensor_tensor(o2, o2, over(p2), ALU.mult))
            dve(lambda e: e.tensor_tensor(o1, o1, o2, ALU.add))
            dve(lambda e: e.tensor_tensor(mx, p1, p2, ALU.add))
            dve(lambda e: e.reciprocal(mx, mx))
            dve(lambda e: e.tensor_tensor(pg, pg, mx, ALU.mult))
            dve(lambda e: e.tensor_tensor(o1, o1, over(pg), ALU.mult))
            table = col[:, 256:320].rearrange("p (t g n) -> p t g n", t=NT, g=4)
            for t in range(NT):
                for g in range(4):
                    dve(lambda e, t=t, g=g: e.tensor_scalar(table[:, t, g, :], o1[:, t, :], oh[:, t, g:g + 1], None,
                                                            ALU.mult))
            for t in range(NT):
                r = transpose(bank[0][0:16, t * P:(t + 1) * P], col[:, 256 + 16 * t:272 + 16 * t], after=[dve_now()],
                              signal=None if t == 3 else False)
            turned = tmp[0][0:16, :]
            dve(lambda e: e.tensor_copy(turned, bank[0][0:16, :]), after=[r])
            for n in range(N_EXPERTS):
                b = bank[1 + n % 4]
                r = pe(lambda e, n=n, b=b: e.matmul(b[:, :], ident[0:16, n:n + 1].to_broadcast([16, P]), turned,
                                                    start=True, stop=True), after=[dve_now(), act_now(3) if n > 3 else act_now()],
                       own=False)
                act(lambda e, n=n, b=b: e.activation(gates[:, n, :], b[:, :], ACT.Copy), after=[r], own=False)
            return gates

        def experts(gates):
            pairs = 2 * AT_ONCE
            with prog.loop(N_EXPERTS // AT_ONCE) as group:
                gate = lambda p, group=group: gates[:, group.i * AT_ONCE + p // 2, :]
                for p in range(pairs):
                    gate_up(p % 2, (lambda p=p: finish((p - 1) % 2, lambda: 2 * (p - 1), lambda: gate(p - 1)))
                            if p else None, free=dve_now(4) if p == 0 else None)
                for n in range(pairs):
                    ready = down(n, pairs, True, (lambda: finish((pairs - 1) % 2, lambda: 2 * (pairs - 1),
                                                                 lambda: gate(pairs - 1))) if n == 0 else None)
                add_to_residual(ready, 1.0)

        rms_norm(xT, par2("mix_norm"), xn, KC)
        sync_all()
        A = Arena()
        ga = fox(A)
        sync_all()
        A = Arena()
        ga2 = A.take(SEQ)
        dve(lambda e: e.tensor_copy(ga2[32:48, :], ga[32:48, :]))
        sync_all()
        gla(ga2, A)
        sync_all()
        project_out()
        sync_all()
        A = Arena()
        cross(A)
        sync_all()
        rms_norm(xT, par2("moe_norm"), xn, KC)
        sync_all()
        gates = router()
        sync_all()
        split_slot()
        rms_norm(xT, par2("moe_norm"), xn, KC, split=True)
        sync_all()
        experts(gates)
        sync_all()
        rms_norm(xT, par2("final_norm"), xn, KC)
        done = sp(lambda e: e.dma_start(y_out, xn), after=[dve_now()])
        assert prog.slot == SECOND_SLOTS, prog.slot
        sp.wait(done)


        def stream(e, n_slots, source):
            for s in range(RING):
                e.dma_start(ring[:, s, :], source(s)).then_inc(prog.landed[s].sem, 16)
            with e.Fori(1, n_slots // RING) as i:
                for s in range(RING):
                    e.wait_ge(prog.used.sem, i * RING + (s - RING + 1))
                    e.dma_start(ring[:, s, :], source(i * RING + s)).then_inc(prog.landed[s].sem, 16)

        setup, loop = [], None
        layer_loop = next(it for it in sp.items if it[0] == "loop")
        at = sp.items.index(layer_loop)
        layer = layer_loop[1]
        layer_loop[2].insert(0, ("op", lambda e: stream(e, LAYER_SLOTS, lambda k: w1_in[layer.i * LAYER_SLOTS + k]),
                                 [], None))
        sp.items.insert(at + 1, ("op", lambda e: stream_second(e), [], None))

        rest = sp.items[at + 2:]
        del sp.items[at + 2:]

        def stream_second(e):
            for s in range(RING):
                e.dma_start(ring[:, s, :], w2_in[s]).then_inc(prog.landed[s].sem, 16)
            before_memory = 20
            with e.Fori(1, before_memory // RING) as i:
                for s in range(RING):
                    e.wait_ge(prog.used.sem, i * RING + (s - RING + 1))
                    e.dma_start(ring[:, s, :], w2_in[i * RING + s]).then_inc(prog.landed[s].sem, 16)
            sp.emit(e, rest[:1])
            with e.Fori(before_memory // RING, SECOND_SLOTS // RING) as i:
                for s in range(RING):
                    e.wait_ge(prog.used.sem, i * RING + (s - RING + 1))
                    e.dma_start(ring[:, s, :], w2_in[i * RING + s]).then_inc(prog.landed[s].sem, 16)
            sp.emit(e, rest[1:])

        block = ctx.enter_context(nc.Block())

        @block.sync
        def _(e):
            sp.emit(e)

        @block.tensor
        def _(e):
            pe.emit(e)

        @block.scalar
        def _(e):
            act.emit(e)

        @block.vector
        def _(e):
            dve.emit(e)

        @block.gpsimd
        def _(e):
            pool.emit(e)


def layout(inputs):
    import numpy as np

    f = lambda name: np.ascontiguousarray(inputs[name])

    def gate_slots(w):
        n = w.shape[1] // SLOT_COLS
        return w.reshape(KC, P, n, SLOT_COLS).transpose(2, 1, 0, 3).reshape(n, P, SLOT)

    def down_slots(w):
        n = w.shape[0] // (2 * P)
        return w.reshape(n, 2, P, D).transpose(0, 2, 1, 3).reshape(n, P, SLOT)

    def ffn_slots(gate, up, down):
        g, u, d = gate_slots(gate), gate_slots(up), down_slots(down)
        out, at = [], 0
        for pairs in FFN_PARTS:
            out += [x for n in range(at, at + pairs) for x in (g[n], u[n])] + list(d[at:at + pairs])
            at += pairs
        return out

    def chan(v):
        return v.reshape(-1, P).T

    def rep(v):
        return np.broadcast_to(v.reshape(1, -1), (P, v.size))

    def pack(columns, parts):
        out = np.zeros((P, SLOT), np.float32)
        for name, v in parts.items():
            a, w = columns[name]
            assert v.shape[1] == w, name
            out[:v.shape[0], a:a + w] = v
        return out

    heads = lambda w, order: w.reshape(*w.shape[:-1], -1, HD)[..., order, :].reshape(*w.shape[:-1], -1)
    q_order = [0, 4, 1, 5, 2, 6, 3, 7]
    by_half = [0, 2, 1, 3]
    slots1 = []
    for l in range(DEPTH):
        w = f("w_in")[l]
        att, rw, gd = w[:, :1352], w[:, 1352:1352 + 896], w[:, 2248:]
        odd = np.zeros((D, 256), np.float32)
        odd[:, 0:64] = att[:, 1280:1344]
        odd[:, 64:72] = att[:, 1344:1352]
        odd[:, 72:76] = gd[:, 1024:1028][:, by_half]
        odd[:, 76:80] = gd[:, 1028:1032][:, by_half]
        odd[:, 128:256] = rw[:, 768:896]
        lora = np.concatenate([f("rwkv_w_up")[l], f("rwkv_a_up")[l], f("rwkv_g_up")[l]], 0)
        up = np.zeros((P, 256), np.float32)
        up[:32] = f("rwkv_v_up")[0]
        conv = f("gdn_conv")[l].reshape(4, 6, P).transpose(2, 1, 0).reshape(P, 24)
        slots1.append(pack(PAR1, {
            "ffn_norm0": chan(f("ffn_norm")[l, 0]), "ffn_norm1": chan(f("ffn_norm")[l, 1]),
            "mix_norm": chan(f("mix_norm")[l]),
            "qk_norm": rep(np.concatenate([f("att_q_norm")[l]] * 8 + [f("att_k_norm")[l]] * 2)),
            "mu": chan(f("rwkv_mu")[l]), "w0": chan(f("rwkv_w0")[l]), "a0": chan(f("rwkv_a0")[l]),
            "k_k": chan(f("rwkv_k_k")[l]), "k_a": chan(f("rwkv_k_a")[l]), "r_k": chan(f("rwkv_r_k")[l].reshape(-1)),
            "gn_w": chan(f("rwkv_gn_w")[l]), "gn_b": chan(f("rwkv_gn_b")[l]), "v0": chan(f("rwkv_v0")[0]),
            "conv": conv, "a_log": rep(f("gdn_a_log")[l][by_half]), "dt_bias": rep(f("gdn_dt_bias")[l][by_half]),
            "o_norm": chan(np.tile(f("gdn_o_norm")[l], 4)), "lora_up": lora,
            "v_down": f("rwkv_v_down")[0].reshape(2, P, 32).transpose(1, 0, 2).reshape(P, 64), "v_up": up}))
        slots1 += ffn_slots(f("ffn_w_gate")[l, 0], f("ffn_w_up")[l, 0], f("ffn_w_down")[l, 0])
        slots1 += list(gate_slots(heads(att[:, :512], q_order)))
        slots1 += list(gate_slots(att[:, 512:768]))
        slots1 += list(gate_slots(att[:, 768:1280]))
        slots1 += list(gate_slots(odd))
        slots1 += list(gate_slots(rw[:, :768]))
        slots1 += list(gate_slots(gd[:, :1024]))
        slots1 += list(down_slots(f("w_out")[l]))
        slots1 += ffn_slots(f("ffn_w_gate")[l, 1], f("ffn_w_up")[l, 1], f("ffn_w_down")[l, 1])
    w = f("w_in_2")[0]
    o = [int(a) for a in np.cumsum([512, 512, 512, 8, 256, 256, 512, 512, 16])]
    odd = np.zeros((D, 256), np.float32)
    odd[:, 0:8], odd[:, 32:48] = w[:, o[2]:o[3]], w[:, o[7]:o[8]]
    rt = np.zeros((D, 256), np.float32)
    rt[:, 0:4], rt[:, 4:20] = f("w_router_group_2")[0], f("w_router_expert_2")[0]
    forget = np.zeros((P, 1), np.float32)
    forget[:8, 0] = f("b_forget_2")[0]
    alpha = np.zeros((P, 256), np.float32)
    alpha[32:48] = f("w_alpha_up_2")[0]
    slots2 = [pack(PAR2, {
        "mem_norm": chan(f("mem_norm_2")), "mix_norm": chan(f("mix_norm_2")[0]),
        "cross_norm": chan(f("cross_norm_2")[0]), "moe_norm": chan(f("moe_norm_2")[0]),
        "final_norm": chan(f("final_norm_2")), "b_forget": forget, "b_alpha": chan(f("b_alpha_2")[0]),
        "fox_gain": chan(f("fox_out_gain_2")[0]), "gla_gain": chan(f("gla_out_gain_2")[0]),
        "b_router": rep(np.concatenate([f("b_router_group_2")[0], f("b_router_expert_2")[0]])), "alpha_up": alpha})]
    slots2 += list(gate_slots(w[:, :o[2]])) + list(gate_slots(odd))
    slots2 += list(gate_slots(w[:, o[3]:o[7]]))
    slots2 += list(down_slots(f("w_out_2")[0]))
    for name in ("w_xq_2", "w_xk_2", "w_xv_2"):
        slots2 += list(gate_slots(f(name)[0]))
    slots2 += list(down_slots(f("w_xo_2")[0])) + list(gate_slots(rt))
    for g in range(N_EXPERTS // AT_ONCE):
        own = range(AT_ONCE * g, AT_ONCE * (g + 1))
        for n in own:
            pairs = zip(gate_slots(f("w_expert_gate_2")[0, n]), gate_slots(f("w_expert_up_2")[0, n]))
            slots2 += [x for pair in pairs for x in pair]
        for n in own:
            slots2 += list(down_slots(f("w_expert_down_2")[0, n]))
    slots2.append(np.zeros((P, SLOT), np.float32))

    r, s = np.arange(P)[:, None], np.arange(P)[None, :]
    lev = [((r >> (n + 1)) == (s >> (n + 1))) & ((r >> n) % 2 == 1) & ((s >> n) % 2 == 0) for n in range(7)]
    half = HD // 2
    inv = np.float32(10000.0) ** (-np.arange(half, dtype=np.float32) / np.float32(half))
    ang = np.arange(SEQ, dtype=np.float32)[:, None] * inv[None, :]
    cos, sin = np.cos(ang), np.sin(ang)
    rope = np.concatenate([cos, cos, -sin, sin], 1).reshape(NT, P, 2 * P // 2).transpose(1, 0, 2).reshape(P, -1)
    cmask = np.concatenate([np.zeros((P, 3 * P)), np.where(s > r, NEG, 0.0)], 1)
    const = np.concatenate([np.eye(P), np.ones((P, P)), (r // HD) == (s // HD), rope, cmask, r <= s, r >= s, r > s,
                            r < s] + lev + [m.T for m in lev] + [np.broadcast_to([[4., 3., 2., 1.]], (P, 4))],
                           1).astype(np.float32)
    turn = lambda a: np.ascontiguousarray(a.reshape(a.shape[0], KC, P).transpose(2, 1, 0))
    return {"x_t": turn(f("x")[0]), "mem_t": turn(f("mem_2")[0]), "consts": np.ascontiguousarray(const),
            "slots_1": np.stack(slots1), "slots_2": np.stack(slots2)}


def kernel(**inputs):
    import numpy as np
    import concourse.bacc as bacc
    from concourse.bass_utils import run_bass_kernel_spmd

    arrays = layout(inputs)
    nc = bacc.Bacc("TRN2", target_bir_lowering=False, num_devices=1)
    ins = [nc.dram_tensor(n, a.shape, F32, kind="ExternalInput").ap() for n, a in arrays.items()]
    out = nc.dram_tensor("y_t", (P, KC, SEQ), F32, kind="ExternalOutput").ap()
    build(nc, *ins, out)
    r = run_bass_kernel_spmd(nc, [arrays], core_ids=[0])
    y = np.asarray(r.results[0]["y_t"])
    return np.ascontiguousarray(y.transpose(2, 1, 0).reshape(1, SEQ, D))
```

```python
from contextlib import ExitStack, contextmanager

import concourse.bass as bass
from concourse import mybir

F32 = mybir.dt.float32
F32R = mybir.dt.float32r
U32 = mybir.dt.uint32
ALU = mybir.AluOpType
ACT = mybir.ActivationFunctionType
AX = mybir.AxisListType.X

P = 128
DEPTH, D, SEQ, D_FF = 2, 1024, 512, 2816
KC = D // P
NT = SEQ // P
SLOT = 2048
SLOT_COLS = SLOT // KC
RING = 2
PAIRS = D_FF // (2 * P)
FFN_PARTS = (6, 5)
FFN_SLOTS = 3 * PAIRS
IN_SLOTS = 13
LAYER_SLOTS = 1 + 2 * FFN_SLOTS + IN_SLOTS + 4
E_SLOTS = 6
N_EXPERTS, GROUPS, PER_GROUP = 16, 4, 4
AT_ONCE = 2
SECOND_SLOTS = 1 + 13 + 4 + 6 + 2 + 1 + N_EXPERTS * E_SLOTS + 1
MEM = 256
HD = 64
TOPK = 128
ARENA = 28000
CROSS_AT = ARENA - 2 * 4 * MEM
DSA_ARENA = 10 * SEQ + 10 * 512
STEPS = 1
NEG = -1e30
EPS = 1e-6

CONST = {}
_at = 0
for _n, _w in [("ident", P), ("ones", P), ("bones", P), ("rope", NT * 2 * HD), ("cmask", 4 * P), ("upper", P),
               ("lower", P), ("slower", P), ("supper", P), ("lev", 7 * P), ("levT", 7 * P), ("rank4", 4)]:
    CONST[_n] = (_at, _w)
    _at += _w
NCONST = _at

def _columns(widths):
    out, at = {}, 0
    for name, w in widths:
        out[name] = (at, w)
        at += w
    return out, at


PAR1, NPAR1 = _columns([
    ("ffn_norm0", KC), ("ffn_norm1", KC), ("mix_norm", KC), ("qk_norm", 10 * HD), ("mu", 7), ("w0", 2), ("a0", 2),
    ("k_k", 2), ("k_a", 2), ("r_k", 2), ("gn_w", 2), ("gn_b", 2), ("v0", 2), ("conv", 24), ("a_log", 4),
    ("dt_bias", 4), ("o_norm", 2), ("lora_up", 256), ("v_down", 64), ("v_up", 256)])
PAR2, NPAR2 = _columns([
    ("mem_norm", KC), ("mix_norm", KC), ("cross_norm", KC), ("moe_norm", KC), ("final_norm", KC), ("b_forget", 1),
    ("b_alpha", 2), ("fox_gain", 4), ("gla_gain", 4), ("b_router", 20), ("alpha_up", 256)])
NPAR = max(NPAR1, NPAR2)


class Counter:

    def __init__(self, sem, step=1):
        self.sem, self.step, self.path, self.off = sem, step, (), 0

    def bump(self):
        self.off += self.step
        return self.now()

    def now(self, back=0):
        return (self, self.path, self.off - back)


class Loop:

    def __init__(self, n):
        self.n, self.delta, self.i = n, {}, None

    def value(self, k):
        return self.i * k


class Line:

    def __init__(self, prog, name, counter):
        self.prog, self.name, self.counter, self.items, self.seen = prog, name, counter, [], {}
        self.tokens, self.owed = {}, {}

    def now(self, back=0):
        if self.prog.strand is None:
            return self.counter.now(back)
        own = self.tokens.get(self.prog.strand, [])
        return own[-1 - back] if len(own) > back else None

    def __call__(self, fn, after=(), signal=None, own=True):
        strand = self.prog.strand
        waits = list(after) + self.owed.pop(strand, []) + ([self.now()] if own else [])
        self.items.append(("op", fn, self._new(waits), None if signal is False else (signal or self.counter)))
        if signal is False:
            return None
        token = (signal or self.counter).bump()
        if strand is not None:
            self.tokens.setdefault(strand, []).append(token)
        return token

    def wait(self, *after):
        if self.prog.strand is None:
            self.items.append(("op", None, self._new(after), None))
        else:
            self.owed.setdefault(self.prog.strand, []).extend(after)

    def _new(self, waits):
        best = {}
        for c, path, off in (w for w in waits if w is not None):
            if off <= 0 and not path:
                continue
            if c not in best or (path == c.path and off > best[c][1]) or best[c][0] != path:
                best[c] = (path, off)
        out = []
        for c, (path, off) in best.items():
            if self.seen.get(c, (None, 0))[0] == path and self.seen[c][1] >= off:
                continue
            self.seen[c] = (path, off)
            out.append((c, path, off))
        return out

    def emit(self, eng, items=None):
        for item in self.items if items is None else items:
            if item[0] == "loop":
                _, loop, body, start = item
                with eng.Fori(0, loop.n) as i:
                    loop.i = i
                    self.emit(eng, body)
                loop.i = None
                continue
            _, fn, waits, signal = item
            for counter, path, off in waits:
                value = off
                for loop, base in path:
                    turn = loop.delta.get(counter, 0)
                    value = value + base + (loop.i * turn if loop.i is not None else (loop.n - 1) * turn)
                eng.wait_ge(counter.sem, value)
            if fn is not None:
                made = fn(eng)
                if signal is not None:
                    made.then_inc(signal.sem, signal.step)


class Program:

    def __init__(self, nc, ctx):
        self.nc = nc
        self.sem = lambda name: ctx.enter_context(nc.semaphore(name))
        self.counters = []
        self.used = self.counter("slots_used")
        self.landed = [self.counter(f"slot{n}_landed", 16) for n in range(RING)]
        self.pe, self.act, self.dve, self.pool = (Line(self, n, self.counter(f"{n}_done"))
                                                  for n in ("pe", "act", "dve", "pool"))
        self.sp = Line(self, "sp", self.counter("misc_dma", 16))
        self.lines = [self.pe, self.act, self.dve, self.pool, self.sp]
        self.arrived, self.met, self.cleared = self.sem("arrived"), self.sem("met"), self.sem("cleared")
        self.slot = 0
        self.layer = None
        self.strand = None

    def weave(self, strands):
        for line in self.lines:
            line.tokens, line.owed = {}, {}
        live = dict(strands)
        while live:
            for name in list(live):
                steps, work = live[name]
                self.strand = name
                for _ in range(steps):
                    if next(work, self) is self:
                        del live[name]
                        break
        self.strand = None

    def counter(self, name, step=1):
        c = Counter(self.sem(name), step)
        self.counters.append(c)
        return c

    @contextmanager
    def loop(self, n):
        loop = Loop(n)
        saved = [(line, line.items) for line in self.lines]
        at = [(c, c.path, c.off) for c in self.counters]
        for c, path, off in at:
            c.path, c.off = (*path, (loop, off)), 0
        for line in self.lines:
            line.items, line.seen = [], {}
        first = self.slot
        yield loop
        assert (self.slot - first) % RING == 0
        self.slot = first + n * (self.slot - first)
        for c, path, off in at:
            loop.delta[c] = c.off
            c.path, c.off = path, off + n * c.off
        for line, items in saved:
            if line.items:
                items.append(("loop", loop, line.items, None))
            line.items, line.seen = items, {}

    @contextmanager
    def layers(self, n):
        self.layer = Loop(n)
        saved = [(line, line.items) for line in self.lines]
        for line in self.lines:
            line.items = []
        yield self.layer
        for line, items in saved:
            items.append(("loop", self.layer, line.items, None))
            line.items = items
        self.layer = None

    def epoch(self, before):
        layer = self.layer
        done = [c.now() for c in self.counters]

        def count(k):
            return k * (before + 1) + (layer.i * k if layer is not None else 0)

        for line in self.lines:
            line.wait(*done)
            if line is not self.sp:
                line.items.append(("op", lambda e: e.sem_inc(self.arrived, 1), [], None))
                line.items.append(("op", lambda e: e.wait_ge(self.cleared, count(1)), [], None))
        self.sp.items.append(("op", lambda e: e.wait_ge(self.arrived, count(4)), [], None))
        self.sp.items.append(("op", lambda e: e.sem_inc(self.met, 1), [], None))
        for c in self.counters:
            self.sp.items.append(("op", lambda e, c=c: e.sem_clear(c.sem), [], None))
        self.sp.items.append(("op", lambda e: e.sem_inc(self.cleared, 1), [], None))
        for c in self.counters:
            c.off = 0
        for line in self.lines:
            line.seen = {}
        self.slot = 0

    def take(self):
        s = self.slot % RING
        self.slot += 1
        return s, self.landed[s].bump()


def build(nc, x_in, mem_in, const_in, w1_in, w2_in, y_out):
    with ExitStack() as ctx:
        def sb(name, n):
            return ctx.enter_context(nc.sbuf_tensor(name, [P, n], F32))

        prog = Program(nc, ctx)
        pe, act, dve, pool, sp = prog.pe, prog.act, prog.dve, prog.pool, prog.sp
        pe_now, act_now, dve_now, pool_now = pe.now, act.now, dve.now, pool.now

        def used_now():
            return prog.used.now() if prog.strand is None else pe.now()

        bank = [ctx.enter_context(nc.psum_tensor(f"bank{n}", [P, 512], F32)) for n in range(8)]
        xT = sb("xT", KC * SEQ)[:, :].rearrange("p (c t) -> p c t", c=KC)
        xn_at = -(-nc.sbuf_base // 32) * 32
        xn = sb("xn", KC * SEQ)[:, :].rearrange("p (c t) -> p c t", c=KC)
        ring = sb("ring", RING * SLOT)[:, :].rearrange("p (s n) -> p s n", s=RING)
        const = sb("const", NCONST)
        par = sb("par", NPAR)
        mixed_at = -(-nc.sbuf_base // 32) * 32
        mixed = sb("mixed", KC * SEQ)[:, :].rearrange("p (c t) -> p c t", c=KC)
        tmp = [sb(f"tmp{n}", 512) for n in range(4)]
        v_first = sb("v_first", 2 * SEQ)
        is_first = sb("is_first", 1)
        eps = sb("eps", 4)
        col = sb("col", 320)
        col2 = sb("col2", 128)
        arena_at = -(-nc.sbuf_base // 32) * 32
        arena = sb("arena", ARENA)

        def over(name, offset, n):
            return nc.alloc_sbuf_tensor_at(name, [P, n], F32R, offset=offset)

        x_hi, x_lo = (over(n, at, KC * SEQ)[:, :].rearrange("p (c t) -> p c t", c=KC)
                      for n, at in (("x_hi", xn_at), ("x_lo", mixed_at)))
        HT = 2 * max(FFN_PARTS)
        h_hi, h_lo = (over(n, arena_at + 4 * (4 * SLOT + m * HT * SEQ), HT * SEQ)[:, :].rearrange("p (f t) -> p f t", t=SEQ)
                      for m, n in enumerate(("h_hi", "h_lo")))
        w_hi, w_lo = (over(n, arena_at + 4 * m * 2 * SLOT, 2 * SLOT)[:, :].rearrange(
            "p (s n) -> p s n", s=2) for m, n in enumerate(("w_hi", "w_lo")))
        GATES_AT = 4 * SLOT + (HT + 4 * AT_ONCE) * SEQ
        assert GATES_AT + N_EXPERTS * SEQ <= ARENA

        def C(name, n=None):
            a, w = CONST[name]
            return const[:, a:a + w] if n is None else const[:, a + n * P:a + (n + 1) * P]

        def par1(name):
            a, w = PAR1[name]
            return par[:, a:a + w]

        def par2(name):
            a, w = PAR2[name]
            return par[:, a:a + w]

        class Arena:

            def __init__(self, at=0):
                self.at = at

            def take(self, n):
                a = self.at
                self.at += n
                assert self.at <= ARENA, self.at
                return arena[:, a:a + n]

        ident, ones, bones = C("ident"), C("ones"), C("bones")

        def wide(ap, shape):
            return ap.unsqueeze(len(ap.shape)).to_broadcast(shape)

        def sweep(ap, n):
            return ap.unsqueeze(1).to_broadcast([P, n, ap.shape[-1]])


        def everything():
            return [used_now(), pe_now(), act_now(), dve_now(), pool_now()]

        def reciprocal_root(out, in_, scale, eps_col, after):
            t = act(lambda e: e.activation(out, in_, ACT.Sqrt, bias=eps[:out.shape[0], eps_col:eps_col + 1],
                                           scale=scale), after=after)
            return dve(lambda e: e.reciprocal(out, out), after=[t])

        def rms_norm(src, gains, out, width, n=SEQ, ready=None, split=False):
            ready = ready or [dve_now()] * width
            mm = [None] * 4
            for c in range(width):
                square = act(lambda e, c=c: e.activation(tmp[c % 4][:, :n], src[:, c, :], ACT.Square),
                             after=[ready[c]] + ([mm[c % 4]] if mm[c % 4] else [pe_now(), ready[0]]), own=False)
                mm[c % 4] = pe(lambda e, c=c: e.matmul(bank[0][:, :n], ones, tmp[c % 4][:, :n], start=c == 0,
                                                       stop=c == width - 1),
                               after=[square] + ([ready[0], act_now(1)] if c == 0 else []), own=False)
            rstd = tmp[3][:, :n]
            reciprocal_root(rstd, bank[0][:, :n], 1.0 / (width * P), 0, [pe_now()])
            if split:
                there = []
                for c in range(width):
                    full = tmp[c % 3][:, :n]
                    t = dve(lambda e, c=c, full=full: e.scalar_tensor_tensor(
                        out=full, in0=src[:, c, :], scalar=gains[:, c:c + 1], in1=rstd, op0=ALU.mult,
                        op1=ALU.mult), own=c == 0, after=[pe_now(), used_now(), act_now(2)])
                    hi = act(lambda e, c=c, full=full: e.activation(x_hi[:, c, :], full, ACT.Copy), after=[t],
                             own=False)
                    there.append(dve(lambda e, c=c, full=full: e.tensor_tensor(
                        x_lo[:, c, :], full, x_hi[:, c, :].bitcast(F32), ALU.subtract), after=[hi], own=False))
                return there
            return [dve(lambda e, c=c: e.scalar_tensor_tensor(
                out=out[:, c, :], in0=src[:, c, :], scalar=gains[:, c:c + 1], in1=rstd, op0=ALU.mult,
                op1=ALU.mult), own=c == 0, after=[pe_now(), used_now()]) for c in range(width)]

        def columns(slot):
            return ring[:, slot, :].rearrange("p (k n) -> p k n", k=KC)

        def rows(slot):
            return ring[:, slot, :].rearrange("p (f n) -> p f n", f=2)

        def by_channel(slot, c0, out, src, last, after=(), m=P, n=SEQ):
            w = columns(slot)
            for k in range(KC):
                t = pe(lambda e, k=k: e.matmul(out, w[:, k, c0:c0 + m], src[:, k, :n], start=k == 0,
                                               stop=k == KC - 1),
                       after=after if k == 0 else (), own=False,
                       signal=(prog.used if last else pe.counter) if k == KC - 1 else False)
            return t

        def by_token(slot, c0, n, out, src, tile, last, after=(), chunks=None):
            w = columns(slot)
            for k in range(KC):
                t = pe(lambda e, k=k: e.matmul(out, src[:, k, tile * P:(tile + 1) * P], w[:, k, c0:c0 + n],
                                               start=k == 0, stop=k == KC - 1),
                       after=[*(after if k == 0 else ()), *([chunks[k]] if chunks else ())], own=False,
                       signal=(prog.used if last else pe.counter) if k == KC - 1 else False)
            return t


        def split_slot():
            s, there = prog.take()
            hi = act(lambda e: e.activation(w_hi[:, s, :], ring[:, s, :], ACT.Copy), after=[there, pe_now()],
                     own=False)
            dve(lambda e: e.tensor_tensor(w_lo[:, s, :], ring[:, s, :], w_hi[:, s, :].bitcast(F32), ALU.subtract),
                after=[hi, used_now(), pe_now()], own=False, signal=prog.used)

        def passes(s):
            return ((w_hi[:, s, :], 0), (w_hi[:, s, :], 1), (w_lo[:, s, :], 0))

        def split_products(out, s, pick, data, ks, start, stop, after=(), signal=None, chunks=None):
            for k in ks:
                for n, (w, part) in enumerate(passes(s)):
                    end = k == ks[-1] and n == 2
                    t = pe(lambda e, k=k, w=w, part=part, n=n, end=end: e.matmul(
                        out, pick(w, k), data(part, k), start=start and k == ks[0] and n == 0, stop=stop and end),
                        after=[*(after if k == ks[0] else ()), *([chunks[k]] if chunks else ())] if n == 0 else (),
                        own=False, signal=signal if end else False)
            return t

        def gate_up(j, finish_before=None, free=None, chunks=None):
            column = lambda w, k, f: w.rearrange("p (k n) -> p k n", k=KC)[:, k, f * P:(f + 1) * P]
            xs = lambda part, k: (x_hi, x_lo)[part][:, k, :]
            for n in range(2):
                ready = [used_now()] + ([free or dve_now()] if n == 0 else [])
                s = (prog.slot - 1) % RING
                split_slot()
                if n == 0 and finish_before is not None:
                    finish_before()
                for f in range(2):
                    split_products(bank[4 * j + 2 * n + f][:, :], s, lambda w, k, f=f: column(w, k, f), xs,
                                   range(KC), True, True, after=ready, chunks=chunks)

        def finish(j, index, gate=None):
            for f in range(2):
                full, g, u = tmp[2 * j + f][:, :], bank[4 * j + f], bank[4 * j + 2 + f]
                silu = act(lambda e, g=g, full=full: e.activation(full, g[:, :], ACT.Silu),
                           after=[pe_now(), dve_now()], own=False)
                dve(lambda e, u=u, full=full: e.tensor_tensor(full, full, u[:, :], ALU.mult),
                    after=[silu, pe_now()], own=False)
                if gate is not None:
                    dve(lambda e, full=full: e.tensor_tensor(full, full, gate(), ALU.mult))
                dve(lambda e, f=f, full=full: e.tensor_scalar(h_hi[:, index() + f, :], full, 1.0, None, ALU.mult))
                dve(lambda e, f=f, full=full: e.tensor_tensor(
                    h_lo[:, index() + f, :], full, h_hi[:, index() + f, :].bitcast(F32), ALU.subtract))

        def down(n, n_slots, ahead, post=None, busy=0, chunks=None):
            free = used_now()
            s = (prog.slot - 1) % RING
            order = range(KC)
            if post is not None:
                order = [(d + 4 * (1 - busy)) % KC for d in range(KC)]
                before = dve_now()
                post()
            after = dve_now()
            if ahead:
                split_slot()
            rows_ = lambda w, k, d: w.rearrange("p (f n) -> p f n", f=2)[:, k, d * P:(d + 1) * P]
            out = [None] * KC
            for i, d in enumerate(order):
                ready = [free] + ([before if i < 4 else after] if post is not None else [])
                last = n == n_slots - 1
                out[d] = split_products(
                    bank[d][:, :], s, lambda w, k, d=d: rows_(w, k, d),
                    lambda part, k: (h_hi, h_lo)[part][:, 2 * n + k, :], range(2), n == 0, last, after=ready,
                    chunks=chunks, signal=None if last or i == KC - 1 else False)
            return out

        def add_to_residual(ready, scale):
            for d in range(KC):
                dve(lambda e, d=d: e.scalar_tensor_tensor(out=xT[:, d, :], in0=bank[d][:, :], scalar=scale,
                                                          in1=xT[:, d, :], op0=ALU.mult, op1=ALU.add),
                    after=[ready[d]], own=d == 0)

        def ffn(norm, added=None):
            if added is None:
                split_slot()
            chunks = rms_norm(xT, norm, xn, KC, ready=added, split=True)
            for part, pairs in enumerate(FFN_PARTS):
                gate_up(0, free=dve_now(4) if part else chunks[0], chunks=None if part else chunks)
                turns, odd = divmod(pairs - 1, 2)
                with prog.loop(turns) as turn:
                    gate_up(1, lambda turn=turn: finish(0, lambda: turn.i * 4))
                    gate_up(0, lambda turn=turn: finish(1, lambda: turn.i * 4 + 2))
                if odd:
                    gate_up(1, lambda turns=turns: finish(0, lambda: 4 * turns))
                for n in range(pairs):
                    ready = down(n, pairs, part + 1 < len(FFN_PARTS) or n + 1 < pairs,
                                 (lambda turns=turns, odd=odd: finish(odd, lambda: 4 * turns + 2 * odd)) if n == 0 else None,
                                 busy=odd)
                add_to_residual(ready, 0.5)

        def project_out(n_slots=4, ahead=False):
            sync_all()
            split_slot()
            chunks = []
            for c in range(2 * n_slots):
                hi = act(lambda e, c=c: e.activation(h_hi[:, c, :], mixed[:, c, :], ACT.Copy), own=False)
                chunks.append(dve(lambda e, c=c: e.tensor_tensor(
                    h_lo[:, c, :], mixed[:, c, :], h_hi[:, c, :].bitcast(F32), ALU.subtract), after=[hi], own=False))
            for n in range(n_slots):
                ready = down(n, n_slots, ahead or n + 1 < n_slots, chunks=chunks[2 * n:2 * n + 2])
            add_to_residual(ready, 1.0)
            return [dve_now(KC - 1 - d) for d in range(KC)]

        def load_parameters(n):
            slot, there = prog.take()
            copied = pool(lambda e: e.tensor_copy(par[:, :n], ring[:, slot, :n]), after=[there], own=False,
                          signal=prog.used)
            for line in (pe, act, dve):
                line.wait(copied)

        def sync_all():
            done = everything()
            for line in (pe, act, dve, pool):
                line.wait(*done)

        def transpose(out, in_, after=(), signal=None):
            n = in_.shape[0]
            return pe(lambda e: e.transpose(out, in_, ident[:n, :n]), after=after, own=False, signal=signal)

        def unit_inverse(Lt, T, Tt, after):
            pe.wait(*after)
            for lv in range(1, 7):
                last = lv == 6
                stages = []
                for q in range(NT):
                    yield
                    t = [pe(lambda e, q=q, h=h: e.matmul(bank[q][:, h * P:(h + 1) * P], Lt[:, q, h, :],
                                                         T[:, q, h, :], start=True, stop=True),
                            after=[dve_now()] if q == 0 and h == 0 else (), own=False,
                            signal=None if h == 3 else False) for h in range(4)][3]
                    stages.append(dve(lambda e, q=q, lv=lv: e.tensor_tensor(
                        tmp[q][:, :].rearrange("p (h s) -> p h s", h=4),
                        bank[q][:, :].rearrange("p (h s) -> p h s", h=4), sweep(C("lev", lv), 4), ALU.mult),
                        after=[t], own=False))
                for q in range(NT):
                    yield
                    b0, b1 = bank[q], bank[4]
                    if not last:
                        t0 = [pe(lambda e, q=q, h=h, b0=b0: e.matmul(b0[:, h * P:(h + 1) * P], Tt[:, q, h, :],
                                                              tmp[q][:, h * P:(h + 1) * P], start=True, stop=True),
                                 after=[stages[q]], own=False, signal=None if h == 3 else False)
                              for h in range(4)][3]
                    t1 = [pe(lambda e, q=q, h=h, b1=b1: e.matmul(b1[:, h * P:(h + 1) * P], tmp[q][:, h * P:(h + 1) * P],
                                                          Tt[:, q, h, :], start=True, stop=True),
                             after=[stages[q], dve_now()], own=False, signal=None if h == 3 else False)
                          for h in range(4)][3]
                    if not last:
                        dve(lambda e, q=q, b0=b0: e.tensor_tensor(T[:, q], T[:, q], b0[:, :].rearrange(
                            "p (h s) -> p h s", h=4), ALU.add), after=[t0], own=False)
                    dve(lambda e, q=q, b1=b1: e.tensor_tensor(Tt[:, q], Tt[:, q], b1[:, :].rearrange(
                        "p (h s) -> p h s", h=4), ALU.add), after=[t1], own=False)

        def attention(rows_of, scale, A, banks=(5, 6, 7), stat_at=0):
            SCORES, TURNED, OUT = (bank[n] for n in banks)
            p_rows, turned = ([A.take(512) for _ in range(2)] for _ in range(2))
            stat = col2[:, stat_at:stat_at + 8].rearrange("p (b n) -> p b n", b=2)
            n = len(rows_of)
            tok = {}
            for i in range(n + 2):
                if 1 <= i <= n:
                    w, p_row, (mx, nm, sm, iv) = rows_of[i - 1][0], p_rows[(i - 1) % 2], [
                        stat[:, (i - 1) % 2, m:m + 1] for m in range(4)]
                    dve(lambda e, sm=sm, iv=iv: e.reciprocal(iv, sm), after=[tok["exp", i - 1]])
                    tok["p", i - 1] = dve(lambda e, p_row=p_row, w=w, iv=iv: e.tensor_scalar(
                        p_row[:, :w], p_row[:, :w], iv, None, ALU.mult))
                if i < n:
                    w, scores, mask = rows_of[i][:3]
                    p_row, (mx, nm, sm, iv) = p_rows[i % 2], [stat[:, i % 2, m:m + 1] for m in range(4)]
                    made = scores(SCORES[:, :w])
                    for k, product in enumerate(made):
                        t = pe(product, after=[tok.get(("read", i - 1))] if k == 0 else (), own=False,
                               signal=None if k == len(made) - 1 else False)
                    free = tok.get(("turn", i - 2))
                    if mask is None:
                        dve(lambda e, mx=mx, w=w: e.tensor_reduce(mx, SCORES[:, :w], AX, ALU.max), after=[t],
                            own=False)
                    else:
                        tok["read", i] = dve(lambda e, mx=mx, w=w, p_row=p_row, mask=mask: e.tensor_tensor_reduce(
                            out=p_row[:, :w], in0=SCORES[:, :w], in1=mask, scale=1.0, scalar=-3e38, op0=ALU.add,
                            op1=ALU.max, accum_out=mx), after=[t, free], own=True)
                    t = dve(lambda e, mx=mx, nm=nm: e.tensor_scalar(nm, mx, -scale, None, ALU.mult))
                    src = SCORES if mask is None else p_row
                    tok["exp", i] = act(lambda e, src=src, p_row=p_row, nm=nm, sm=sm, w=w: e.activation(
                        p_row[:, :w], src[:, :w], ACT.Exp, bias=nm, scale=scale, accum_out=sm), after=[t, free],
                        own=False)
                    if mask is None:
                        tok["read", i] = tok["exp", i]
                yield
                if 1 <= i <= n:
                    w, p_row, dst = rows_of[i - 1][0], p_rows[(i - 1) % 2], turned[(i - 1) % 2]
                    for k in range(w // P):
                        t = transpose(TURNED[:, k * P:(k + 1) * P], p_row[:, k * P:(k + 1) * P],
                                      after=[tok["p", i - 1], tok.get(("turned", i - 2))] if k == 0 else (),
                                      signal=None if k == w // P - 1 else False)
                    tok["turn", i - 1] = t
                    tok["turned", i - 1] = act(lambda e, dst=dst, w=w: e.activation(dst[:, :w], TURNED[:, :w], ACT.Copy),
                                               after=[t, tok.get(("values", i - 3))], own=False)
                yield
                if i >= 2:
                    w, values, part, dst = rows_of[i - 2][0], *rows_of[i - 2][3:]
                    src = turned[i % 2]
                    for k in range(w // P):
                        t = pe(lambda e, k=k, values=values, part=part, src=src, w=w: e.matmul(
                            OUT[part, 0:P], values(k), src[:, k * P:(k + 1) * P], start=k == 0,
                            stop=k == w // P - 1), after=[tok["turned", i - 2], tok.get(("out", i - 3))],
                            own=False, signal=None if k == w // P - 1 else False)
                    tok["values", i - 2] = t
                    tok["out", i - 2] = act(lambda e, part=part, dst=dst: e.activation(dst, OUT[part, 0:P], ACT.Copy),
                                            after=[t], own=False)
                yield


        there = [sp(lambda e: e.dma_start(const[:, :], const_in), own=False),
                 sp(lambda e: e.dma_start(xT, x_in), own=False)][-1]
        for n, v in enumerate((1e-6, 1e-12, 64e-5, 0.0)):
            dve(lambda e, n=n, v=v: e.memset(eps[:, n:n + 1], v), own=False)
        dve(lambda e: e.memset(is_first[:, :], 1.0), own=False)
        dve(lambda e: e.memset(v_first[:, :], 0.0), own=False)
        for line in (pe, act, dve, pool):
            line.wait(there)
        prog.epoch(0)


        def attention_projections(tok, A, chunks):
            v = A.take(NT * P).rearrange("p (t n) -> p t n", t=NT)
            for n, (width, dst) in enumerate([(256, 0), (256, 256), (256, 512), (256, 640), (256, 896)]):
                slot, there = prog.take()
                for t in range(NT):
                    b = bank[4 * (n % 2) + t]
                    r = by_token(slot, 0, width, b[:, :width], xn, t, t == NT - 1,
                                 after=[there, act_now(NT) if n in (2, 3) else act_now()] + [chunks[0]],
                                 chunks=None if n else chunks)
                    if n == 2:
                        act(lambda e, b=b, t=t: e.activation(tok[:, t, 512:640], b[:, 0:128], ACT.Copy),
                            after=[r], own=False)
                        act(lambda e, b=b, t=t: e.activation(v[:, t, :], b[:, 128:256], ACT.Copy), after=[r],
                            own=False)
                    else:
                        act(lambda e, b=b, t=t, dst=dst: e.activation(tok[:, t, dst:dst + 256], b[:, 0:256],
                                                                      ACT.Copy), after=[r], own=False)
            return v

        def shifted(raw, mu, out, ready):
            dve(lambda e: e.tensor_tensor(out, raw[:, 0:SEQ], raw[:, 1:SEQ + 1], ALU.subtract), after=ready)
            return dve(lambda e: e.scalar_tensor_tensor(out=out, in0=out, scalar=mu, in1=raw[:, 1:SEQ + 1],
                                                        op0=ALU.mult, op1=ALU.add))

        def mixed_slot(keys, small, lora, raw):
            slot, there = prog.take()
            free = [dve_now(), act_now()]
            for t in range(NT):
                r = by_token(slot, 0, 80, bank[t][:, 0:80], xn, t, False, after=[there] + free)
                act(lambda e, t=t: e.activation(keys[:, t, 0:64], bank[t][:, 0:64], ACT.Copy), after=[r], own=False)
                act(lambda e, t=t: e.activation(small[:, t, :], bank[t][:, 64:80], ACT.Copy), after=[r], own=False)
            r = by_channel(slot, P, bank[4][:, :], xn, True)
            act(lambda e: e.activation(raw[:, 1:SEQ + 1], bank[4][:, :], ACT.Copy), after=[r], own=False)
            dve(lambda e: e.memset(raw[:, 0:1], 0.0))
            shifted(raw, par1("mu")[:, 6:7], lora, [act_now()])
            act(lambda e: e.activation(lora[0:32, :], lora[0:32, :], ACT.Tanh), after=[dve_now()])
            act(lambda e: e.activation(lora[64:128, :], lora[64:128, :], ACT.Sigmoid), after=[dve_now()])

        def dsa(tok, keys, small, v, work, other, A, events):
            heads = tok.rearrange("p t (h d) -> p t h d", d=HD)
            turned = A.take(10 * SEQ).rearrange("p (b t) -> p b t", b=10)
            stat = col2[:, 16:56].rearrange("p (t h) -> p t h", t=NT)
            rope = C("rope").rearrange("p (t n) -> p t n", t=NT)
            w3 = work.rearrange("p (h d) -> p h d", d=HD)
            o3 = other.rearrange("p (h d) -> p h d", d=HD)
            for t in range(NT):
                for n in range(2):
                    act(lambda e, t=t, n=n: e.activation(tok[:, t, (18 + n) * HD:(19 + n) * HD], keys[:, t, 0:64],
                                                         ACT.Copy), after=[act_now(), dve_now()])
                act(lambda e, t=t: e.activation(work[:, 0:640], tok[:, t, 0:640], ACT.Square), after=[dve_now()])
                dve(lambda e, t=t: e.tensor_reduce(stat[:, t, :], w3[:, 0:10, :], AX, ALU.add), after=[act_now()])
                reciprocal_root(stat[:, t, :], stat[:, t, :], 1.0 / HD, 0, [dve_now()])
                dve(lambda e, t=t: e.tensor_tensor(heads[:, t, 0:10, :], heads[:, t, 0:10, :],
                                                   wide(stat[:, t, :], [P, 10, HD]), ALU.mult))
                dve(lambda e, t=t: e.tensor_tensor(tok[:, t, 0:640], tok[:, t, 0:640], par1("qk_norm"), ALU.mult))
                cos, sin = rope[:, t, 0:HD], rope[:, t, HD:2 * HD]
                pool(lambda e, t=t, sin=sin: e.tensor_tensor(w3[:, :, 0:32], heads[:, t, :, 32:64],
                                                             sweep(sin[:, 0:32], 20), ALU.mult),
                     after=[dve_now(), act_now()])
                pool(lambda e, t=t, sin=sin: e.tensor_tensor(w3[:, :, 32:64], heads[:, t, :, 0:32],
                                                             sweep(sin[:, 32:64], 20), ALU.mult))
                dve(lambda e, t=t, cos=cos: e.tensor_tensor(o3, heads[:, t], sweep(cos, 20), ALU.mult),
                    after=[pe_now()])
                r = dve(lambda e: e.tensor_tensor(other, other, work, ALU.add), after=[pool_now()])
                yield
                for b in range(10):
                    dst = bank[5 + b // 4][:, (b % 4) * P:(b % 4 + 1) * P]
                    transpose(dst, other[:, b * P:(b + 1) * P], after=[r, act_now()], signal=None if b == 9 else False)
                for g in range(3):
                    n = 4 if g < 2 else 2
                    act(lambda e, g=g, n=n, t=t: e.activation(
                        turned[:, 4 * g:4 * g + n, t * P:(t + 1) * P],
                        bank[5 + g][:, 0:n * P].rearrange("p (b t) -> p b t", b=n), ACT.Copy), after=[pe_now()])
                yield
            events["rotated"] = everything()
            sync_all()
            dve(lambda e: e.tensor_scalar(small[:, :, 0:8], small[:, :, 0:8], float(8 ** -0.5 * 64 ** -0.5), None,
                                          ALU.mult))
            score, spare, positive2 = A.take(512), A.take(512), [A.take(512) for _ in range(2)]
            keeps = [A.take(512) for _ in range(2)]
            rest = Arena(A.at)
            best, thr, need = col2[:, 64:72], col2[:, 71:72], col2[:, 72:73]
            for q in range(NT):
                w = P * (q + 1)
                mask = C("cmask")[:, 4 * P - w:4 * P]
                keep = keeps[q % 2][:, 0:w]
                if q > 0:
                    added = []
                    for h in range(8):
                        base = HD * (h % 2)
                        b = bank[5 + h % 2]
                        r = pe(lambda e, h=h, b=b, base=base, q=q, w=w: e.matmul(
                            b[:, :w], turned[base:base + HD, 5 + h // 2, q * P:(q + 1) * P],
                            turned[base:base + HD, 9, 0:w], start=True, stop=True),
                            after=[act_now(1) if h > 1 else act_now()], own=False)
                        positive = positive2[h % 2]
                        a = act(lambda e, b=b, positive=positive, w=w: e.activation(positive[:, :w], b[:, :w],
                                                                                    ACT.Relu),
                                after=[r, added[h - 2] if h > 1 else dve_now()], own=False)
                        if h == 0:
                            added.append(dve(lambda e, q=q, w=w, positive=positive: e.tensor_scalar(
                                score[:, :w], positive[:, :w], small[:, q, 0:1], None, ALU.mult), after=[a]))
                        else:
                            added.append(dve(lambda e, q=q, w=w, h=h, positive=positive: e.scalar_tensor_tensor(
                                out=score[:, :w], in0=positive[:, :w], scalar=small[:, q, h:h + 1],
                                in1=score[:, :w], op0=ALU.mult, op1=ALU.add), after=[a]))
                        yield
                    dve(lambda e, w=w, mask=mask: e.tensor_tensor(score[:, :w], score[:, :w], mask, ALU.add))
                    dve(lambda e, w=w: e.tensor_copy(spare[:, :w], score[:, :w]))
                    for _ in range(TOPK // 8 - 1):
                        dve(lambda e, w=w: e.max(best, spare[:, :w]))
                        dve(lambda e, w=w: e.match_replace(spare[:, :w], best, spare[:, :w], 3 * NEG))
                        yield
                    dve(lambda e, w=w: e.max(best, spare[:, :w]))
                    dve(lambda e, w=w, keep=keep: e.tensor_scalar(keep, score[:, :w], thr, None, ALU.is_gt))
                    dve(lambda e, keep=keep: e.tensor_reduce(need, keep, AX, ALU.add))
                    dve(lambda e: e.tensor_scalar(need, need, -1.0, float(TOPK), ALU.mult, ALU.add))
                    yield
                    dve(lambda e, w=w: e.tensor_scalar(score[:, :w], score[:, :w], thr, None, ALU.is_equal))
                    dve(lambda e, w=w: e.tensor_tensor_scan(spare[:, :w], ones[:, 0:1].to_broadcast([P, w]),
                                                            score[:, :w], 0.0, ALU.mult, ALU.add))
                    dve(lambda e, w=w: e.scalar_tensor_tensor(out=score[:, :w], in0=spare[:, :w], scalar=need,
                                                              in1=score[:, :w], op0=ALU.is_le, op1=ALU.mult))
                    dve(lambda e, w=w, keep=keep: e.tensor_tensor(keep, keep, score[:, :w], ALU.add))
                    dve(lambda e, keep=keep: e.tensor_scalar(keep, keep, -1.0, -NEG, ALU.add, ALU.mult))
                else:
                    dve(lambda e, keep=keep, mask=mask: e.tensor_copy(keep, mask))
                yield
                blocks = []
                for h in range(8):
                    base, part = HD * (h // 4), slice(HD * (h % 2), HD * (h % 2) + HD)
                    blocks.append((
                        w, lambda out, h=h, base=base, q=q, w=w: [lambda e: e.matmul(
                            out, turned[base:base + HD, h % 4, q * P:(q + 1) * P], turned[base:base + HD, 4, 0:w],
                            start=True, stop=True)],
                        keep, lambda s, g=h // 4: v[:, s, g * HD:(g + 1) * HD], part,
                        mixed[part, h // 2, q * P:(q + 1) * P]))
                sync_all()
                yield from attention(blocks, HD ** -0.5, Arena(rest.at))

        def head_sum(dst, src, after):
            return pe(lambda e: e.matmul(dst, bones, src, start=True, stop=True), after=after, own=False)

        def normalize(x, scale, eps_col, factor, wrk, banks=(0, 1)):
            before = [dve_now(), pe_now()]
            squares = [act(lambda e, c=c: e.activation(wrk[c], x[:, c, :], ACT.Square), after=before, own=c == 0)
                       for c in range(2)]
            yield
            sums = [head_sum(bank[banks[c]][:, :], wrk[c], [squares[c], *before]) for c in range(2)]
            roots = [act(lambda e, c=c: e.activation(wrk[c], bank[banks[c]][:, :], ACT.Sqrt,
                                                     bias=eps[:, eps_col:eps_col + 1], scale=scale),
                         after=[sums[c]], own=False) for c in range(2)]
            yield
            for c in range(2):
                dve(lambda e, c=c: e.reciprocal(wrk[c], wrk[c]), after=[roots[c]], own=False)
                dve(lambda e, c=c: e.scalar_tensor_tensor(out=x[:, c, :], in0=x[:, c, :], scalar=factor,
                                                          in1=wrk[c], op0=ALU.mult, op1=ALU.mult))

        def two(ap):
            return ap.rearrange("p (c t) -> p c t", c=2)

        def rwkv(lora, A, events):
            scratch = A.take(2 * (SEQ + 1))
            raw = [scratch[:, n * (SEQ + 1):(n + 1) * (SEQ + 1)] for n in range(2)]
            scratch = scratch[:, 0:2 * SEQ]
            r_, k_, v_ = (two(A.take(2 * SEQ)) for _ in range(3))
            for b in range(2):
                dve(lambda e, b=b: e.memset(raw[b][:, 0:1], 0.0))
            for n, dst in enumerate((r_, k_, v_)):
                slot, there = prog.take()
                for c in range(2):
                    b = bank[2 * (n % 2) + c]
                    t = by_channel(slot, c * P, b[:, :], xn, c == 1, after=[there, act_now(1)])
                    act(lambda e, b=b, c=c: e.activation(raw[c][:, 1:SEQ + 1], b[:, :], ACT.Copy),
                        after=[t, dve_now(2)])
                    shifted(raw[c], par1("mu")[:, 2 * n + c:2 * n + c + 1], dst[:, c, :], [act_now()])
                    yield
            ld, a_, kk = (two(A.take(2 * SEQ)) for _ in range(3))
            g_ = mixed[:, 4:6, :]
            up = par1("lora_up")
            for c in range(2):
                for n, (lo, hi, dst, bias) in enumerate(((0, 32, ld, "w0"), (32, 64, a_, "a0"), (64, 128, g_, None))):
                    b = bank[2 + n]
                    t = pe(lambda e, lo=lo, hi=hi, c=c, b=b: e.matmul(b[:, :], up[lo:hi, c * P:(c + 1) * P],
                                                                      lora[lo:hi, :], start=True, stop=True),
                           after=[act_now(), dve_now()])
                    if bias:
                        act(lambda e, b=b, dst=dst, c=c, bias=bias: e.activation(
                            dst[:, c, :], b[:, :], ACT.Sigmoid, bias=par1(bias)[:, c:c + 1]), after=[t])
                    else:
                        act(lambda e, b=b, dst=dst, c=c: e.activation(dst[:, c, :], b[:, :], ACT.Copy), after=[t])
                    yield
            vf, df, vd = two(v_first[:, :]), two(scratch), par1("v_down")
            for c in range(2):
                t = pe(lambda e, c=c: e.matmul(bank[0][0:32, :], vd[:, 32 * c:32 * c + 32], v_[:, c, :],
                                               start=c == 0, stop=c == 1), after=[dve_now(), act_now()])
            low = tmp[3][0:32, :]
            act(lambda e: e.activation(low, bank[0][0:32, :], ACT.Copy), after=[t])
            dve(lambda e: e.tensor_scalar(ld, ld, -0.6065306597126334, None, ALU.mult), after=[act_now(1)])
            for c in range(2):
                dve(lambda e, c=c: e.tensor_scalar(kk[:, c, :], k_[:, c, :], par1("k_k")[:, c:c + 1], None, ALU.mult))
            yield
            for c in range(2):
                t = pe(lambda e, c=c: e.matmul(bank[2 + c][:, :], par1("v_up")[0:32, c * P:(c + 1) * P], low,
                                               start=True, stop=True), after=[act_now()])
                act(lambda e, c=c: e.activation(tmp[c][:, :], bank[2 + c][:, :], ACT.Sigmoid,
                                                bias=par1("v0")[:, c:c + 1]), after=[t])
            sigmoids = act_now()
            yield from normalize(kk, 1.0, 1, 1.0, [tmp[2][:, :], tmp[3][:, :]])
            dve(lambda e: e.tensor_tensor(df, v_, vf, ALU.subtract))
            dve(lambda e: e.scalar_tensor_tensor(out=vf, in0=df, scalar=is_first[:, 0:1], in1=vf, op0=ALU.mult,
                                                 op1=ALU.add))
            dve(lambda e: e.tensor_tensor(df, vf, v_, ALU.subtract))
            for c in range(2):
                dve(lambda e, c=c: e.tensor_tensor(df[:, c, :], df[:, c, :], tmp[c][:, :], ALU.mult),
                    after=[sigmoids])
            dve(lambda e: e.tensor_tensor(v_, v_, df, ALU.add))
            yield
            for c in range(2):
                t_ = tmp[c][:, :]
                dve(lambda e, c=c, t_=t_: e.tensor_scalar(t_, a_[:, c, :], -1.0, par1("k_a")[:, c:c + 1], ALU.add,
                                                          ALU.mult))
                dve(lambda e, c=c, t_=t_: e.scalar_tensor_tensor(out=k_[:, c, :], in0=t_, scalar=1.0,
                                                                 in1=k_[:, c, :], op0=ALU.add, op1=ALU.mult))
            yield
            while "rotated" not in events:
                yield
            for line in (pe, act, dve):
                line.wait(*events["rotated"])
            cm = scratch
            e_pos, e_neg, e_prev = (A.take(2 * SEQ) for _ in range(3))
            tiles = lambda ap: ap.rearrange("p (n t) -> p n t", t=P)
            ldf = ld.rearrange("p c t -> p (c t)")
            for n in range(8):
                dve(lambda e, n=n: e.tensor_tensor_scan(cm[:, n * P:(n + 1) * P], ones, ldf[:, n * P:(n + 1) * P],
                                                        0.0, ALU.mult, ALU.add), own=n == 0)
                if n % 3 == 2:
                    yield
            mid, end = col[:, 0:8], col[:, 8:16]
            dve(lambda e: e.tensor_copy(mid, tiles(cm)[:, :, 63]))
            dve(lambda e: e.tensor_tensor(tiles(cm), tiles(cm), wide(mid, [P, 8, P]), ALU.subtract))
            t = dve(lambda e: e.tensor_tensor(e_prev, cm, ldf, ALU.subtract))
            act(lambda e: e.activation(e_prev, e_prev, ACT.Exp), after=[t])
            act(lambda e: e.activation(e_pos, cm, ACT.Exp))
            act(lambda e: e.activation(e_neg, cm, ACT.Exp, scale=-1.0))
            act(lambda e: e.activation(mid, mid, ACT.Exp))
            t = act(lambda e: e.activation(end, tiles(cm)[:, :, P - 1], ACT.Exp))
            yield
            flat = lambda ap: ap.rearrange("p c t -> p (c t)")
            af, kf, kkf, rf = flat(a_), flat(k_), flat(kk), flat(r_)
            dve(lambda e: e.tensor_tensor(af, af, kkf, ALU.mult), after=[t])
            dve(lambda e: e.tensor_tensor(af, af, e_neg, ALU.mult))
            dve(lambda e: e.scalar_tensor_tensor(out=e_prev, in0=kkf, scalar=-1.0, in1=e_prev, op0=ALU.mult,
                                                 op1=ALU.mult))
            dve(lambda e: e.tensor_tensor(e_neg, kf, e_neg, ALU.mult))
            dve(lambda e: e.tensor_tensor(e_pos, rf, e_pos, ALU.mult))
            bonus = ld
            for c in range(2):
                t = dve(lambda e, c=c: e.scalar_tensor_tensor(out=tmp[c][:, :], in0=r_[:, c, :],
                                                              scalar=par1("r_k")[:, c:c + 1], in1=k_[:, c, :],
                                                              op0=ALU.mult, op1=ALU.mult))
                t = head_sum(bank[c][:, :], tmp[c][:, :], [t, act_now()])
                dve(lambda e, c=c: e.tensor_tensor(bonus[:, c, :], v_[:, c, :], bank[c][:, :], ALU.mult), after=[t])
                yield
            At, Bt, Kt, Rt = e_prev, af, e_neg, e_pos
            sync_all()
            v_tok, b_tok, k_tok = (x.rearrange("p (t n) -> p t n", t=NT) for x in (rf, kf, kkf))
            for n, (src, dst) in enumerate(((flat(v_), v_tok), (Bt, b_tok), (Kt, k_tok))):
                for c in range(2):
                    b = bank[(n * 2 + c) % 4]
                    for t in range(NT):
                        r = transpose(b[:, t * P:(t + 1) * P], src[:, c * SEQ + t * P:c * SEQ + (t + 1) * P],
                                      after=[act_now(3)] if n == 2 else (), signal=None if t == 3 else False)
                    act(lambda e, b=b, dst=dst, c=c: e.activation(dst[:, :, c * P:(c + 1) * P],
                                                                  b[:, :].rearrange("p (t n) -> p t n", t=NT),
                                                                  ACT.Copy), after=[r], own=False)
                    yield
            sync_all()
            quad = lambda ap: ap.rearrange("p (q h t) -> p q h t", q=NT, h=4)
            Lt, T, Tt = (quad(A.take(NT * 4 * P)) for _ in range(3))

            def scores(lhs, rhs, q, b, after=()):
                for half in range(2):
                    for c in range(2):
                        cols = slice(c * SEQ + q * P, c * SEQ + (q + 1) * P)
                        part = slice(half * HD, (half + 1) * HD)
                        t = pe(lambda e, half=half, c=c, cols=cols, part=part: e.matmul(
                            b[half][:, c * P:(c + 1) * P], lhs[part, cols], rhs[part, cols], start=True, stop=True),
                            after=after if half == 0 and c == 0 else (), own=False,
                            signal=None if half and c else False)
                return t

            def masked(dst, b, mask, after):
                for half in range(2):
                    dve(lambda e, half=half: e.tensor_tensor(
                        dst[:, 2 * half:2 * half + 2, :], b[half][:, 0:2 * P].rearrange("p (h t) -> p h t", h=2),
                        sweep(mask, 2), ALU.mult), after=after if half == 0 else (), own=False)

            for q in range(NT):
                b = (bank[0], bank[1])
                t = scores(At, Bt, q, b, [dve_now()])
                masked(T[:, q], b, C("lev", 0), [t])
                b = (bank[2], bank[3])
                t = scores(Bt, At, q, b, [dve_now(2)])
                masked(Tt[:, q], b, C("levT", 0), [t])
                masked(Lt[:, q], b, C("supper"), [t])
                yield
            for X in (T, Tt):
                for q in range(NT):
                    dve(lambda e, X=X, q=q: e.tensor_tensor(X[:, q], X[:, q], sweep(ident, 4), ALU.add),
                        own=q == 0)
            yield from unit_inverse(Lt, T, Tt, [dve_now()])
            sync_all()
            free = flat(v_)
            state, scaled = (free[:, n * 2 * HD:(n + 1) * 2 * HD].rearrange("p (c i) -> p c i", c=2)
                             for n in range(2))
            wv, sa = (free[:, n * 4 * HD:(n + 1) * 4 * HD].rearrange("p (h i) -> p h i", h=4) for n in (1, 2))
            AK, RB, RK = (T[:, n] for n in range(3))
            y = two(scratch)
            dve(lambda e: e.memset(state, 0.0))
            for q in range(NT):
                for n, (lhs, rhs, mask, dst) in enumerate(((Kt, At, "supper", AK), (Bt, Rt, "upper", RB),
                                                           (Kt, Rt, "upper", RK))):
                    b = (bank[2 * (n % 2)], bank[2 * (n % 2) + 1])
                    t = scores(lhs, rhs, q, b, [dve_now(), act_now()] if n == 0 else [dve_now(2)] if n == 2 else ())
                    masked(dst, b, C(mask), [t, pe_now()])
                    yield
                for c in range(2):
                    dve(lambda e, c=c, q=q: e.tensor_scalar(scaled[:, c, :], state[:, c, :],
                                                            mid[:, 4 * c + q:4 * c + q + 1], None, ALU.mult))
                pe.wait(dve_now())
                for half in range(2):
                    part = slice(half * HD, (half + 1) * HD)
                    for c in range(2):
                        h, o = 2 * half + c, bank[2 + half][:, c * HD:(c + 1) * HD]
                        pe(lambda e, part=part, c=c, o=o, q=q: e.matmul(
                            o, At[part, c * SEQ + q * P:c * SEQ + (q + 1) * P], scaled[part, c, :], start=True,
                            stop=False), own=False, signal=False)
                        t = pe(lambda e, h=h, o=o, q=q, c=c, half=half: e.matmul(
                            o, AK[:, h, :], v_tok[:, q, c * P + half * HD:c * P + (half + 1) * HD], start=False,
                            stop=True), own=False)
                    dve(lambda e, half=half: e.tensor_copy(wv[:, 2 * half:2 * half + 2, :], bank[2 + half][
                        :, 0:2 * HD].rearrange("p (h i) -> p h i", h=2)), after=[t], own=False)
                yield
                for h in range(4):
                    t = pe(lambda e, h=h, q=q: e.matmul(bank[4][:, h * HD:(h + 1) * HD], Tt[:, q, h, :],
                                                        wv[:, h, :], start=True, stop=True), after=[dve_now()],
                           own=False)
                dve(lambda e: e.tensor_copy(sa, bank[4][:, 0:256].rearrange("p (h i) -> p h i", h=4)), after=[t])
                yield
                pe.wait(dve_now(), act_now())
                vs = lambda h, q=q: v_tok[:, q, (h % 2) * P + (h // 2) * HD:(h % 2) * P + (h // 2 + 1) * HD]
                for half in range(2):
                    part = slice(half * HD, (half + 1) * HD)
                    for c in range(2):
                        h, o = 2 * half + c, bank[half][part, c * P:(c + 1) * P]
                        cols = slice(c * SEQ + q * P, c * SEQ + (q + 1) * P)
                        pe(lambda e, o=o, part=part, c=c, cols=cols: e.matmul(
                            o, scaled[part, c, :], Rt[part, cols], start=True, stop=False), own=False, signal=False)
                        pe(lambda e, o=o, h=h: e.matmul(o, sa[:, h, :], RB[:, h, :], start=False, stop=False),
                           own=False, signal=False)
                        t = pe(lambda e, o=o, h=h, vs=vs: e.matmul(o, vs(h), RK[:, h, :], start=False, stop=True),
                               own=False)
                    act(lambda e, half=half, part=part, q=q: e.activation(
                        y[part, :, q * P:(q + 1) * P], bank[half][part, 0:2 * P].rearrange("p (c t) -> p c t", c=2),
                        ACT.Copy), after=[t], own=False)
                yield
                for half in range(2):
                    part = slice(half * HD, (half + 1) * HD)
                    for c in range(2):
                        h, o = 2 * half + c, bank[2 + half][part, c * HD:(c + 1) * HD]
                        hs = slice(c * P + half * HD, c * P + (half + 1) * HD)
                        pe(lambda e, o=o, h=h, hs=hs, q=q: e.matmul(o, b_tok[:, q, hs], sa[:, h, :], start=True,
                                                                    stop=False), own=False, signal=False)
                        t = pe(lambda e, o=o, hs=hs, h=h, vs=vs, q=q: e.matmul(o, k_tok[:, q, hs], vs(h), start=False,
                                                                               stop=True), own=False)
                    dve(lambda e, half=half, part=part: e.tensor_tensor(
                        state[part], scaled[part], bank[2 + half][part, 0:2 * HD].rearrange("p (c i) -> p c i", c=2),
                        ALU.add), after=[t], own=False)
                for c in range(2):
                    dve(lambda e, c=c, q=q: e.tensor_scalar(state[:, c, :], state[:, c, :],
                                                            end[:, 4 * c + q:4 * c + q + 1], None, ALU.mult))
                yield
            for c in range(2):
                t = head_sum(bank[c][:, :], y[:, c, :], [act_now(), dve_now()])
                dve(lambda e, c=c: e.scalar_tensor_tensor(out=y[:, c, :], in0=bank[c][:, :], scalar=-1.0 / HD,
                                                          in1=y[:, c, :], op0=ALU.mult, op1=ALU.add), after=[t])
                yield
            yield from normalize(y, 1.0 / HD, 2, 1.0, [tmp[0][:, :], tmp[1][:, :]])
            for c in range(2):
                dve(lambda e, c=c: e.tensor_scalar(y[:, c, :], y[:, c, :], par1("gn_w")[:, c:c + 1],
                                                   par1("gn_b")[:, c:c + 1], ALU.mult, ALU.add))
                dve(lambda e, c=c: e.tensor_tensor(y[:, c, :], y[:, c, :], bonus[:, c, :], ALU.add))
                dve(lambda e, c=c: e.tensor_tensor(g_[:, c, :], y[:, c, :], g_[:, c, :], ALU.mult))
                yield

        def delta_rule(small, A):
            raw = [A.take(SEQ + 3) for _ in range(2)]
            q_, k_, v_ = (two(A.take(2 * SEQ)) for _ in range(3))
            z_ = mixed[:, 6:8, :]
            over = [act_now()]
            for b in range(2):
                over.append(dve(lambda e, b=b: e.memset(raw[b][:, 0:3], 0.0)))
            cw = par1("conv")
            for n, dst in enumerate((q_, k_, v_, z_)):
                slot, there = prog.take()
                for c in range(2):
                    b = bank[2 * (n % 2) + c]
                    t = by_channel(slot, c * P, b[:, :], xn, c == 1,
                                   after=[there, act_now(3), over[0]])
                    if n == 3:
                        act(lambda e, b=b, c=c: e.activation(z_[:, c, :], b[:, :], ACT.Silu), after=[t])
                        yield
                        continue
                    act(lambda e, b=b, c=c: e.activation(raw[c][:, 3:SEQ + 3], b[:, :], ACT.Copy),
                        after=[t, dve_now(4), over[-1]])
                    yield
                    at = 4 * (2 * n + c)
                    dve(lambda e, c=c, dst=dst, at=at: e.tensor_scalar(dst[:, c, :], raw[c][:, 3:SEQ + 3],
                                                                       cw[:, at + 3:at + 4], None, ALU.mult),
                        after=[act_now()])
                    for j in range(3):
                        dve(lambda e, c=c, j=j, dst=dst, at=at: e.scalar_tensor_tensor(
                            out=dst[:, c, :], in0=raw[c][:, j:j + SEQ], scalar=cw[:, at + j:at + j + 1],
                            in1=dst[:, c, :], op0=ALU.mult, op1=ALU.add))
                    act(lambda e, c=c, dst=dst: e.activation(dst[:, c, :], dst[:, c, :], ACT.Silu),
                        after=[dve_now()])
                    yield
            wrk = [tmp[0][:, :], tmp[1][:, :]]
            yield from normalize(q_, 1.0, 0, HD ** -0.5, wrk)
            yield from normalize(k_, 1.0, 0, 1.0, wrk)
            stat = col[:, 0:256].rearrange("p (n t h) -> p n t h", n=16, h=4)
            beta, g, gc, egc, w_, x_, y_, nb, nbe, gl = (stat[:, n] for n in range(10))
            ea = col[:, 256:260]
            act(lambda e: e.activation(beta, small[:, :, 8:12], ACT.Sigmoid), after=[dve_now()])
            dve(lambda e: e.tensor_tensor(g, small[:, :, 12:16], sweep(par1("dt_bias"), NT), ALU.add),
                after=[act_now()])
            yield
            dve(lambda e: e.tensor_scalar(w_, g, 0.0, None, ALU.max))
            dve(lambda e: e.tensor_scalar(x_, g, 0.0, None, ALU.min))
            dve(lambda e: e.tensor_tensor(x_, x_, w_, ALU.subtract))
            yield
            act(lambda e: e.activation(x_, x_, ACT.Exp), after=[dve_now()])
            act(lambda e: e.activation(x_, x_, ACT.Ln, bias=1.0))
            act(lambda e: e.activation(ea, par1("a_log"), ACT.Exp))
            dve(lambda e: e.tensor_tensor(w_, w_, x_, ALU.add), after=[act_now()])
            dve(lambda e: e.scalar_tensor_tensor(out=g, in0=w_, scalar=-1.0, in1=sweep(ea, NT), op0=ALU.mult,
                                                 op1=ALU.mult))
            yield
            pe(lambda e: e.matmul(bank[0][:, 0:16], C("upper"), g, start=True, stop=True),
               after=[dve_now(), act_now()])
            t = pe(lambda e: e.matmul(bank[1][:, 0:16], ones, g, start=True, stop=True))
            yield
            dve(lambda e: e.tensor_copy(gc.rearrange("p t h -> p (t h)"), bank[0][:, 0:16]), after=[t])
            dve(lambda e: e.tensor_copy(gl.rearrange("p t h -> p (t h)"), bank[1][:, 0:16]))
            dve(lambda e: e.tensor_tensor(x_, gl, gc, ALU.subtract))
            act(lambda e: e.activation(egc, gc, ACT.Exp), after=[dve_now()])
            act(lambda e: e.activation(x_, x_, ACT.Exp))
            act(lambda e: e.activation(gl, gl, ACT.Exp))
            yield
            dve(lambda e: e.tensor_scalar(nb, beta, -1.0, None, ALU.mult), after=[act_now()])
            dve(lambda e: e.tensor_tensor(nbe, nb, egc, ALU.mult))
            flat = lambda ap: ap.rearrange("p c t -> p (c t)")
            qf, kf, vf = flat(q_), flat(k_), flat(v_)
            k_tok, vb = (A.take(NT * 256).rearrange("p (t n) -> p t n", t=NT) for _ in range(2))
            sync_all()
            for c in range(2):
                for t in range(NT):
                    r = transpose(bank[c][:, t * P:(t + 1) * P], kf[:, c * SEQ + t * P:c * SEQ + (t + 1) * P],
                                  signal=None if t == 3 else False)
                act(lambda e, c=c: e.activation(k_tok[:, :, c * P:(c + 1) * P],
                                                bank[c][:, :].rearrange("p (t n) -> p t n", t=NT), ACT.Copy),
                    after=[r], own=False)
                for t in range(NT):
                    r = transpose(bank[2 + c][:, t * P:(t + 1) * P], vf[:, c * SEQ + t * P:c * SEQ + (t + 1) * P],
                                  signal=None if t == 3 else False)
                for half in range(2):
                    dve(lambda e, c=c, half=half: e.tensor_tensor(
                        vb[:, :, c * P + half * HD:c * P + (half + 1) * HD],
                        bank[2 + c][:, :].rearrange("p (t n) -> p t n", t=NT)[:, :, half * HD:(half + 1) * HD],
                        wide(beta[:, :, 2 * half + c], [P, NT, HD]), ALU.mult), after=[r], own=False)
                yield
            sync_all()
            quad = lambda ap: ap.rearrange("p (q h t) -> p q h t", q=NT, h=4)
            Lt, T, Tt, Xt = (quad(A.take(NT * 4 * P)) for _ in range(4))
            h4 = lambda ap: ap.rearrange("p (h t) -> p h t", h=4)
            dec, dst_, att = (h4(tmp[n][:, :]) for n in range(3))
            for q in range(NT):
                for h in range(4):
                    t = pe(lambda e, q=q, h=h: e.matmul(bank[4][:, h * P:(h + 1) * P],
                                                        g[:, q, h:h + 1].to_broadcast([P, P]), C("upper"),
                                                        start=True, stop=True), after=[dve_now()], own=False)
                dve(lambda e, q=q: e.tensor_tensor(dec, h4(bank[4][:, :]), wide(gc[:, q, :], [P, 4, P]),
                                                   ALU.subtract), after=[t])
                dve(lambda e: e.tensor_scalar(dec, dec, 0.0, None, ALU.max))
                yield
                act(lambda e: e.activation(dec, dec, ACT.Exp, scale=-1.0), after=[dve_now()])
                dve(lambda e: e.tensor_tensor(dec, dec, sweep(C("lower"), 4), ALU.mult), after=[act_now()])
                for n, src in enumerate((kf, qf)):
                    for half in range(2):
                        for c in range(2):
                            cols = slice(c * SEQ + q * P, c * SEQ + (q + 1) * P)
                            part = slice(half * HD, (half + 1) * HD)
                            t = pe(lambda e, n=n, half=half, c=c, cols=cols, part=part, src=src: e.matmul(
                                bank[2 * n + half][:, c * P:(c + 1) * P], src[part, cols], kf[part, cols],
                                start=True, stop=True), own=False, after=[dve_now()])
                    for half in range(2):
                        dve(lambda e, n=n, half=half: e.tensor_tensor(
                            (dst_, att)[n][:, 2 * half:2 * half + 2, :],
                            bank[2 * n + half][:, 0:2 * P].rearrange("p (h t) -> p h t", h=2),
                            dec[:, 2 * half:2 * half + 2, :], ALU.mult), after=[t, pe_now()])
                    yield
                dve(lambda e, q=q: e.tensor_tensor(dst_, dst_, wide(nb[:, q, :], [P, 4, P]), ALU.mult))
                dve(lambda e: e.tensor_tensor(dst_, dst_, sweep(C("slower"), 4), ALU.mult))
                dve(lambda e, q=q: e.tensor_tensor(T[:, q], dst_, sweep(C("lev", 0), 4), ALU.mult))
                for n, src in enumerate((dst_, att)):
                    for h in range(4):
                        t = transpose(bank[4 - 4 * n][:, h * P:(h + 1) * P], src[:, h, :], after=[dve_now(), act_now()],
                                      signal=None if h == 3 else False)
                    act(lambda e, n=n, q=q: e.activation((Lt, Xt)[n][:, q], h4(bank[4 - 4 * n][:, :]), ACT.Copy),
                        after=[t])
                yield
                dve(lambda e, q=q: e.tensor_tensor(Tt[:, q], Lt[:, q], sweep(C("levT", 0), 4), ALU.mult),
                    after=[act_now(), pe_now()])
            for X in (T, Tt):
                for q in range(NT):
                    dve(lambda e, X=X, q=q: e.tensor_tensor(X[:, q], X[:, q], sweep(ident, 4), ALU.add),
                        own=q == 0)
            sync_all()
            yield from unit_inverse(Lt, T, Tt, [dve_now()])
            for c in range(2):
                for q in range(NT):
                    for half in range(2):
                        h = 2 * half + c
                        t = pe(lambda e, c=c, q=q, h=h, half=half: e.matmul(
                            bank[c][half * HD:(half + 1) * HD, q * P:(q + 1) * P],
                            g[:, q, h:h + 1].to_broadcast([P, HD]), C("upper"), start=True, stop=True),
                            after=[dve_now(), act_now()], own=False)
                act(lambda e, c=c: e.activation(tmp[c][:, :], bank[c][:, :], ACT.Exp), after=[t])
                yield
                dve(lambda e, c=c: e.tensor_tensor(q_[:, c, :], q_[:, c, :], tmp[c][:, :], ALU.mult),
                    after=[act_now()])
            sync_all()
            state = A.take(2 * HD).rearrange("p (c i) -> p c i", c=2)
            rest, vn, vs = (A.take(4 * HD).rearrange("p (h i) -> p h i", h=4) for _ in range(3))
            y = two(A.take(2 * SEQ))
            dve(lambda e: e.memset(state, 0.0))
            for q in range(NT):
                pe.wait(dve_now(), act_now())
                for half in range(2):
                    part = slice(half * HD, (half + 1) * HD)
                    for c in range(2):
                        h, o = 2 * half + c, bank[2 + half][:, c * HD:(c + 1) * HD]
                        t = pe(lambda e, part=part, c=c, o=o, q=q: e.matmul(
                            o, kf[part, c * SEQ + q * P:c * SEQ + (q + 1) * P], state[part, c, :], start=True,
                            stop=True), own=False)
                    for c in range(2):
                        h, o = 2 * half + c, bank[2 + half][:, c * HD:(c + 1) * HD]
                        dve(lambda e, o=o, h=h, q=q, c=c, half=half: e.scalar_tensor_tensor(
                            out=rest[:, h, :], in0=o, scalar=nbe[:, q, h:h + 1],
                            in1=vb[:, q, c * P + half * HD:c * P + (half + 1) * HD], op0=ALU.mult, op1=ALU.add),
                            after=[t], own=False)
                yield
                for h in range(4):
                    t = pe(lambda e, h=h, q=q: e.matmul(bank[4][:, h * HD:(h + 1) * HD], Tt[:, q, h, :],
                                                        rest[:, h, :], start=True, stop=True), after=[dve_now()],
                           own=False)
                v4 = bank[4][:, 0:256].rearrange("p (h i) -> p h i", h=4)
                dve(lambda e, v4=v4: e.tensor_copy(vn, v4), after=[t])
                dve(lambda e, q=q: e.tensor_tensor(vs, vn, wide(x_[:, q, :], [P, 4, HD]), ALU.mult))
                yield
                pe.wait(dve_now())
                for half in range(2):
                    part = slice(half * HD, (half + 1) * HD)
                    for c in range(2):
                        h, o = 2 * half + c, bank[half][part, c * P:(c + 1) * P]
                        cols = slice(c * SEQ + q * P, c * SEQ + (q + 1) * P)
                        pe(lambda e, o=o, part=part, c=c, cols=cols: e.matmul(
                            o, state[part, c, :], qf[part, cols], start=True, stop=False), own=False, signal=False)
                        t = pe(lambda e, o=o, h=h, q=q: e.matmul(o, vn[:, h, :], Xt[:, q, h, :], start=False,
                                                                 stop=True), own=False)
                    act(lambda e, half=half, part=part, q=q: e.activation(
                        y[part, :, q * P:(q + 1) * P], bank[half][part, 0:2 * P].rearrange("p (c t) -> p c t", c=2),
                        ACT.Copy), after=[t], own=False)
                for half in range(2):
                    part = slice(half * HD, (half + 1) * HD)
                    for c in range(2):
                        h, o = 2 * half + c, bank[2 + half][part, c * HD:(c + 1) * HD]
                        hs = slice(c * P + half * HD, c * P + (half + 1) * HD)
                        t = pe(lambda e, o=o, h=h, hs=hs, q=q: e.matmul(o, k_tok[:, q, hs], vs[:, h, :], start=True,
                                                                        stop=True), own=False)
                    for c in range(2):
                        h, o = 2 * half + c, bank[2 + half][part, c * HD:(c + 1) * HD]
                        dve(lambda e, o=o, part=part, c=c, h=h, q=q: e.scalar_tensor_tensor(
                            out=state[part, c, :], in0=state[part, c, :], scalar=gl[part, q, h:h + 1], in1=o,
                            op0=ALU.mult, op1=ALU.add), after=[t, pe_now()], own=False)
                yield
            sync_all()
            yield from normalize(y, 1.0 / HD, 0, 1.0, wrk)
            for c in range(2):
                dve(lambda e, c=c: e.scalar_tensor_tensor(out=z_[:, c, :], in0=y[:, c, :],
                                                          scalar=par1("o_norm")[:, c:c + 1], in1=z_[:, c, :],
                                                          op0=ALU.mult, op1=ALU.mult))

        with prog.layers(DEPTH):
            load_parameters(NPAR1)
            ffn(par1("ffn_norm0"))
            chunks = rms_norm(xT, par1("mix_norm"), xn, KC, ready=[dve_now(KC - 1 - d) for d in range(KC)])
            A = Arena()
            small = A.take(NT * 16).rearrange("p (t n) -> p t n", t=NT)
            lora = A.take(SEQ)
            late = Arena(ARENA - 20 * NT * HD - NT * HD - 2 * 20 * HD)
            tok = late.take(20 * NT * HD).rearrange("p (t n) -> p t n", t=NT)
            keys = late.take(NT * HD).rearrange("p (t n) -> p t n", t=NT)
            work, other = (late.take(20 * HD) for _ in range(2))
            v = attention_projections(tok, A, chunks)
            recurrent = Arena(A.at + DSA_ARENA)
            mixed_slot(keys, small, lora, arena[:, recurrent.at:recurrent.at + SEQ + 1])
            sync_all()
            events = {}

            def recurrences():
                yield from rwkv(lora, Arena(recurrent.at), events)
                yield from delta_rule(small, Arena(recurrent.at))

            prog.weave({"recurrent": (STEPS, recurrences()),
                        "attention": (1, dsa(tok, keys, small, v, work, other, A, events))})
            sync_all()
            ffn(par1("ffn_norm1"), project_out(ahead=True))
            dve(lambda e: e.memset(is_first[:, :], 0.0))
            assert prog.slot == LAYER_SLOTS, prog.slot
            prog.epoch(1)


        load_parameters(NPAR2)

        def fox_projections(A):
            q_, k_ = (A.take(4 * SEQ).rearrange("p (c t) -> p c t", c=4) for _ in range(2))
            v = A.take(NT * 512).rearrange("p (t n) -> p t n", t=NT)
            n = 0
            for dst in (q_, k_):
                for s in range(2):
                    slot, there = prog.take()
                    for c in range(2):
                        b = bank[n % 4]
                        n += 1
                        t = by_channel(slot, c * P, b[:, :], xn, c == 1, after=[there, act_now()])
                        act(lambda e, b=b, dst=dst, c=2 * s + c: e.activation(dst[:, c, :], b[:, :], ACT.Copy),
                            after=[t], own=False)
            for s in range(2):
                slot, there = prog.take()
                for t in range(NT):
                    b = bank[4 + t]
                    r = by_token(slot, 0, 256, b[:, 0:256], xn, t, t == NT - 1, after=[there, act_now()])
                    act(lambda e, b=b, t=t, s=s: e.activation(v[:, t, 256 * s:256 * s + 256], b[:, 0:256], ACT.Copy),
                        after=[r], own=False)
            slot, there = prog.take()
            t = by_channel(slot, 0, bank[0][0:48, :], xn, True, after=[there, act_now()], m=48)
            cf, ga = A.take(SEQ), A.take(SEQ)
            s1, s2 = tmp[0][0:8, :], tmp[1][0:8, :]
            act(lambda e: e.activation(ga[32:48, :], bank[0][32:48, :], ACT.Copy), after=[t])
            log_sigmoid(cf[0:8, :], bank[0][0:8, :], par2("b_forget")[0:8, 0:1], s1, s2)
            dve(lambda e: e.tensor_tensor_scan(s1, ones[0:8, 0:1].to_broadcast([8, SEQ]), cf[0:8, :], 0.0, ALU.mult,
                                               ALU.add))
            dve(lambda e: e.tensor_scalar(cf[0:8, :], s1, -(HD ** 0.5), None, ALU.mult))
            return q_, k_, v, cf, ga

        def fox_attention(q_, k_, v, cf, A):
            blocks = []
            for q in range(NT):
                w = P * (q + 1)
                for h in range(8):
                    part = slice(HD * (h % 2), HD * (h % 2) + HD)
                    blocks.append((
                        w, lambda out, q=q, h=h, part=part, w=w: [
                            lambda e: e.matmul(out, q_[part, h // 2, q * P:(q + 1) * P], k_[part, h // 2, 0:w],
                                               start=True, stop=False),
                            lambda e: e.matmul(out, ident[0:8, h:h + 1].to_broadcast([8, P]), cf[0:8, 0:w],
                                               start=False, stop=True)],
                        C("cmask")[:, 4 * P - w:4 * P], lambda s, h=h: v[:, s, h * HD:(h + 1) * HD], part,
                        mixed[part, h // 2, q * P:(q + 1) * P]))
            wrk = [A.take(SEQ) for _ in range(2)]
            yield from attention(blocks, HD ** -0.5, A)
            for c in range(2):
                yield from normalize(mixed[:, 2 * c:2 * c + 2, :], 1.0 / HD, 0, 1.0, wrk, banks=(5, 6))
            for c in range(4):
                dve(lambda e, c=c: e.tensor_scalar(mixed[:, c, :], mixed[:, c, :], par2("fox_gain")[:, c:c + 1], None,
                                                   ALU.mult))

        def log_sigmoid(out, in_, bias, s1, s2):
            dve(lambda e: e.tensor_scalar(out, in_, bias, None, ALU.add), after=[pe_now(), used_now(), act_now()])
            dve(lambda e: e.tensor_scalar(s1, out, 0.0, None, ALU.max))
            dve(lambda e: e.tensor_scalar(s2, out, 0.0, None, ALU.min))
            dve(lambda e: e.tensor_tensor(s1, s2, s1, ALU.subtract))
            act(lambda e: e.activation(s1, s1, ACT.Exp), after=[dve_now()])
            act(lambda e: e.activation(s1, s1, ACT.Ln, bias=1.0))
            dve(lambda e: e.tensor_tensor(out, s2, s1, ALU.subtract), after=[act_now()])

        def gla(ga, A, events):
            q_, k_ = (A.take(2 * SEQ) for _ in range(2))
            gate = A.take(4 * SEQ).rearrange("p (c t) -> p c t", c=4)
            v = A.take(NT * 512).rearrange("p (t n) -> p t n", t=NT)
            for dst, scale in ((q_, HD ** -0.5), (k_, 1.0)):
                slot, there = prog.take()
                for c in range(2):
                    b = bank[c]
                    t = by_channel(slot, c * P, b[:, :], xn, c == 1, after=[there, act_now()])
                    act(lambda e, b=b, dst=dst, c=c, scale=scale: e.activation(dst[:, c * SEQ:(c + 1) * SEQ],
                                                                              b[:, :], ACT.Copy, scale=scale),
                        after=[t])
                    yield
            for s in range(2):
                slot, there = prog.take()
                for t in range(NT):
                    b = bank[t]
                    r = by_token(slot, 0, 256, b[:, 0:256], xn, t, t == NT - 1, after=[there, act_now(1)])
                    act(lambda e, b=b, t=t, s=s: e.activation(v[:, t, 256 * s:256 * s + 256], b[:, 0:256], ACT.Copy),
                        after=[r], own=False)
                    yield
            for s in range(2):
                slot, there = prog.take()
                for c in range(2):
                    b = bank[2 * s + c]
                    t = by_channel(slot, c * P, b[:, :], xn, c == 1, after=[there, act_now()])
                    act(lambda e, b=b, c=2 * s + c: e.activation(gate[:, c, :], b[:, :], ACT.Silu), after=[t],
                        own=False)
                    yield
            events["projected"] = True
            la, cs, eq, ek = (A.take(2 * SEQ) for _ in range(4))
            for c in range(2):
                pe(lambda e, c=c: e.matmul(bank[2 + c][:, :], par2("alpha_up")[32:48, c * P:(c + 1) * P],
                                           ga[32:48, :], start=True, stop=True), after=[act_now(), dve_now()])
                log_sigmoid(la[:, c * SEQ:(c + 1) * SEQ], bank[2 + c][:, :], par2("b_alpha")[:, c:c + 1], tmp[0][:, :],
                            tmp[1][:, :])
                yield
            dve(lambda e: e.tensor_scalar(la, la, 1.0 / 16.0, None, ALU.mult))
            for n in range(8):
                dve(lambda e, n=n: e.tensor_tensor_scan(cs[:, n * P:(n + 1) * P], ones, la[:, n * P:(n + 1) * P],
                                                        0.0, ALU.mult, ALU.add), own=n == 0)
            yield
            tiles = lambda ap: ap.rearrange("p (n t) -> p n t", t=P)
            end = col[:, 0:8]
            dve(lambda e: e.tensor_copy(end, tiles(cs)[:, :, P - 1]))
            dve(lambda e: e.tensor_tensor(tiles(ek), wide(end, [P, 8, P]), tiles(cs), ALU.subtract))
            act(lambda e: e.activation(ek, ek, ACT.Exp), after=[dve_now()])
            act(lambda e: e.activation(end, end, ACT.Exp))
            yield
            dve(lambda e: e.tensor_tensor(ek, ek, k_, ALU.mult), after=[act_now()])
            k_tok = A.take(NT * 256).rearrange("p (t n) -> p t n", t=NT)
            sync_all()
            for c in range(2):
                for t in range(NT):
                    r = transpose(bank[c][:, t * P:(t + 1) * P], ek[:, c * SEQ + t * P:c * SEQ + (t + 1) * P],
                                  signal=None if t == 3 else False)
                act(lambda e, c=c: e.activation(k_tok[:, :, c * P:(c + 1) * P],
                                                bank[c][:, :].rearrange("p (t n) -> p t n", t=NT), ACT.Copy),
                    after=[r], own=False)
                yield
            sync_all()
            att = A.take(NT * 4 * P).rearrange("p (q h t) -> p q h t", q=NT, h=4)

            def level_scores(kx, qx, use):
                for q in range(NT):
                    for half in range(2):
                        use(q, half, score_pair(kx, qx, q, half))
                    yield

            def score_pair(kx, qx, q, half):
                b = bank[(2 * q + half) % 4]
                for c in range(2):
                    cols = slice(c * SEQ + q * P, c * SEQ + (q + 1) * P)
                    part = slice(half * HD, (half + 1) * HD)
                    t = pe(lambda e, b=b, c=c, cols=cols, part=part: e.matmul(
                        b[:, c * P:(c + 1) * P], kx[part, cols], qx[part, cols], start=True, stop=True),
                        after=[dve_now(3)] if c == 0 else (), own=False, signal=None if c else False)
                return t

            def pair_of(q, half):
                return (att[:, q, 2 * half:2 * half + 2, :],
                        bank[(2 * q + half) % 4][:, 0:2 * P].rearrange("p (h t) -> p h t", h=2))

            def diagonal(q, half, t):
                dst, src = pair_of(q, half)
                dve(lambda e: e.tensor_tensor(dst, src, sweep(ident, 2), ALU.mult), after=[t], own=False)

            pe.wait(dve_now())
            yield from level_scores(k_, q_, diagonal)
            dve(lambda e: e.memset(eq, 0.0), after=[pe_now()])
            dve(lambda e: e.memset(ek, 0.0))
            for lv in range(7):
                half_w = 1 << lv
                view = lambda ap, h=half_w: ap.rearrange("p (n s h) -> p n s h", s=2, h=h)
                ref = view(cs)[:, :, 0, half_w - 1].unsqueeze(2).to_broadcast([P, 512 // half_w, half_w])
                late, early = view(cs)[:, :, 1, :], view(cs)[:, :, 0, :]
                dve(lambda e, ref=ref, late=late, view=view: e.tensor_tensor(view(eq)[:, :, 1, :], late, ref,
                                                                             ALU.subtract), after=[pe_now()])
                dve(lambda e, ref=ref, early=early, view=view: e.tensor_tensor(view(ek)[:, :, 0, :], ref, early,
                                                                               ALU.subtract))
                act(lambda e, view=view: e.activation(view(eq)[:, :, 1, :], view(eq)[:, :, 1, :], ACT.Exp),
                    after=[dve_now()])
                act(lambda e, view=view: e.activation(view(ek)[:, :, 0, :], view(ek)[:, :, 0, :], ACT.Exp))
                yield
                dve(lambda e, view=view: e.tensor_tensor(view(eq)[:, :, 1, :], view(eq)[:, :, 1, :],
                                                         view(q_)[:, :, 1, :], ALU.mult), after=[act_now()])
                dve(lambda e, view=view: e.tensor_tensor(view(ek)[:, :, 0, :], view(ek)[:, :, 0, :],
                                                         view(k_)[:, :, 0, :], ALU.mult))
                pe.wait(dve_now())
                mask = sweep(C("levT", lv), 2).bitcast(U32)

                def into(q, half, t, mask=mask):
                    dst, src = pair_of(q, half)
                    dve(lambda e: e.copy_predicated(dst, mask, src), after=[t], own=False)

                yield from level_scores(ek, eq, into)
            act(lambda e: e.activation(eq, cs, ACT.Exp), after=[pe_now(), dve_now()])
            dve(lambda e: e.tensor_tensor(eq, eq, q_, ALU.mult), after=[act_now()])
            yield
            sync_all()
            state = A.take(2 * P).rearrange("p (c v) -> p c v", c=2)
            dve(lambda e: e.memset(state, 0.0))
            for q in range(NT):
                pe.wait(dve_now(), act_now())
                for half in range(2):
                    part = slice(half * HD, (half + 1) * HD)
                    for c in range(2):
                        h, head = 2 * half + c, 2 * c + half
                        o = bank[half][:, c * P:(c + 1) * P]
                        pe(lambda e, o=o, part=part, c=c, q=q: e.matmul(
                            o, state[part, c, :], eq[part, c * SEQ + q * P:c * SEQ + (q + 1) * P], start=True,
                            stop=False), own=False, signal=False)
                        t = pe(lambda e, o=o, h=h, head=head, q=q: e.matmul(
                            o, v[:, q, head * P:(head + 1) * P], att[:, q, h, :], start=False, stop=True), own=False)
                    act(lambda e, half=half, q=q: e.activation(
                        mixed[:, 4 + half:8:2, q * P:(q + 1) * P],
                        bank[half][:, 0:2 * P].rearrange("p (c t) -> p c t", c=2), ACT.Copy), after=[t], own=False)
                yield
                for half in range(2):
                    part = slice(half * HD, (half + 1) * HD)
                    for c in range(2):
                        head, o = 2 * c + half, bank[2 + half][part, c * P:(c + 1) * P]
                        hs = slice(c * P + half * HD, c * P + (half + 1) * HD)
                        t = pe(lambda e, o=o, hs=hs, head=head, q=q: e.matmul(
                            o, k_tok[:, q, hs], v[:, q, head * P:(head + 1) * P], start=True, stop=True), own=False)
                    for c in range(2):
                        o = bank[2 + half][part, c * P:(c + 1) * P]
                        dve(lambda e, o=o, part=part, c=c, q=q: e.scalar_tensor_tensor(
                            out=state[part, c, :], in0=state[part, c, :], scalar=end[part, 4 * c + q:4 * c + q + 1],
                            in1=o, op0=ALU.mult, op1=ALU.add), after=[t, pe_now()], own=False)
                yield
            sync_all()
            wrk = [ap[:, n * SEQ:(n + 1) * SEQ] for ap in (la, ek) for n in range(2)]
            squares = [act(lambda e, h=h: e.activation(wrk[h], mixed[:, 4 + h, :], ACT.Square), own=False)
                       for h in range(4)]
            yield
            sums = [pe(lambda e, h=h: e.matmul(bank[h][:, :], ones, wrk[h], start=True, stop=True),
                       after=[squares[h]], own=False) for h in range(4)]
            roots = [act(lambda e, h=h: e.activation(wrk[h], bank[h][:, :], ACT.Sqrt, bias=eps[:, 0:1],
                                                     scale=1.0 / P), after=[sums[h]], own=False) for h in range(4)]
            yield
            for h in range(4):
                y = mixed[:, 4 + h, :]
                dve(lambda e, h=h: e.reciprocal(wrk[h], wrk[h]), after=[roots[h]], own=False)
                dve(lambda e, y=y, h=h: e.scalar_tensor_tensor(out=y, in0=y, scalar=par2("gla_gain")[:, h:h + 1],
                                                               in1=wrk[h], op0=ALU.mult, op1=ALU.mult))
                dve(lambda e, y=y, h=h: e.tensor_tensor(y, y, gate[:, h, :], ALU.mult))

        def memory(mem, loaded, k_, v, events):
            squares = [tmp[2][:, n * MEM:(n + 1) * MEM] for n in range(2)]
            rstd, SUM = tmp[3][:, :MEM], bank[4]
            read = [None, None]
            for c in range(KC):
                t = act(lambda e, c=c: e.activation(squares[c % 2], mem[:, c, :], ACT.Square),
                        after=[loaded, read[c % 2]], own=False)
                read[c % 2] = t = pe(lambda e, c=c: e.matmul(SUM[:, :MEM], ones, squares[c % 2], start=c == 0,
                                                             stop=c == KC - 1), after=[t], own=False)
                yield
            reciprocal_root(rstd, SUM[:, :MEM], 1.0 / D, 0, [t])
            for c in range(KC):
                dve(lambda e, c=c: e.scalar_tensor_tensor(out=mem[:, c, :], in0=mem[:, c, :],
                                                          scalar=par2("mem_norm")[:, c:c + 1], in1=rstd,
                                                          op0=ALU.mult, op1=ALU.mult), own=c == 0)
                if c % 3 == 2:
                    yield
            while "projected" not in events:
                yield
            for s in range(2):
                slot, there = prog.take()
                for c in range(2):
                    t = by_channel(slot, c * P, SUM[:, :MEM], mem, c == 1, after=[there, dve_now(), act_now()], n=MEM)
                    act(lambda e, c=2 * s + c: e.activation(k_[:, c, :], SUM[:, :MEM], ACT.Copy), after=[t],
                        own=False)
                    yield
            for s in range(2):
                slot, there = prog.take()
                for t in range(2):
                    r = by_token(slot, 0, 256, SUM[:, 0:256], mem, t, t == 1, after=[there, act_now()])
                    act(lambda e, t=t, s=s: e.activation(v[:, t, 256 * s:256 * s + 256], SUM[:, 0:256], ACT.Copy),
                        after=[r], own=False)
                    yield

        def cross(k_, v, added, A):
            chunks = rms_norm(xT, par2("cross_norm"), xn, KC, ready=added)
            q_ = A.take(4 * SEQ).rearrange("p (c t) -> p c t", c=4)
            sync = everything()
            act.wait(*sync)
            for s in range(2):
                slot, there = prog.take()
                for c in range(2):
                    b = bank[2 * s + c]
                    t = by_channel(slot, c * P, b[:, :], xn, c == 1, after=[there, chunks[-1]])
                    act(lambda e, b=b, c=2 * s + c: e.activation(q_[:, c, :], b[:, :], ACT.Copy), after=[t],
                        own=False)
            sync_all()
            blocks = [[], []]
            for q in range(NT):
                for h in range(4):
                    blocks[h % 2].append((MEM, lambda out, h=h, q=q: [lambda e: e.matmul(
                        out, q_[:, h, q * P:(q + 1) * P], k_[:, h, :], start=True, stop=True)],
                        None, lambda s, h=h: v[:, s, h * P:(h + 1) * P], slice(0, P), mixed[:, h, q * P:(q + 1) * P]))
            prog.weave({"even heads": (1, attention(blocks[0], P ** -0.5, A)),
                        "odd heads": (1, attention(blocks[1], P ** -0.5, A, (1, 2, 3), 8))})
            return project_out(2, ahead=True)

        def router(chunks):
            gates = arena[:, GATES_AT:GATES_AT + N_EXPERTS * SEQ].rearrange("p (e t) -> p e t", e=N_EXPERTS)
            ready = [used_now()]
            s = (prog.slot - 1) % RING
            split_slot()
            for t in range(NT):
                for k in range(KC):
                    for n, (w, part) in enumerate(passes(s)):
                        end = k == KC - 1 and n == 2
                        w20 = w.rearrange("p (k n) -> p k n", k=KC)[:, k, 0:20]
                        r = pe(lambda e, t=t, k=k, n=n, w20=w20, part=part, end=end: e.matmul(
                            bank[t][:, 0:20], (x_hi, x_lo)[part][:, k, t * P:(t + 1) * P], w20,
                            start=k == 0 and n == 0, stop=end), after=[*ready, chunks[k]], own=False, signal=None if end else False)
                dve(lambda e, t=t: e.tensor_tensor(col[:, 20 * t:20 * t + 20], bank[t][:, 0:20], par2("b_router"),
                                                   ALU.add), after=[r])
            logits = col[:, 0:80].rearrange("p (t n) -> p t n", t=NT)
            four = lambda n: col[:, 96 + 16 * n:112 + 16 * n].rearrange("p (t n) -> p t n", t=NT)
            one = lambda n: col[:, 80 + 4 * n:84 + 4 * n]
            ex, oh, es, o1, o2, w_ = (four(n) for n in range(6))
            mx, pg, p1, p2 = (one(n) for n in range(4))
            big = col[:, 192:256].rearrange("p (t e n) -> p t e n", t=NT, e=4)
            rank = sweep(C("rank4"), NT)
            over = lambda ap: wide(ap, [P, NT, 4])

            def first_of(dst, src, top):
                dve(lambda e: e.tensor_tensor(dst, src, over(top), ALU.is_equal))
                dve(lambda e: e.tensor_tensor(dst, dst, rank, ALU.mult))
                dve(lambda e: e.tensor_reduce(mx, dst, AX, ALU.max))
                dve(lambda e: e.tensor_tensor(dst, dst, over(mx), ALU.is_equal))

            def softmax4(dst, src):
                dve(lambda e: e.tensor_reduce(mx, src, AX, ALU.max))
                dve(lambda e: e.tensor_tensor(dst, src, over(mx), ALU.subtract))
                act(lambda e: e.activation(dst, dst, ACT.Exp), after=[dve_now()])
                dve(lambda e: e.tensor_reduce(mx, dst, AX, ALU.add), after=[act_now()])
                dve(lambda e: e.reciprocal(mx, mx))
                dve(lambda e: e.tensor_tensor(dst, dst, over(mx), ALU.mult))

            softmax4(ex, logits[:, :, 0:4])
            dve(lambda e: e.tensor_reduce(pg, ex, AX, ALU.max))
            first_of(oh, ex, pg)
            for t in range(NT):
                for g in range(4):
                    dve(lambda e, t=t, g=g: e.tensor_scalar(big[:, t, :, g], logits[:, t, 4 + 4 * g:8 + 4 * g],
                                                            oh[:, t, g:g + 1], None, ALU.mult))
            dve(lambda e: e.tensor_reduce(es.rearrange("p t n -> p (t n)"), big.rearrange("p t e n -> p (t e) n"),
                                          AX, ALU.add))
            softmax4(es, es)
            dve(lambda e: e.tensor_reduce(p1, es, AX, ALU.max))
            first_of(o1, es, p1)
            dve(lambda e: e.scalar_tensor_tensor(out=w_, in0=o1, scalar=-4.0, in1=es, op0=ALU.mult, op1=ALU.add))
            dve(lambda e: e.tensor_reduce(p2, w_, AX, ALU.max))
            first_of(o2, w_, p2)
            dve(lambda e: e.tensor_tensor(o1, o1, over(p1), ALU.mult))
            dve(lambda e: e.tensor_tensor(o2, o2, over(p2), ALU.mult))
            dve(lambda e: e.tensor_tensor(o1, o1, o2, ALU.add))
            dve(lambda e: e.tensor_tensor(mx, p1, p2, ALU.add))
            dve(lambda e: e.reciprocal(mx, mx))
            dve(lambda e: e.tensor_tensor(pg, pg, mx, ALU.mult))
            dve(lambda e: e.tensor_tensor(o1, o1, over(pg), ALU.mult))
            table = col[:, 256:320].rearrange("p (t g n) -> p t g n", t=NT, g=4)
            for t in range(NT):
                for g in range(4):
                    dve(lambda e, t=t, g=g: e.tensor_scalar(table[:, t, g, :], o1[:, t, :], oh[:, t, g:g + 1], None,
                                                            ALU.mult))
            for t in range(NT):
                r = transpose(bank[0][0:16, t * P:(t + 1) * P], col[:, 256 + 16 * t:272 + 16 * t], after=[dve_now()],
                              signal=None if t == 3 else False)
            turned = tmp[0][0:16, :]
            dve(lambda e: e.tensor_copy(turned, bank[0][0:16, :]), after=[r])
            for n in range(N_EXPERTS):
                b = bank[1 + n % 4]
                line = (act, dve)[n % 2]
                r = pe(lambda e, n=n, b=b: e.matmul(b[:, :], ident[0:16, n:n + 1].to_broadcast([16, P]), turned,
                                                    start=True, stop=True),
                       after=[line.now(1)] if n > 3 else [dve_now(), act_now()], own=False)
                if line is act:
                    act(lambda e, n=n, b=b: e.activation(gates[:, n, :], b[:, :], ACT.Copy), after=[r], own=False)
                else:
                    dve(lambda e, n=n, b=b: e.tensor_copy(gates[:, n, :], b[:, :]), after=[r], own=False)
            return gates

        def experts(gates):
            pairs = 2 * AT_ONCE
            with prog.loop(N_EXPERTS // AT_ONCE) as group:
                gate = lambda p, group=group: gates[:, group.i * AT_ONCE + p // 2, :]
                for p in range(pairs):
                    gate_up(p % 2, (lambda p=p: finish((p - 1) % 2, lambda: 2 * (p - 1), lambda: gate(p - 1)))
                            if p else None, free=dve_now(4) if p == 0 else None)
                for n in range(pairs):
                    ready = down(n, pairs, True, (lambda: finish((pairs - 1) % 2, lambda: 2 * (pairs - 1),
                                                                 lambda: gate(pairs - 1))) if n == 0 else None,
                                 busy=1)
                add_to_residual(ready, 1.0)

        rms_norm(xT, par2("mix_norm"), xn, KC)
        sync_all()
        A = Arena()
        k_mem = A.take(4 * MEM).rearrange("p (c t) -> p c t", c=4)
        v_mem = A.take(2 * 512).rearrange("p (t n) -> p t n", t=2)
        mem = A.take(KC * MEM).rearrange("p (c m) -> p c m", c=KC)
        loaded = sp(lambda e: e.dma_start(mem, mem_in), own=False)
        fq, fk, fv, cf, ga = fox_projections(A)
        sync_all()
        events = {}
        prog.weave({"gla": (STEPS, gla(ga, Arena(A.at + 6 * 512), events)),
                    "attention": (2, fox_attention(fq, fk, fv, cf, A)),
                    "memory": (1, memory(mem, loaded, k_mem, v_mem, events))})
        sync_all()
        k_late, v_late = (arena[:, CROSS_AT + n * 4 * MEM:CROSS_AT + (n + 1) * 4 * MEM] for n in range(2))
        flat_k, flat_v = (arena[:, n * 4 * MEM:(n + 1) * 4 * MEM] for n in range(2))
        dve(lambda e: e.tensor_copy(k_late, flat_k))
        dve(lambda e: e.tensor_copy(v_late, flat_v))
        added = project_out()
        added = cross(k_late.rearrange("p (c t) -> p c t", c=4), v_late.rearrange("p (t n) -> p t n", t=2), added,
                      Arena())
        gates = router(rms_norm(xT, par2("moe_norm"), xn, KC, ready=added, split=True))
        sync_all()
        experts(gates)
        rms_norm(xT, par2("final_norm"), xn, KC, ready=[dve_now(KC - 1 - d) for d in range(KC)])
        done = sp(lambda e: e.dma_start(y_out, xn), after=[dve_now()])
        assert prog.slot == SECOND_SLOTS, prog.slot
        sp.wait(done)


        def stream(e, n_slots, source):
            for s in range(RING):
                e.dma_start(ring[:, s, :], source(s)).then_inc(prog.landed[s].sem, 16)
            with e.Fori(1, n_slots // RING) as i:
                for s in range(RING):
                    e.wait_ge(prog.used.sem, i * RING + (s - RING + 1))
                    e.dma_start(ring[:, s, :], source(i * RING + s)).then_inc(prog.landed[s].sem, 16)

        layer_loop = next(it for it in sp.items if it[0] == "loop")
        at = sp.items.index(layer_loop)
        layer = layer_loop[1]
        layer_loop[2].insert(0, ("op", lambda e: stream(e, LAYER_SLOTS, lambda k: w1_in[layer.i * LAYER_SLOTS + k]),
                                 [], None))
        sp.items.insert(at + 1, ("op", lambda e: stream_second(e), [], None))

        rest = sp.items[at + 2:]
        del sp.items[at + 2:]

        def stream_second(e):
            sp.emit(e, rest[:1])
            stream(e, SECOND_SLOTS, lambda k: w2_in[k])
            sp.emit(e, rest[1:])

        block = ctx.enter_context(nc.Block())

        @block.sync
        def _(e):
            sp.emit(e)

        @block.tensor
        def _(e):
            pe.emit(e)

        @block.scalar
        def _(e):
            act.emit(e)

        @block.vector
        def _(e):
            dve.emit(e)

        @block.gpsimd
        def _(e):
            pool.emit(e)


def layout(inputs):
    import numpy as np

    f = lambda name: np.ascontiguousarray(inputs[name])

    def gate_slots(w):
        n = w.shape[1] // SLOT_COLS
        return w.reshape(KC, P, n, SLOT_COLS).transpose(2, 1, 0, 3).reshape(n, P, SLOT)

    def down_slots(w):
        n = w.shape[0] // (2 * P)
        return w.reshape(n, 2, P, D).transpose(0, 2, 1, 3).reshape(n, P, SLOT)

    def ffn_slots(gate, up, down):
        g, u, d = gate_slots(gate), gate_slots(up), down_slots(down)
        out, at = [], 0
        for pairs in FFN_PARTS:
            out += [x for n in range(at, at + pairs) for x in (g[n], u[n])] + list(d[at:at + pairs])
            at += pairs
        return out

    def chan(v):
        return v.reshape(-1, P).T

    def rep(v):
        return np.broadcast_to(v.reshape(1, -1), (P, v.size))

    def pack(columns, parts):
        out = np.zeros((P, SLOT), np.float32)
        for name, v in parts.items():
            a, w = columns[name]
            assert v.shape[1] == w, name
            out[:v.shape[0], a:a + w] = v
        return out

    heads = lambda w, order: w.reshape(*w.shape[:-1], -1, HD)[..., order, :].reshape(*w.shape[:-1], -1)
    q_order = [0, 4, 1, 5, 2, 6, 3, 7]
    by_half = [0, 2, 1, 3]
    slots1 = []
    for l in range(DEPTH):
        w = f("w_in")[l]
        att, rw, gd = w[:, :1352], w[:, 1352:1352 + 896], w[:, 2248:]
        odd = np.zeros((D, 256), np.float32)
        odd[:, 0:64] = att[:, 1280:1344]
        odd[:, 64:72] = att[:, 1344:1352]
        odd[:, 72:76] = gd[:, 1024:1028][:, by_half]
        odd[:, 76:80] = gd[:, 1028:1032][:, by_half]
        odd[:, 128:256] = rw[:, 768:896]
        lora = np.concatenate([f("rwkv_w_up")[l], f("rwkv_a_up")[l], f("rwkv_g_up")[l]], 0)
        up = np.zeros((P, 256), np.float32)
        up[:32] = f("rwkv_v_up")[0]
        conv = f("gdn_conv")[l].reshape(4, 6, P).transpose(2, 1, 0).reshape(P, 24)
        slots1.append(pack(PAR1, {
            "ffn_norm0": chan(f("ffn_norm")[l, 0]), "ffn_norm1": chan(f("ffn_norm")[l, 1]),
            "mix_norm": chan(f("mix_norm")[l]),
            "qk_norm": rep(np.concatenate([f("att_q_norm")[l]] * 8 + [f("att_k_norm")[l]] * 2)),
            "mu": chan(f("rwkv_mu")[l]), "w0": chan(f("rwkv_w0")[l]), "a0": chan(f("rwkv_a0")[l]),
            "k_k": chan(f("rwkv_k_k")[l]), "k_a": chan(f("rwkv_k_a")[l]), "r_k": chan(f("rwkv_r_k")[l].reshape(-1)),
            "gn_w": chan(f("rwkv_gn_w")[l]), "gn_b": chan(f("rwkv_gn_b")[l]), "v0": chan(f("rwkv_v0")[0]),
            "conv": conv, "a_log": rep(f("gdn_a_log")[l][by_half]), "dt_bias": rep(f("gdn_dt_bias")[l][by_half]),
            "o_norm": chan(np.tile(f("gdn_o_norm")[l], 4)), "lora_up": lora,
            "v_down": f("rwkv_v_down")[0].reshape(2, P, 32).transpose(1, 0, 2).reshape(P, 64), "v_up": up}))
        slots1 += ffn_slots(f("ffn_w_gate")[l, 0], f("ffn_w_up")[l, 0], f("ffn_w_down")[l, 0])
        slots1 += list(gate_slots(heads(att[:, :512], q_order)))
        slots1 += list(gate_slots(att[:, 512:768]))
        slots1 += list(gate_slots(att[:, 768:1280]))
        slots1 += list(gate_slots(odd))
        slots1 += list(gate_slots(rw[:, :768]))
        slots1 += list(gate_slots(gd[:, :1024]))
        slots1 += list(down_slots(f("w_out")[l]))
        slots1 += ffn_slots(f("ffn_w_gate")[l, 1], f("ffn_w_up")[l, 1], f("ffn_w_down")[l, 1])
    w = f("w_in_2")[0]
    o = [int(a) for a in np.cumsum([512, 512, 512, 8, 256, 256, 512, 512, 16])]
    odd = np.zeros((D, 256), np.float32)
    odd[:, 0:8], odd[:, 32:48] = w[:, o[2]:o[3]], w[:, o[7]:o[8]]
    rt = np.zeros((D, 256), np.float32)
    rt[:, 0:4], rt[:, 4:20] = f("w_router_group_2")[0], f("w_router_expert_2")[0]
    forget = np.zeros((P, 1), np.float32)
    forget[:8, 0] = f("b_forget_2")[0]
    alpha = np.zeros((P, 256), np.float32)
    alpha[32:48] = f("w_alpha_up_2")[0]
    slots2 = [pack(PAR2, {
        "mem_norm": chan(f("mem_norm_2")), "mix_norm": chan(f("mix_norm_2")[0]),
        "cross_norm": chan(f("cross_norm_2")[0]), "moe_norm": chan(f("moe_norm_2")[0]),
        "final_norm": chan(f("final_norm_2")), "b_forget": forget, "b_alpha": chan(f("b_alpha_2")[0]),
        "fox_gain": chan(f("fox_out_gain_2")[0]), "gla_gain": chan(f("gla_out_gain_2")[0]),
        "b_router": rep(np.concatenate([f("b_router_group_2")[0], f("b_router_expert_2")[0]])), "alpha_up": alpha})]
    slots2 += list(gate_slots(w[:, :o[2]])) + list(gate_slots(odd))
    slots2 += list(gate_slots(w[:, o[3]:o[7]]))
    slots2 += list(gate_slots(f("w_xk_2")[0])) + list(gate_slots(f("w_xv_2")[0]))
    slots2 += list(down_slots(f("w_out_2")[0])) + list(gate_slots(f("w_xq_2")[0]))
    slots2 += list(down_slots(f("w_xo_2")[0])) + list(gate_slots(rt))
    for g in range(N_EXPERTS // AT_ONCE):
        own = range(AT_ONCE * g, AT_ONCE * (g + 1))
        for n in own:
            pairs = zip(gate_slots(f("w_expert_gate_2")[0, n]), gate_slots(f("w_expert_up_2")[0, n]))
            slots2 += [x for pair in pairs for x in pair]
        for n in own:
            slots2 += list(down_slots(f("w_expert_down_2")[0, n]))
    slots2.append(np.zeros((P, SLOT), np.float32))

    r, s = np.arange(P)[:, None], np.arange(P)[None, :]
    lev = [((r >> (n + 1)) == (s >> (n + 1))) & ((r >> n) % 2 == 1) & ((s >> n) % 2 == 0) for n in range(7)]
    half = HD // 2
    inv = np.float32(10000.0) ** (-np.arange(half, dtype=np.float32) / np.float32(half))
    ang = np.arange(SEQ, dtype=np.float32)[:, None] * inv[None, :]
    cos, sin = np.cos(ang), np.sin(ang)
    rope = np.concatenate([cos, cos, -sin, sin], 1).reshape(NT, P, 2 * P // 2).transpose(1, 0, 2).reshape(P, -1)
    cmask = np.concatenate([np.zeros((P, 3 * P)), np.where(s > r, NEG, 0.0)], 1)
    const = np.concatenate([np.eye(P), np.ones((P, P)), (r // HD) == (s // HD), rope, cmask, r <= s, r >= s, r > s,
                            r < s] + lev + [m.T for m in lev] + [np.broadcast_to([[4., 3., 2., 1.]], (P, 4))],
                           1).astype(np.float32)
    turn = lambda a: np.ascontiguousarray(a.reshape(a.shape[0], KC, P).transpose(2, 1, 0))
    return {"x_t": turn(f("x")[0]), "mem_t": turn(f("mem_2")[0]), "consts": np.ascontiguousarray(const),
            "slots_1": np.stack(slots1), "slots_2": np.stack(slots2)}


def kernel(**inputs):
    import numpy as np
    import concourse.bacc as bacc
    from concourse.bass_utils import run_bass_kernel_spmd

    arrays = layout(inputs)
    nc = bacc.Bacc("TRN2", target_bir_lowering=False, num_devices=1)
    ins = [nc.dram_tensor(n, a.shape, F32, kind="ExternalInput").ap() for n, a in arrays.items()]
    out = nc.dram_tensor("y_t", (P, KC, SEQ), F32, kind="ExternalOutput").ap()
    build(nc, *ins, out)
    r = run_bass_kernel_spmd(nc, [arrays], core_ids=[0])
    y = np.asarray(r.results[0]["y_t"])
    return np.ascontiguousarray(y.transpose(2, 1, 0).reshape(1, SEQ, D))
```
